# Optimizing a Trainium2 kernel written in Bass

```python
import jax
import jax.numpy as jnp
from jax import lax
import numpy as np

D_MODEL = 1024
BATCH = 1
SEQ = 1024
DEPTH = 1

ATTN_HEAD_DIM = 64
ATTN_WIDTH = D_MODEL // 2
ATTN_HEADS = ATTN_WIDTH // ATTN_HEAD_DIM
HGRN_EXPAND = 128
HGRN_WIDTH = D_MODEL - ATTN_WIDTH
HGRN_HEADS = HGRN_WIDTH // HGRN_EXPAND
HGRN_HEAD_V = HGRN_WIDTH // HGRN_HEADS
IN_SPLITS = (ATTN_WIDTH, ATTN_WIDTH, ATTN_WIDTH, ATTN_HEADS,
             HGRN_WIDTH, HGRN_WIDTH, HGRN_WIDTH, HGRN_WIDTH)
IN_PROJ_WIDTH = 3 * ATTN_WIDTH + ATTN_HEADS + 4 * HGRN_WIDTH
Q_BLOCK = 128
HGRN_CHUNK = 64
N_GROUPS = 4
EXPERTS_PER_GROUP = 4
N_EXPERTS = N_GROUPS * EXPERTS_PER_GROUP
TOP_K_IN_GROUP = 2
D_EXPERT = D_MODEL // 2
NORM_EPS = 1e-6

kernel_name = "hybrid_fox_hgrn2_hmoe_adaln_layer"

def rms_norm(x, g):
    xf = x.astype(jnp.float32)
    y = xf * lax.rsqrt(jnp.mean(xf * xf, axis=-1, keepdims=True) + NORM_EPS)
    return (y * g.astype(jnp.float32)).astype(x.dtype)

def split_heads(t, n_heads):
    b, s, w = t.shape
    return t.reshape(b, s, n_heads, w // n_heads).transpose(0, 2, 1, 3)

def merge_heads(t):
    b, h, s, d = t.shape
    return t.transpose(0, 2, 1, 3).reshape(b, s, h * d)

def forgetting_attention(q, k, v, log_f):
    s_len, dh = q.shape[2], q.shape[3]
    scale = dh ** -0.5
    cum = jnp.cumsum(log_f, axis=-1)
    outs = []
    for i in range(s_len // Q_BLOCK):
        q0 = i * Q_BLOCK
        k_end = q0 + Q_BLOCK
        scores = jnp.einsum('bhqd,bhkd->bhqk', q[:, :, q0:k_end], k[:, :, :k_end]).astype(jnp.float32) * scale
        scores = scores + cum[:, :, q0:k_end, None] - cum[:, :, None, :k_end]
        causal = (q0 + jnp.arange(Q_BLOCK))[:, None] >= jnp.arange(k_end)[None, :]
        scores = jnp.where(causal, scores, -jnp.inf)
        probs = jax.nn.softmax(scores, axis=-1).astype(v.dtype)
        outs.append(jnp.einsum('bhqk,bhkd->bhqd', probs, v[:, :, :k_end]))
    return jnp.concatenate(outs, axis=2)

def hgrn2_chunkwise(q, k, v, log_f):
    b, h, s_len, dk = q.shape
    dv = v.shape[-1]
    n_chunks = s_len // HGRN_CHUNK

    def to_chunks(t):
        return t.reshape(b, h, n_chunks, HGRN_CHUNK, t.shape[-1]).transpose(2, 0, 1, 3, 4)

    tri = jnp.tril(jnp.ones((HGRN_CHUNK, HGRN_CHUNK), dtype=bool))[None, None, :, :, None]

    def step(state, inp):
        qc, kc, vc, gc = inp
        cum = jnp.cumsum(gc, axis=2)
        diff = jnp.where(tri, cum[:, :, :, None, :] - cum[:, :, None, :, :], -jnp.inf)
        scores = jnp.einsum('bhtk,bhtsk,bhsk->bhts', qc, jnp.exp(diff), kc)
        out = jnp.einsum('bhts,bhsv->bhtv', scores, vc) + jnp.einsum('bhtk,bhkv->bhtv', qc * jnp.exp(cum), state)
        last = cum[:, :, -1:, :]
        state = jnp.exp(last[:, :, 0, :])[..., None] * state + jnp.einsum('bhsk,bhsv->bhkv', kc * jnp.exp(last - cum), vc)
        return state, out

    state0 = jnp.zeros((b, h, dk, dv), jnp.float32)
    _, out = lax.scan(step, state0, (to_chunks(q), to_chunks(k), to_chunks(v), to_chunks(log_f)))
    return out.transpose(1, 2, 0, 3, 4).reshape(b, h, s_len, dv)

def hierarchical_moe(h, w_rg, b_rg, w_re, b_re, w_gate, w_up, w_down):
    f32 = jnp.float32
    hf = h.astype(f32)
    group_probs = jax.nn.softmax(hf @ w_rg.astype(f32) + b_rg.astype(f32), axis=-1)
    group_p, group_idx = lax.top_k(group_probs, 1)
    expert_logits = (hf @ w_re.astype(f32) + b_re.astype(f32)).reshape(-1, N_GROUPS, EXPERTS_PER_GROUP)
    group_onehot = jax.nn.one_hot(group_idx[:, 0], N_GROUPS, dtype=f32)
    in_group = jnp.einsum('tg,tge->te', group_onehot, expert_logits)
    top_logits, top_local = lax.top_k(in_group, TOP_K_IN_GROUP)
    weights = jax.nn.softmax(top_logits, axis=-1) * group_p
    expert_ids = group_idx * EXPERTS_PER_GROUP + top_local
    gates = jnp.einsum('tk,tke->te', weights, jax.nn.one_hot(expert_ids, N_EXPERTS, dtype=f32))
    y = jnp.zeros(h.shape, f32)
    for e in range(N_EXPERTS):
        act = jax.nn.silu(h @ w_gate[e]) * (h @ w_up[e])
        y = y + gates[:, e:e + 1] * (act @ w_down[e]).astype(f32)
    return y.astype(h.dtype)

def setup_inputs(seed: int = 0) -> dict:
    key = jax.random.key(seed)
    ks = jax.random.split(key, 21)
    f32 = jnp.float32

    def nrm(k, shape, s):
        return jax.random.normal(k, shape, f32) * s

    return {
        "x": nrm(ks[0], (BATCH, SEQ, D_MODEL), 1.0),
        "c": nrm(ks[1], (BATCH, D_MODEL), 1.0),
        "w_ada": nrm(ks[2], (DEPTH, D_MODEL, 6 * D_MODEL), D_MODEL ** -0.5),
        "b_ada": nrm(ks[3], (DEPTH, 6 * D_MODEL), 0.02),
        "norm1_g": 1.0 + nrm(ks[4], (DEPTH, D_MODEL), 0.02),
        "w_in": nrm(ks[5], (DEPTH, D_MODEL, IN_PROJ_WIDTH), D_MODEL ** -0.5),
        "b_fox": 1.0 + nrm(ks[6], (DEPTH, ATTN_HEADS), 0.1),
        "q_norm_g": 1.0 + nrm(ks[7], (DEPTH, ATTN_HEAD_DIM), 0.02),
        "k_norm_g": 1.0 + nrm(ks[8], (DEPTH, ATTN_HEAD_DIM), 0.02),
        "attn_out_g": 1.0 + nrm(ks[9], (DEPTH, ATTN_WIDTH), 0.02),
        "hgrn_lb": nrm(ks[10], (DEPTH + 1, HGRN_WIDTH), 1.0),
        "hgrn_out_g": 1.0 + nrm(ks[11], (DEPTH, HGRN_WIDTH), 0.02),
        "w_out": nrm(ks[12], (DEPTH, D_MODEL, D_MODEL), D_MODEL ** -0.5),
        "norm2_g": 1.0 + nrm(ks[13], (DEPTH, D_MODEL), 0.02),
        "w_router_group": nrm(ks[14], (DEPTH, D_MODEL, N_GROUPS), D_MODEL ** -0.5),
        "b_router_group": nrm(ks[15], (DEPTH, N_GROUPS), 0.01),
        "w_router_expert": nrm(ks[16], (DEPTH, D_MODEL, N_EXPERTS), D_MODEL ** -0.5),
        "b_router_expert": nrm(ks[17], (DEPTH, N_EXPERTS), 0.01),
        "w_gate": nrm(ks[18], (DEPTH, N_EXPERTS, D_MODEL, D_EXPERT), D_MODEL ** -0.5),
        "w_up": nrm(ks[19], (DEPTH, N_EXPERTS, D_MODEL, D_EXPERT), D_MODEL ** -0.5),
        "w_down": nrm(ks[20], (DEPTH, N_EXPERTS, D_EXPERT, D_MODEL), D_EXPERT ** -0.5),
    }

def reference(x, c, w_ada, b_ada, norm1_g, w_in, b_fox, q_norm_g, k_norm_g, attn_out_g,
              hgrn_lb, hgrn_out_g, w_out, norm2_g, w_router_group, b_router_group,
              w_router_expert, b_router_expert, w_gate, w_up, w_down):
    b, s, d = x.shape
    f32 = jnp.float32
    split_at = np.cumsum(IN_SPLITS)[:-1].tolist()
    lower_bounds = jnp.cumsum(jax.nn.softmax(hgrn_lb.astype(f32), axis=0), axis=0)
    for l in range(DEPTH):
        mod = jax.nn.silu(c) @ w_ada[l] + b_ada[l]
        shift1, scale1, gate1, shift2, scale2, gate2 = jnp.split(mod[:, None, :], 6, axis=-1)

        h = rms_norm(x, norm1_g[l]) * (1 + scale1) + shift1
        proj = h @ w_in[l]
        aq, ak, av, af, hq, hf, hi, hg = jnp.split(proj, split_at, axis=-1)

        aq = rms_norm(split_heads(aq, ATTN_HEADS), q_norm_g[l])
        ak = rms_norm(split_heads(ak, ATTN_HEADS), k_norm_g[l])
        av = split_heads(av, ATTN_HEADS)
        fox_log_f = jax.nn.log_sigmoid(af.astype(f32) + b_fox[l].astype(f32)).transpose(0, 2, 1)
        ao = forgetting_attention(aq, ak, av, fox_log_f)
        ao = merge_heads(rms_norm(ao, attn_out_g[l].reshape(ATTN_HEADS, 1, ATTN_HEAD_DIM)))

        lb = lower_bounds[l].reshape(HGRN_HEADS, 1, HGRN_EXPAND)
        forget = lb + (1 - lb) * jax.nn.sigmoid(split_heads(hf, HGRN_HEADS).astype(f32))
        ho = hgrn2_chunkwise(jax.nn.silu(split_heads(hq, HGRN_HEADS).astype(f32)), 1 - forget,
                             split_heads(hi, HGRN_HEADS).astype(f32), jnp.log(forget))
        ho = rms_norm(ho, hgrn_out_g[l].reshape(HGRN_HEADS, 1, HGRN_HEAD_V)) * jax.nn.silu(split_heads(hg, HGRN_HEADS).astype(f32))
        ho = merge_heads(ho).astype(x.dtype)

        x = x + gate1 * (jnp.concatenate([ao, ho], axis=-1) @ w_out[l])

        h2 = rms_norm(x, norm2_g[l]) * (1 + scale2) + shift2
        y = hierarchical_moe(h2.reshape(b * s, d), w_router_group[l], b_router_group[l],
                             w_router_expert[l], b_router_expert[l],
                             w_gate[l], w_up[l], w_down[l]).reshape(b, s, d)
        x = x + gate2 * y
    return x


_drawn_inputs = setup_inputs


def setup_inputs(seed=0):
    import zlib

    import numpy as np

    out = dict(_drawn_inputs(seed))
    spreads = {}
    factors = {'norm1_g': 3.594,
     'q_norm_g': 8.0,
     'k_norm_g': 7.905,
     'attn_out_g': 34.152,
     'hgrn_out_g': 16.491,
     'b_router_group': 64.0,
     'b_router_expert': 64.0,
     'b_fox': 2.854,
     'norm2_g': 8.0}
    for name, (base, spread) in spreads.items():
        noise = np.random.default_rng([zlib.crc32(name.encode()), seed]).standard_normal(out[name].shape)
        drawn = base * np.exp(spread * noise) if base else spread * noise
        out[name] = jnp.asarray(drawn.astype(out[name].dtype))
    for name, factor in factors.items():
        out[name] = (out[name] * factor).astype(out[name].dtype)
    return out
```

```python
from contextlib import ExitStack

import concourse.bass as bass
from concourse import mybir

P = 128
D = 1024
KD = D // P
SEQ = 1024
NT = SEQ // P
HALF = 512
AH, DH = 8, 64
AW = AH * DH
AUG = DH + 2
GH, DK = 4, 128
GW = GH * DK
LEVELS = 7
G, EG = 4, 4
NE = G * EG
NR = G + NE
F = 512
KF = F // P
MINT = 2 * SEQ // P
MAXT = 2 * SEQ // P + NE - 1
TS = 32
EPS = 1e-6
BIG = 3.0e38
FAR = 1.0e30

C_AQ, C_AK, C_AV, C_AF = 0, AW, 2 * AW, 3 * AW
C_HQ = 3 * AW + AH
C_HF, C_HI, C_HG = C_HQ + GW, C_HQ + 2 * GW, C_HQ + 3 * GW

F32 = mybir.dt.float32
I32 = mybir.dt.int32
ALU = mybir.AluOpType
ACT = mybir.ActivationFunctionType
X = mybir.AxisListType.X
ds = bass.ds


class Steps:

    def __init__(self, eng, sem):
        self.eng, self.sem, self.base, self.n = eng, sem, 0, 0

    def did(self, ins):
        ins.then_inc(self.sem, 1)
        self.n += 1

    def done(self):
        self.eng.wait_ge(self.sem, self.base + self.n)

    def then(self, ins):
        self.did(ins)
        self.done()

    def then_alone(self, ins):
        self.did(ins)
        wait_alone(self.eng, self.sem, self.base + self.n)


def wait_alone(eng, sem, value):
    eng.wait_ge(sem, value)
    eng.nop().then_inc(PASSED[0], 1)


PASSED = []


def over(ap, axis, shape):
    return ap.unsqueeze(axis).broadcast_to(shape)


def build(nc, a):
    with ExitStack() as kernel_memory:
        def keep(name, shape, dt=F32):
            return kernel_memory.enter_context(nc.sbuf_tensor(name, shape, dt))

        PASSED[:] = [kernel_memory.enter_context(nc.semaphore("passed"))]
        ps = kernel_memory.enter_context(nc.psum_tensor("ps", [P, 8, HALF], F32))
        c = {
            "ident": keep("ident", [P, P]),
            "ones": keep("ones", [P, P]),
            "upto": keep("upto", [P, P]),
            "before": keep("before", [P, P]),
            "causal": keep("causal", [P, P]),
            "cum": keep("cum", [P, NT, AH]),
            "ncum": keep("ncum", [P, NT, AH]),
            "eps": keep("eps", [P, 1]),
            "lg": keep("lg", [P, NT, NR]),
            "brt": keep("brt", [P, NR]),
            "mod": keep("mod", [P, 4, D]),
        }
        with ExitStack() as m:
            for n in ("ao", "ho"):
                c[n] = m.enter_context(nc.sbuf_tensor(n, [P, NT, AW], F32))
            with ExitStack() as mh:
                c["hT"] = mh.enter_context(nc.sbuf_tensor("hT", [P, KD, SEQ], F32))
                c["csil"] = mh.enter_context(nc.sbuf_tensor("csil", [P, KD, P], F32))
                normalise(nc, a, c, ps)
                hgrn(nc, a, c, ps)
                attention(nc, a, c, ps)
            project_out(nc, a, c, ps)
        experts(nc, a, c, ps)


def normalise(nc, a, c, ps):
    with ExitStack() as m:
        def sb(name, shape, dt=F32):
            return m.enter_context(nc.sbuf_tensor(name, shape, dt))

        def sem(name):
            return m.enter_context(nc.semaphore(name))

        ccol, cexp, crec = (sb(n, [P, KD]) for n in ("ccol", "cexp", "crec"))
        wada = sb("wada1", [P, 2, KD, HALF])
        brow = sb("brow1", [1, 2, HALF])
        g1 = sb("g1", [P, D])
        sh = sb("sh", [P, 2, D])
        xt = sb("xt", [P, 2, D])
        sq = sb("sq", [P, D])
        h = sb("h", [P, D])
        ss, rs = sb("ss", [P, NT]), sb("rs", [P, NT])
        waf = sb("waf", [P, KD, AH])
        bfox = sb("bfox", [P, AH])
        z, mn, ab, pre = (sb(n, [P, NT, AH]) for n in ("z", "mn", "ab", "pre"))
        lf = sb("lf", [P, NT, AH])

        s_c, s_g, s_w, s_w2, s_x, s_x2, s_af = (sem(f"n_{n}") for n in ("c", "g", "w", "w2", "x", "x2", "af"))
        s_const, s_csil, s_row = (sem(f"n_{n}") for n in ("const", "csil", "row"))
        s_sq, s_h, s_tr, s_ev = (sem(f"n_{n}") for n in ("sq", "h", "tr", "ev"))
        s_cexp, s_v, s_z, s_ab, s_lf, s_cum, s_free, s_pool = (
            sem(f"n_{n}") for n in ("cexp", "v", "z", "ab", "lf", "cum", "free", "pool"))
        s_a, s_eps, s_rt = sem("n_a"), sem("n_eps"), sem("n_rt")
        x3 = a["x"].rearrange("b (t p) d -> (b t) p d", p=P)
        w_ada = a["w_ada"][0].rearrange("(p k) n -> p k n", k=KD)
        w_in = a["w_in"][0].rearrange("(k p) n -> p k n", p=P)
        w_sem = [s_w, s_w2]
        x_sem = [s_x, s_x2]

        with nc.Block() as block:
            @block.sync
            def _(sp):
                sp.dma_start(ccol[:, :], a["c"][0].rearrange("(p k) -> p k", k=KD)).then_inc(s_c, 16)
                for r in range(2):
                    sp.dma_start(wada[:, r], w_ada[:, :, r * HALF:(r + 1) * HALF]).then_inc(w_sem[r], 16)
                    sp.dma_start(brow[:, r], a["b_ada"][0:1, r * HALF:(r + 1) * HALF]).then_inc(w_sem[r], 16)
                for i in range(2):
                    sp.dma_start(xt[:, i], x3[i]).then_inc(x_sem[i], 16)
                sp.dma_start(g1[:, :], a["norm1_g"][0].partition_broadcast(P)).then_inc(s_g, 16)
                for r in range(2, 4):
                    sp.wait_ge(s_row, r - 1)
                    sp.dma_start(wada[:, r % 2], w_ada[:, :, r * HALF:(r + 1) * HALF]).then_inc(w_sem[r % 2], 16)
                    sp.dma_start(brow[:, r % 2], a["b_ada"][0:1, r * HALF:(r + 1) * HALF]).then_inc(w_sem[r % 2], 16)
                sp.dma_start(waf[:, :, :], w_in[:, :, C_AF:C_AF + AH]).then_inc(s_af, 16)
                sp.dma_start(bfox[:, :], a["b_fox"][0].partition_broadcast(P)).then_inc(s_af, 16)
                for i in range(2, NT):
                    sp.wait_ge(s_free, i - 1)
                    sp.dma_start(xt[:, i % 2], x3[i]).then_inc(x_sem[i % 2], 16)

            @block.gpsimd
            def _(pool):
                v = Steps(pool, s_pool)
                v.did(pool.memset(c["ident"][:, :], 0.0))
                v.did(pool.memset(c["ones"][:, :], 1.0))
                pool.memset(c["eps"][:, :], EPS).then_inc(s_eps, 1)
                v.did(pool.memset(c["upto"][:, :], 1.0))
                v.did(pool.memset(c["before"][:, :], 1.0))
                v.then(pool.memset(c["causal"][:, :], 0.0))
                def keep_where(t, op, fill):
                    pool.affine_select(out=t[:, :], in_=t[:, :], compare_op=op, fill=fill, base=0,
                                       pattern=[[1, P]], channel_multiplier=-1).then_inc(s_const, 1)
                keep_where(c["ident"], ALU.not_equal, 1.0)
                keep_where(c["upto"], ALU.is_ge, 0.0)
                keep_where(c["before"], ALU.is_gt, 0.0)
                pool.affine_select(out=c["causal"][:, :], in_=c["causal"][:, :], compare_op=ALU.is_ge, fill=-FAR,
                                   base=0, pattern=[[-1, P]], channel_multiplier=1).then_inc(s_const, 1)

            @block.scalar
            def _(act):
                act.wait_ge(s_c, 16)
                act.activation(cexp[:, :], ccol[:, :], ACT.Exp, scale=-1.0).then_inc(s_cexp, 1)
                for i in range(NT):
                    act.wait_ge(x_sem[i % 2], 16 * (i // 2 + 1))
                    if i:
                        act.wait_ge(s_sq, i)
                    act.activation(sq[:, :], xt[:, i % 2], ACT.Square, accum_out=ss[:, i:i + 1]).then_inc(s_sq, 1)
                    act.wait_ge(s_sq, i + 1)
                    act.wait_ge(s_eps, 1)
                    act.activation(rs[:, i:i + 1], ss[:, i:i + 1], ACT.Sqrt, scale=1.0 / D,
                                   bias=c["eps"][:, :]).then_inc(s_rt, 1)
                    if i:
                        for b in range(2):
                            act.wait_ge(s_tr, 2 * i - 1 + b)
                            act.copy(c["hT"][:, 4 * b:4 * b + 4, (i - 1) * P:i * P],
                                     ps[:, 4 + b].rearrange("p (k t) -> p k t", t=P)).then_inc(s_ev, 1)
                for b in range(2):
                    act.wait_ge(s_tr, 2 * NT - 1 + b)
                    act.copy(c["hT"][:, 4 * b:4 * b + 4, (NT - 1) * P:],
                             ps[:, 4 + b].rearrange("p (k t) -> p k t", t=P)).then_inc(s_ev, 1)
                act.wait_ge(s_ab, 1)
                act.activation(ab[:, :, :], ab[:, :, :], ACT.Exp, scale=-1.0).then_inc(s_a, 1)
                act.wait_ge(s_a, 1)
                act.activation(ab[:, :, :], ab[:, :, :], ACT.Ln, bias=1.0).then_inc(s_lf, 1)

            @block.vector
            def _(dve):
                v = Steps(dve, s_v)
                dve.wait_ge(s_cexp, 1)
                v.then(dve.tensor_scalar(crec[:, :], cexp[:, :], 1.0, None, ALU.add))
                v.then(dve.reciprocal(crec[:, :], crec[:, :]))
                v.then(dve.tensor_tensor(crec[:, :], crec[:, :], ccol[:, :], ALU.mult))
                dve.tensor_copy(c["csil"][:, :, :], over(crec[:, :], 2, [P, KD, P])).then_inc(s_csil, 1)
                for r in range(4):
                    dve.wait_ge(s_row, r + 1)
                    v.did(dve.tensor_copy(sh[:, r // 2, (r % 2) * HALF:(r % 2 + 1) * HALF], ps[:, r % 2]))
                dve.wait_ge(s_g, 16)
                v.done()
                v.then(dve.scalar_tensor_tensor(sh[:, 1], sh[:, 1], 1.0, g1[:, :], ALU.add, ALU.mult))
                for i in range(NT):
                    dve.wait_ge(s_rt, i + 1)
                    v.then(dve.reciprocal(rs[:, i:i + 1], rs[:, i:i + 1]))
                    if i:
                        dve.wait_ge(s_tr, 2 * i)
                    dve.scalar_tensor_tensor(h[:, :], xt[:, i % 2], rs[:, i:i + 1], sh[:, 1],
                                             ALU.mult, ALU.mult).then_inc(s_free, 1)
                    dve.wait_ge(s_free, i + 1)
                    dve.tensor_tensor(h[:, :], h[:, :], sh[:, 0], ALU.add).then_inc(s_h, 1)
                dve.wait_ge(s_af, 32)
                dve.wait_ge(s_z, 1)
                v.then(dve.tensor_tensor(z[:, :, :], ps[:, 6, 0:NT * AH].rearrange("p (t h) -> p t h", h=AH),
                                         over(bfox[:, :], 1, [P, NT, AH]), ALU.add))
                v.did(dve.tensor_scalar(mn[:, :, :], z[:, :, :], 0.0, None, ALU.min))
                dve.scalar_tensor_tensor(ab[:, :, :], z[:, :, :], -1.0, z[:, :, :], ALU.mult, ALU.max).then_inc(s_ab, 1)
                dve.wait_ge(s_lf, 1)
                v.done()
                v.did(dve.memset(pre[:, 0, :], 0.0))
                v.then(dve.tensor_tensor(lf[:, :, :], mn[:, :, :], ab[:, :, :], ALU.subtract))
                for i in range(1, NT):
                    v.then(dve.tensor_tensor(pre[:, i], pre[:, i - 1], lf[:, i - 1], ALU.add))
                dve.nop().then_inc(s_cum, 1)
                dve.wait_ge(s_z, 2)
                cm = ps[:, 7, 0:NT * AH].rearrange("p (t h) -> p t h", h=AH)
                v.did(dve.tensor_copy(c["cum"][:, :, :], cm))
                v.then(dve.tensor_scalar(c["ncum"][:, :, :], cm, -1.0, None, ALU.mult))

            @block.tensor
            def _(pe):
                pe.wait_ge(s_const, 4)
                pe.wait_ge(s_csil, 1)
                for r in range(4):
                    pe.wait_ge(w_sem[r % 2], 32 * (r // 2 + 1))
                    if r >= 2:
                        pe.wait_ge(s_v, 3 + r - 1)
                    for k in range(KD):
                        pe.matmul(ps[:, r % 2], c["csil"][:, k], wada[:, r % 2, k], start=(k == 0), stop=False)
                    pe.matmul(ps[:, r % 2], c["ones"][0:1, :], brow[0:1, r % 2], start=False,
                              stop=True).then_inc(s_row, 1)
                for i in range(NT):
                    pe.wait_ge(s_h, i + 1)
                    for b in range(2):
                        if i:
                            pe.wait_ge(s_ev, 2 * i - 1 + b)
                        for k in range(4):
                            last = pe.transpose(ps[:, 4 + b, k * P:(k + 1) * P],
                                                h[:, (4 * b + k) * P:(4 * b + k + 1) * P], c["ident"][:, :])
                        last.then_inc(s_tr, 1)
                pe.wait_ge(s_ev, 2 * NT)
                pe.wait_ge(s_af, 32)
                for i in range(NT):
                    for k in range(KD):
                        last = pe.matmul(ps[:, 6, i * AH:(i + 1) * AH], c["hT"][:, k, i * P:(i + 1) * P],
                                         waf[:, k], start=(k == 0), stop=(k == KD - 1))
                last.then_inc(s_z, 1)
                pe.wait_ge(s_cum, 1)
                pe.matmul(ps[:, 7, 0:NT * AH], c["upto"][:, :], lf[:, :, :].rearrange("p t h -> p (t h)"),
                          start=True, stop=False)
                pe.matmul(ps[:, 7, 0:NT * AH], c["ones"][:, :], pre[:, :, :].rearrange("p t h -> p (t h)"),
                          start=False, stop=True).then_inc(s_z, 1)


def hgrn(nc, a, c, ps):
    with ExitStack() as m:
        def sb(name, shape, dt=F32):
            return m.enter_context(nc.sbuf_tensor(name, shape, dt))

        def sem(name):
            return m.enter_context(nc.semaphore(name))

        wt = sb("wt", [P, KD, 2, DK])
        wv = sb("wv", [P, KD, 2, DK])
        uf = sb("uf", [P, 2, SEQ])
        uq = sb("uq", [P, 2, SEQ])
        xq = sb("xq", [P, 2, SEQ])
        xv = sb("xv", [P, 2, NT, 2 * DK])
        ug = sb("ug", [P, 2, NT, DK])
        cum = sb("hcum", [P, SEQ])
        kk = sb("kk", [P, SEQ])
        kend = sb("kend", [P, SEQ])
        qe = sb("qe", [P, SEQ])
        ecum = sb("ecum", [P, SEQ])
        lev = sb("lev", [P, 2, SEQ])
        sc = sb("sc", [P, NT, P])
        kx = sb("kx", [P, NT, P])
        st = sb("st", [P, NT, DK])
        masks = sb("masks", [P, LEVELS, P], I32)
        ti, si = sb("ti", [P, P], I32), sb("si", [P, P], I32)
        tf, ge = sb("tf", [P, P]), sb("ge", [P, LEVELS + 1, P])
        reset = sb("reset", [P, SEQ], mybir.dt.bfloat16)
        lbx, lbw, lb, oml = sb("lbx", [P, 2, GH]), sb("lbw", [P, 2, GH]), sb("lb", [P, GH]), sb("oml", [P, GH])
        gout = sb("gout", [P, GW])
        ss, rs = sb("hss", [P, NT]), sb("hrs", [P, NT])

        s_wt, s_wv, s_k = sem("h_wt"), sem("h_wv"), sem("h_k")
        s_pj, s_pje = sem("h_pj"), sem("h_pje")
        s_tri, s_e = sem("h_tri"), sem("h_e")
        s_v, s_a, s_ka = sem("h_v"), sem("h_a"), sem("h_ka")
        s_f, s_lf, s_dk, s_ek, s_ec = (sem(f"h_{n}") for n in ("f", "lf", "dk", "ek", "ec"))
        s_d, s_x, s_l = (sem(f"h_{n}") for n in ("d", "x", "l"))
        s_kend, s_kt, s_kte, s_u, s_st = (sem(f"h_{n}") for n in ("kend", "kt", "kte", "u", "st"))
        s_g, s_ge, s_o, s_os, s_oe, s_qk, s_po = (sem(f"h_{n}") for n in ("g", "ge", "o", "os", "oe", "qk", "po"))
        s_sub, s_raw, s_ss, s_rt = sem("h_sub"), sem("h_raw"), sem("h_ss"), sem("h_rt")
        w_in = a["w_in"][0].rearrange("(k p) n -> p k n", p=P)
        UNITS = 4 + NT
        GR = [0, 2]

        with nc.Block() as block:
            @block.sync
            def _(sp):
                sp.dma_start(lbx[:, :, :], a["hgrn_lb"].rearrange("l (h p) -> p l h", p=P),
                             allow_slow_non_contiguous=True).then_inc(s_k, 16)
                sp.dma_start(gout[:, :], a["hgrn_out_g"][0].partition_broadcast(P)).then_inc(s_k, 16)

                def load_t(h):
                    sp.dma_start(wt[:, :, 0], w_in[:, :, ds(h * DK + C_HF, DK)]).then_inc(s_wt, 16)
                    sp.dma_start(wt[:, :, 1], w_in[:, :, ds(h * DK + C_HQ, DK)]).then_inc(s_wt, 16)

                def load_v(h):
                    sp.dma_start(wv[:, :, 0], w_in[:, :, ds(h * DK + C_HI, DK)]).then_inc(s_wv, 16)
                    sp.dma_start(wv[:, :, 1], w_in[:, :, ds(h * DK + C_HG, DK)]).then_inc(s_wv, 16)

                load_t(0)
                load_v(0)
                with sp.Fori(1, GH) as h:
                    sp.wait_ge(s_pj, h * UNITS - UNITS + 4)
                    load_t(h)
                    sp.wait_ge(s_pj, h * UNITS)
                    load_v(h)

            @block.gpsimd
            def _(pool):
                pool.iota(ti[:, :], [[1, P]], base=0, channel_multiplier=0).then_inc(s_po, 1)
                pool.iota(si[:, :], [[0, P]], base=0, channel_multiplier=1).then_inc(s_po, 1)
                pool.memset(reset[:, :], 1.0).then_inc(s_po, 1)
                pool.wait_ge(s_po, 3)
                pool.memset(reset[:, :].rearrange("p (c t) -> p c t", t=P)[:, :, 0:1], 0.0).then_inc(s_po, 1)

            @block.scalar
            def _(act):
                act.wait_ge(s_k, 32)
                act.wait_ge(s_sub, 1)
                act.activation(lbw[:, :, :], lbw[:, :, :], ACT.Exp).then_inc(s_a, 1)

                def copy_out(u, h, par):
                    act.wait_ge(s_pj, h * UNITS + u + 1)
                    bank = ps[:, 6 + u % 2]
                    if u == 0:
                        act.wait_ge(s_raw, h + 1)
                    if u < 2:
                        act.activation(uf[:, par, u * HALF:(u + 1) * HALF], bank, ACT.Exp,
                                       scale=-1.0).then_inc(s_pje, 1)
                    elif u < 4:
                        b = u - 2
                        act.copy(xq[:, par, b * HALF:(b + 1) * HALF], bank).then_inc(s_e, 1)
                        act.activation(uq[:, par, b * HALF:(b + 1) * HALF], bank, ACT.Exp,
                                       scale=-1.0).then_inc(s_pje, 1)
                    else:
                        act.copy(xv[:, par, u - 4], bank[:, 0:2 * DK]).then_inc(s_e, 1)
                        act.activation(ug[:, par, u - 4], bank[:, DK:2 * DK], ACT.Exp,
                                       scale=-1.0).then_inc(s_pje, 1)

                def head(h, more):
                    nxt = (h + 1) % 2
                    act.wait_ge(s_f, h + 1)
                    act.activation(kend[:, :], kend[:, :], ACT.Ln).then_inc(s_lf, 1)
                    if more:
                        copy_out(0, h + 1, nxt)
                    act.wait_ge(s_dk, h + 1)
                    act.activation(kend[:, :], kend[:, :], ACT.Exp).then_inc(s_ek, 1)
                    act.activation(ecum[:, :], cum[:, :], ACT.Exp).then_inc(s_ec, 1)
                    if more:
                        copy_out(1, h + 1, nxt)
                    for b in range(2):
                        act.wait_ge(s_kt, 2 * h + b + 1)
                        act.copy(kx[:, 4 * b:4 * b + 4], ps[:, b].rearrange("p (c t) -> p c t", t=P)).then_inc(s_kte, 1)
                    if more:
                        copy_out(2, h + 1, nxt)
                    for l in range(LEVELS):
                        act.wait_ge(s_d, h * LEVELS + l + 1)
                        act.activation(lev[:, l % 2], lev[:, l % 2], ACT.Exp).then_inc(s_x, 1)
                        if more:
                            for u in UNIT_AFTER[l]:
                                copy_out(u, h + 1, nxt)
                    for b in range(2):
                        act.wait_ge(s_o, 2 * h + b + 1)
                        act.activation(sc[:, 4 * b:4 * b + 4], ps[:, 4 + b].rearrange("p (c t) -> p c t", t=P),
                                       ACT.Square).then_inc(s_os, 1)
                    act.wait_ge(s_ss, h + 1)
                    act.activation(rs[:, :], ss[:, :], ACT.Sqrt, scale=1.0 / DK, bias=c["eps"][:, :]).then_inc(s_rt, 1)

                for u in range(UNITS):
                    copy_out(u, 0, 0)
                with act.Fori(0, GH - 1) as h:
                    head(h, True)
                head(GH - 1, False)

            @block.vector
            def _(dve):
                dve.wait_ge(s_k, 32)
                v = Steps(dve, s_v)
                v.then(dve.tensor_tensor(lb[:, :], lbx[:, 0], lbx[:, 1], ALU.max))
                dve.tensor_tensor(lbw[:, :, :], lbx[:, :, :], over(lb[:, :], 1, [P, 2, GH]),
                                  ALU.subtract).then_inc(s_sub, 1)
                dve.wait_ge(s_a, 1)
                v.then(dve.tensor_tensor(oml[:, :], lbw[:, 0], lbw[:, 1], ALU.add))
                v.then(dve.reciprocal(oml[:, :], oml[:, :]))
                v.did(dve.tensor_tensor(lb[:, :], lbw[:, 0], oml[:, :], ALU.mult))
                v.then(dve.tensor_tensor(oml[:, :], lbw[:, 1], oml[:, :], ALU.mult))
                dve.wait_ge(s_po, 4)
                v.then(dve.tensor_tensor(ti[:, :], ti[:, :], si[:, :], ALU.bitwise_xor))
                v.then(dve.tensor_copy(tf[:, :], ti[:, :]))
                v.then(dve.tensor_tensor(tf[:, :], tf[:, :], c["before"][:, :], ALU.mult))
                for l in range(LEVELS + 1):
                    v.did(dve.tensor_scalar(ge[:, l], tf[:, :], float(1 << l), None, ALU.is_ge))
                v.done()
                v.did(dve.tensor_tensor(masks[:, :, :], ge[:, 0:LEVELS], ge[:, 1:], ALU.subtract))
                v.did(dve.memset(st[:, 0], 0.0))
                v.done()
                before_heads = v.n

                def head(h):
                    par = h % 2
                    v.base, v.n = before_heads + h * V_STEPS, 0
                    dve.wait_ge(s_pje, h * UNITS + UNITS)
                    dve.wait_ge(s_e, (h + 1) * (UNITS - 2))
                    u = uf[:, par].rearrange("p a t -> p (a t)") if len(uf[:, par].shape) == 3 else uf[:, par]
                    uqh = uq[:, par].rearrange("p a t -> p (a t)") if len(uq[:, par].shape) == 3 else uq[:, par]
                    xqh = xq[:, par].rearrange("p a t -> p (a t)") if len(xq[:, par].shape) == 3 else xq[:, par]
                    v.then_alone(dve.tensor_scalar(u, u, 1.0, None, ALU.add))
                    v.then(dve.reciprocal(u, u))
                    dve.tensor_scalar(kend[:, :], u, oml[:, ds(h, 1)], lb[:, ds(h, 1)], ALU.mult,
                                      ALU.add).then_inc(s_f, 1)
                    v.then(dve.tensor_scalar(u, u, oml[:, ds(h, 1)], lb[:, ds(h, 1)], ALU.mult, ALU.add))
                    v.did(dve.tensor_scalar(kk[:, :], u, -1.0, 1.0, ALU.mult, ALU.add))
                    v.then_alone(dve.tensor_scalar(uqh, uqh, 1.0, None, ALU.add))
                    v.then(dve.reciprocal(uqh, uqh))
                    dve.tensor_tensor(xqh, xqh, uqh, ALU.mult).then_inc(s_qk, 1)
                    dve.wait_ge(s_lf, h + 1)
                    v.then(dve.tensor_tensor_scan(cum[:, :], reset[:, :], kend[:, :], 0.0, ALU.mult, ALU.add))
                    cc = cum[:, :].rearrange("p (c t) -> p c t", t=P)
                    ke = kend[:, :].rearrange("p (c t) -> p c t", t=P)
                    dve.tensor_tensor(ke, cc[:, :, P - 1:P].broadcast_to([P, NT, P]), cc,
                                      ALU.subtract).then_inc(s_dk, 1)

                    def exponents(l):
                        half = 1 << l
                        cb = cum[:, :].rearrange("p (b w) -> p b w", w=2 * half)
                        lb_ = lev[:, l % 2].rearrange("p (b w) -> p b w", w=2 * half)
                        nb = SEQ // (2 * half)
                        mid = cb[:, :, half - 1:half].broadcast_to([P, nb, half])
                        if l >= 2:
                            dve.wait_ge(s_g, h * (LEVELS + 1) + l)
                        v.did(dve.tensor_tensor(lb_[:, :, half:], cb[:, :, half:], mid, ALU.subtract))
                        dve.tensor_tensor(lb_[:, :, 0:half], mid, cb[:, :, 0:half], ALU.subtract).then_inc(s_d, 1)
                        v.done()

                    def factors(l):
                        half = 1 << l
                        w = 2 * half
                        lb_ = lev[:, l % 2].rearrange("p (b w) -> p b w", w=w)
                        qb = xqh.rearrange("p (b w) -> p b w", w=w)
                        kb = kk[:, :].rearrange("p (b w) -> p b w", w=w)
                        dve.wait_ge(s_x, h * LEVELS + l + 1)
                        v.did(dve.tensor_tensor(lb_[:, :, half:], lb_[:, :, half:], qb[:, :, half:], ALU.mult))
                        v.then(dve.tensor_tensor(lb_[:, :, 0:half], lb_[:, :, 0:half], kb[:, :, 0:half], ALU.mult))
                        dve.nop().then_inc(s_l, 1)

                    dve.wait_ge(s_qk, h + 1)
                    exponents(0)
                    dve.wait_ge(s_ek, h + 1)
                    dve.tensor_tensor(kend[:, :], kend[:, :], kk[:, :], ALU.mult).then_inc(s_kend, 1)
                    factors(0)
                    exponents(1)
                    dve.wait_ge(s_ec, h + 1)
                    v.did(dve.tensor_tensor(qe[:, :], ecum[:, :], xqh, ALU.mult))
                    for b in range(2):
                        dve.wait_ge(s_g, h * (LEVELS + 1) + 1)
                        v.did(dve.tensor_tensor(sc[:, 4 * b:4 * b + 4], ps[:, GR[0] + b].rearrange("p (c t) -> p c t", t=P),
                                                over(c["ident"][:, :], 1, [P, 4, P]), ALU.mult))
                    v.done()
                    dve.nop().then_inc(s_ge, 1)
                    dve.wait_ge(s_u, h + 1)
                    for i in range(NT - 1):
                        v.then(dve.scalar_tensor_tensor(
                            st[:, i + 1], st[:, i], ecum[:, i * P + P - 1:i * P + P],
                            ps[:, 4 + i // 4, (i % 4) * P:(i % 4 + 1) * P], ALU.mult, ALU.add))
                    dve.nop().then_inc(s_st, 1)
                    for l in range(LEVELS):
                        if l:
                            factors(l)
                        if 1 <= l < LEVELS - 1:
                            exponents(l + 1)
                        wait_alone(dve, s_g, h * (LEVELS + 1) + l + 2)
                        for b in range(2):
                            v.did(dve.copy_predicated(
                                sc[:, 4 * b:4 * b + 4], over(masks[:, l], 1, [P, 4, P]),
                                ps[:, GR[(l + 1) % 2] + b].rearrange("p (c t) -> p c t", t=P)))
                        v.done()
                        dve.nop().then_inc(s_ge, 1)
                    g = ug[:, par]
                    hg = xv[:, par]
                    if len(g.shape) == 4:
                        g, hg = (t.rearrange("p a c t -> p (a c) t") for t in (g, hg))
                    v.then_alone(dve.tensor_scalar(g, g, 1.0, None, ALU.add))
                    v.then(dve.reciprocal(g, g))
                    v.then(dve.tensor_tensor(g, g, hg[:, :, DK:], ALU.mult))
                    v.then(dve.tensor_tensor(g, g, over(gout[:, ds(h * DK, DK)], 1, [P, NT, DK]), ALU.mult))
                    dve.wait_ge(s_os, 2 * h + 2)
                    dve.tensor_reduce(ss[:, :], sc[:, :, :], X, ALU.add).then_inc(s_ss, 1)
                    dve.wait_ge(s_rt, h + 1)
                    v.then(dve.reciprocal(rs[:, :], rs[:, :]))
                    v.then(dve.tensor_tensor(g, g, over(rs[:, :], 2, [P, NT, DK]), ALU.mult))
                    for b in range(2):
                        v.did(dve.tensor_tensor(c["ho"][:, 4 * b:4 * b + 4, ds(h * DK, DK)],
                                                ps[:, 4 + b].rearrange("p (c t) -> p c t", t=P),
                                                g[:, 4 * b:4 * b + 4], ALU.mult))
                    v.done()
                    dve.nop().then_inc(s_oe, 1)
                    dve.nop().then_inc(s_raw, 1)
                    assert v.n == V_STEPS, v.n

                dve.nop().then_inc(s_raw, 1)
                dve.nop().then_inc(s_raw, 1)
                dve.nop().then_inc(s_ge, 1)
                dve.nop().then_inc(s_ge, 1)
                with dve.Fori(0, GH) as h:
                    head(h)

            @block.tensor
            def _(pe):
                def unit(u, h, ahead):
                    out = ps[:, 6 + u % 2]
                    if u == 0:
                        pe.wait_ge(s_wt, h * 32 + 32 * ahead + 32)
                    if u == 4:
                        pe.wait_ge(s_wv, h * 32 + 32 * ahead + 32)
                    if ahead or u >= 2:
                        pe.wait_ge(s_pje, h * UNITS + (ahead * UNITS + u - 1))
                    for k in range(KD):
                        if u < 4:
                            last = pe.matmul(out, wt[:, k, u // 2], c["hT"][:, k, (u % 2) * HALF:(u % 2 + 1) * HALF],
                                             start=(k == 0), stop=(k == KD - 1))
                        else:
                            last = pe.matmul(out[:, 0:2 * DK], c["hT"][:, k, (u - 4) * P:(u - 3) * P],
                                             wv[:, k].rearrange("p a b -> p (a b)"),
                                             start=(k == 0), stop=(k == KD - 1))
                    last.then_inc(s_pj, 1)

                def gram(n, h):
                    if n == 0:
                        pe.wait_ge(s_kte, 2 * h + 2)
                        pe.wait_ge(s_ge, h * (LEVELS + 1) + 1)
                    else:
                        pe.wait_ge(s_l, h * LEVELS + n)
                        pe.wait_ge(s_ge, h * (LEVELS + 1) + n + 1)
                    for i in range(NT):
                        out = ps[:, GR[n % 2] + i // 4, (i % 4) * P:(i % 4 + 1) * P]
                        if n == 0:
                            q = xq[:, h % 2, i * P:(i + 1) * P]
                            if len(q.shape) == 3:
                                q = q.rearrange("p a t -> p (a t)")
                            last = pe.matmul(out, kk[:, i * P:(i + 1) * P], q, start=True, stop=True)
                        else:
                            s = lev[:, (n - 1) % 2, i * P:(i + 1) * P]
                            last = pe.matmul(out, s, s, start=True, stop=True)
                    last.then_inc(s_g, 1)

                def head(h, more):
                    def units(*us):
                        for u in us:
                            if more:
                                unit(u, h, 1)
                    v = xv[:, h % 2]
                    if len(v.shape) == 4:
                        v = v.rearrange("p a c t -> p (a c) t")
                    units(0)
                    pe.wait_ge(s_kend, h + 1)
                    for b in range(2):
                        pe.wait_ge(s_ge, h * (LEVELS + 1) + 2)
                        for i in range(4 * b, 4 * b + 4):
                            last = pe.transpose(ps[:, b, (i % 4) * P:(i % 4 + 1) * P], kend[:, i * P:(i + 1) * P],
                                                c["ident"][:, :])
                        last.then_inc(s_kt, 1)
                    units(1)
                    pe.wait_ge(s_kte, 2 * h + 2)
                    pe.wait_ge(s_oe, h + 1)
                    for i in range(NT):
                        last = pe.matmul(ps[:, 4 + i // 4, (i % 4) * P:(i % 4 + 1) * P], kx[:, i], v[:, i, 0:DK],
                                         start=True, stop=True)
                    last.then_inc(s_u, 1)
                    units(2)
                    gram(0, h)
                    for l in range(LEVELS):
                        gram(l + 1, h)
                        units(*UNIT_AFTER[l])
                    pe.wait_ge(s_st, h + 1)
                    for b in range(2):
                        pe.wait_ge(s_ge, (h + 1) * (LEVELS + 1) + 2)
                        for i in range(4 * b, 4 * b + 4):
                            out = ps[:, 4 + b, (i % 4) * P:(i % 4 + 1) * P]
                            pe.matmul(out, sc[:, i], v[:, i, 0:DK], start=True, stop=False)
                            last = pe.matmul(out, qe[:, i * P:(i + 1) * P], st[:, i], start=False, stop=True)
                        last.then_inc(s_o, 1)

                pe.nop().then_inc(s_oe, 1)
                for u in range(UNITS):
                    unit(u, 0, 0)
                with pe.Fori(0, GH - 1) as h:
                    head(h, True)
                head(GH - 1, False)


UNIT_AFTER = [(3,), (4,), (5,), (6, 7), (8, 9), (10,), (11,)]
V_STEPS = 60


def attention(nc, a, c, ps):
    with ExitStack() as m:
        def sb(name, shape, dt=F32):
            return m.enter_context(nc.sbuf_tensor(name, shape, dt))

        def sem(name):
            return m.enter_context(nc.semaphore(name))

        wq = sb("wq", [P, KD, 3, DH])
        raw = sb("raw", [P, 2, NT, 3 * DH])
        sqr = sb("sqr", [P, NT, 2 * DH])
        qk = sb("qk", [P, NT, 2, AUG])
        qT, kT = sb("qT", [AUG, SEQ]), sb("kT", [AUG, SEQ])
        p = sb("p", [P, 2, SEQ])
        pT = sb("pT", [P, 4, 4, P])
        o = sb("o", [P, NT, DH])
        osq = sb("osq", [P, NT, DH])
        nm, rsum = sb("nm", [P, NT]), sb("rsum", [P, NT])
        rin, oss = sb("rin", [P, NT]), sb("oss", [P, NT])
        ss = sb("ass", [P, NT, 2])
        gqk = sb("gqk", [P, 2, DH])
        gatt = sb("gatt", [P, AW])
        wada = sb("wada2", [P, KD, HALF])
        blank = sb("blank", [P, D])
        brow = sb("brow2", [1, HALF])

        s_k, s_w, s_ada_w = sem("a_k"), sem("a_w"), sem("a_adaw")
        s_pj, s_cp, s_pje, s_norm, s_qkt, s_qT, s_kT = (
            sem(f"a_{n}") for n in ("pj", "cp", "pje", "norm", "qkt", "qT", "kT"))
        s_s, s_nm, s_p, s_t, s_te0, s_te1, s_pv, s_o1 = (
            sem(f"a_{n}") for n in ("s", "nm", "p", "t", "te0", "te1", "pv", "o1"))
        s_ada, s_adae, s_v = sem("a_ada"), sem("a_adae"), sem("a_v")
        s_blank, s_bl = sem("a_blank"), sem("a_bl")
        s_ss, s_rt, s_oss, s_ort = sem("a_ss"), sem("a_rt"), sem("a_oss"), sem("a_ort")
        w_in = a["w_in"][0].rearrange("(k p) n -> p k n", p=P)
        w_ada = a["w_ada"][0].rearrange("(p k) n -> p k n", k=KD)
        mod = c["mod"][:, :, :].rearrange("p a (b n) -> p (a b) n", n=HALF)

        groups = [[(g, min(4, qi + 1 - 4 * g)) for g in range(qi // 4 + 1)] for qi in range(NT)]
        first = [sum(len(x) for x in groups[:qi]) for qi in range(NT)]
        NG = sum(len(x) for x in groups)
        tile_of = [qi for qi in range(NT) for _ in groups[qi]]
        assert NG % 4 == 0

        def scores(qi):
            return ps[:, 2 * (qi % 2):2 * (qi % 2) + 2].rearrange("p b n -> p (b n)")

        def copy_group(eng, copy, q, size, h, done):
            eng.wait_ge(s_t, h * NG + q + 2)
            eng.wait_ge(s_pv, h * NT + (tile_of[q - 4] + 1 if q >= 4 else 0) + 1)
            copy(pT[:, q % 4, 0:size].rearrange("p b q -> p (b q)"), ps[:, 4 + q % 2, 0:size * P]).then_inc(done, 1)

        with nc.Block() as block:
            @block.sync
            def _(sp):
                sp.dma_start(gqk[:, 0], a["q_norm_g"][0].partition_broadcast(P)).then_inc(s_k, 16)
                sp.dma_start(gqk[:, 1], a["k_norm_g"][0].partition_broadcast(P)).then_inc(s_k, 16)
                sp.dma_start(gatt[:, :], a["attn_out_g"][0].partition_broadcast(P)).then_inc(s_k, 16)

                def head_weights(h):
                    for n, col in enumerate((C_AQ, C_AK, C_AV)):
                        sp.dma_start(wq[:, :, n], w_in[:, :, ds(h * DH + col, DH)]).then_inc(s_w, 16)

                def ada_weights(h):
                    sp.dma_start(wada[:, :, :], w_ada[:, :, ds(h * HALF + 2 * D, HALF)]).then_inc(s_ada_w, 16)
                    sp.dma_start(brow[:, :], a["b_ada"][0:1, ds(h * HALF + 2 * D, HALF)]).then_inc(s_ada_w, 16)

                head_weights(0)
                ada_weights(0)
                with sp.Fori(1, AH) as h:
                    sp.wait_ge(s_pj, h * NT)
                    head_weights(h)
                    sp.wait_ge(s_ada, h)
                    ada_weights(h)

            @block.gpsimd
            def _(pool):
                pool.memset(blank[:, :], 0.0).then_inc(s_blank, 1)
                pool.wait_ge(s_blank, 1)
                with pool.Fori(MINT, MAXT) as t:
                    pool.dma_start(a["y_dram"][ds(t * P, P), :], blank[:, :]).then_inc(s_bl, 16)
                pool.wait_ge(s_bl, 16 * (MAXT - MINT))

            @block.scalar
            def _(act):
                def copy_out(i, h, par):
                    act.wait_ge(s_pj, h * NT + i + 1)
                    if i == 0 and not (isinstance(h, int) and h == 0):
                        act.wait_ge(s_pv, (h - 1) * NT + 1)
                        act.wait_ge(s_norm, h)
                    act.copy(raw[:, par, i], ps[:, 7, 0:3 * DH]).then_inc(s_cp, 1)
                    act.activation(sqr[:, i], ps[:, 7, 0:2 * DH], ACT.Square).then_inc(s_pje, 1)

                def head(h, more):
                    for b in range(2):
                        act.wait_ge(s_qkt, 2 * h + 1)
                        act.copy(qT[:, b * HALF:(b + 1) * HALF], ps[0:AUG, 4 + b]).then_inc(s_qT, 1)
                    for i in range(NT):
                        act.wait_ge(s_nm, h * NT + i + 1)
                        act.wait_ge(s_t, h * NG + (first[i - 1] if i >= 2 else 0) + 1)
                        act.activation(p[:, i % 2, 0:(i + 1) * P], scores(i)[:, 0:(i + 1) * P], ACT.Exp,
                                       bias=nm[:, i:i + 1], accum_out=rsum[:, i:i + 1]).then_inc(s_p, 1)
                        if more:
                            copy_out(i, h + 1, (h + 1) % 2)
                        for n, (g, size) in enumerate(groups[i]):
                            q = first[i] + n
                            if q % 2 == 0:
                                copy_group(act, act.copy, q, size, h, s_te0)
                    if more:
                        qk_root(h + 1)
                    act.wait_ge(s_oss, h + 1)
                    act.activation(oss[:, :], oss[:, :], ACT.Sqrt, scale=1.0 / DH, bias=c["eps"][:, :]).then_inc(s_ort, 1)

                def qk_root(h):
                    act.wait_ge(s_ss, h + 1)
                    act.activation(ss[:, :, :], ss[:, :, :], ACT.Sqrt, scale=1.0 / DH, bias=c["eps"][:, :]).then_inc(s_rt, 1)

                for i in range(NT):
                    copy_out(i, 0, 0)
                qk_root(0)
                with act.Fori(0, AH - 1) as h:
                    head(h, True)
                head(AH - 1, False)

            @block.vector
            def _(dve):
                v = Steps(dve, s_v)
                dve.wait_ge(s_k, 48)
                v.did(dve.memset(qk[:, :, 0, AUG - 1:AUG], 1.0))
                v.did(dve.memset(qk[:, :, 1, AUG - 2:AUG - 1], 1.0))
                v.then(dve.tensor_scalar(gqk[:, 0], gqk[:, 0], DH ** -0.5, None, ALU.mult))

                def norm(h):
                    dve.wait_ge(s_pje, h * NT + NT)
                    dve.wait_ge(s_cp, h * NT + NT)
                    r = raw[:, h % 2]
                    if len(r.shape) == 4:
                        r = r.rearrange("p a t n -> p (a t) n")
                    dve.tensor_reduce(ss[:, :, :], sqr[:, :, :].rearrange("p t (a d) -> p t a d", a=2), X,
                                      ALU.add).then_inc(s_ss, 1)
                    dve.wait_ge(s_rt, h + 1)
                    v.then(dve.reciprocal(ss[:, :, :], ss[:, :, :]))
                    v.then(dve.tensor_tensor(qk[:, :, :, 0:DH], r[:, :, 0:2 * DH].rearrange("p t (a d) -> p t a d", a=2),
                                             over(ss[:, :, :], 3, [P, NT, 2, DH]), ALU.mult))
                    v.did(dve.tensor_tensor(qk[:, :, :, 0:DH], qk[:, :, :, 0:DH],
                                            over(gqk[:, :, :], 1, [P, NT, 2, DH]), ALU.mult))
                    v.did(dve.tensor_copy(qk[:, :, 0, DH:DH + 1], c["cum"][:, :, ds(h, 1)]))
                    v.did(dve.tensor_copy(qk[:, :, 1, DH + 1:DH + 2], c["ncum"][:, :, ds(h, 1)]))
                    v.done()
                    dve.nop().then_inc(s_norm, 1)

                def odd_groups(i, h):
                    for n, (g, size) in enumerate(groups[i]):
                        q = first[i] + n
                        if q % 2:
                            copy_group(dve, dve.tensor_copy, q, size, h, s_te1)

                def head(h, more):
                    v.base, v.n = before_heads + h * A_STEPS, 0
                    for b in range(2):
                        dve.wait_ge(s_qkt, 2 * h + 2)
                        v.did(dve.tensor_copy(kT[:, b * HALF:(b + 1) * HALF], ps[0:AUG, b]))
                    v.done()
                    dve.nop().then_inc(s_kT, 1)
                    for i in range(NT):
                        dve.wait_ge(s_s, h * NT + i + 1)
                        d = scores(i)[:, i * P:(i + 1) * P]
                        v.then(dve.tensor_tensor(d, d, c["causal"][:, :], ALU.add))
                        dve.tensor_reduce(nm[:, i:i + 1], scores(i)[:, 0:(i + 1) * P], X, ALU.max,
                                          negate=True).then_inc(s_nm, 1)
                        if i:
                            odd_groups(i - 1, h)
                    odd_groups(NT - 1, h)
                    if more:
                        norm(h + 1)
                    dve.wait_ge(s_ada, h + 1)
                    dve.tensor_copy(mod[:, ds(h, 1)], ps[:, 7:8]).then_inc(s_adae, 1)
                    dve.wait_ge(s_p, h * NT + NT + 1)
                    v.then(dve.reciprocal(rin[:, :], rsum[:, :]))
                    dve.wait_ge(s_pv, h * NT + NT + 1)
                    v.then(dve.tensor_tensor(o[:, :, :], ps[:, 6].rearrange("p (t d) -> p t d", d=DH),
                                             over(rin[:, :], 2, [P, NT, DH]), ALU.mult))
                    dve.nop().then_inc(s_o1, 1)
                    v.then(dve.tensor_tensor(osq[:, :, :], o[:, :, :], o[:, :, :], ALU.mult))
                    dve.tensor_reduce(oss[:, :], osq[:, :, :], X, ALU.add).then_inc(s_oss, 1)
                    dve.wait_ge(s_ort, h + 1)
                    v.then(dve.reciprocal(oss[:, :], oss[:, :]))
                    v.then(dve.tensor_tensor(o[:, :, :], o[:, :, :], over(oss[:, :], 2, [P, NT, DH]), ALU.mult))
                    v.then(dve.tensor_tensor(c["ao"][:, :, ds(h * DH, DH)], o[:, :, :],
                                             over(gatt[:, ds(h * DH, DH)], 1, [P, NT, DH]), ALU.mult))
                    assert v.n == A_STEPS or not more, v.n

                norm(0)
                before_heads = v.n
                with dve.Fori(0, AH - 1) as h:
                    head(h, True)
                head(AH - 1, False)

            @block.tensor
            def _(pe):
                for s in (s_p, s_t, s_pv, s_o1):
                    pe.nop().then_inc(s, 1)

                def project(i, h):
                    if i == 0:
                        pe.wait_ge(s_w, 48 * h + 48)
                    if not (isinstance(h, int) and h == 0):
                        pe.wait_ge(s_cp, h * NT + i)
                        pe.wait_ge(s_pje, h * NT + i)
                        if i == 0 and not (isinstance(h, int) and h == 1):
                            pe.wait_ge(s_adae, h - 1)
                    elif i:
                        pe.wait_ge(s_cp, i)
                        pe.wait_ge(s_pje, i)
                    for k in range(KD):
                        last = pe.matmul(ps[:, 7, 0:3 * DH], c["hT"][:, k, i * P:(i + 1) * P],
                                         wq[:, k].rearrange("p a d -> p (a d)"), start=(k == 0), stop=(k == KD - 1))
                    last.then_inc(s_pj, 1)

                def score(i, h):
                    pe.wait_ge(s_p, h * NT + (i - 1 if i else 0) + 1)
                    for n0 in range(0, (i + 1) * P, HALF):
                        n1 = min(n0 + HALF, (i + 1) * P)
                        last = pe.matmul(scores(i)[:, n0:n1], qT[:, i * P:(i + 1) * P], kT[:, n0:n1],
                                         start=True, stop=True)
                    last.then_inc(s_s, 1)

                def turn(i, h):
                    pe.wait_ge(s_p, h * NT + i + 2)
                    for n, (g, size) in enumerate(groups[i]):
                        q = first[i] + n
                        if q >= 2:
                            pe.wait_ge((s_te0, s_te1)[q % 2], h * (NG // 2) + q // 2)
                        for b in range(size):
                            kb = 4 * g + b
                            last = pe.transpose(ps[:, 4 + q % 2, b * P:(b + 1) * P],
                                                p[:, i % 2, kb * P:(kb + 1) * P], c["ident"][:, :])
                        last.then_inc(s_t, 1)

                def values(i, h):
                    if i == 0:
                        pe.wait_ge(s_o1, h + 1)
                    v = raw[:, h % 2]
                    if len(v.shape) == 4:
                        v = v.rearrange("p a t n -> p (a t) n")
                    last_q = first[i] + len(groups[i]) - 1
                    pe.wait_ge(s_te0, h * (NG // 2) + last_q // 2 + 1)
                    if last_q:
                        pe.wait_ge(s_te1, h * (NG // 2) + (last_q + 1) // 2)
                    for kb in range(i + 1):
                        q = first[i] + kb // 4
                        last = pe.matmul(ps[:, 6, i * DH:(i + 1) * DH], pT[:, q % 4, kb % 4],
                                         v[:, kb, 2 * DH:3 * DH], start=(kb == 0), stop=(kb == i))
                    last.then_inc(s_pv, 1)

                def ada(h):
                    pe.wait_ge(s_ada_w, 32 * h + 32)
                    if not (isinstance(h, int) and h == AH - 1):
                        pe.wait_ge(s_cp, h * NT + 2 * NT)
                        pe.wait_ge(s_pje, h * NT + 2 * NT)
                    else:
                        pe.wait_ge(s_adae, h)
                    for k in range(KD):
                        pe.matmul(ps[:, 7], c["csil"][:, k], wada[:, k], start=(k == 0), stop=False)
                    pe.matmul(ps[:, 7], c["ones"][0:1, :], brow[0:1, :], start=False, stop=True).then_inc(s_ada, 1)

                def head(h, more):
                    pe.wait_ge(s_norm, h + 1)
                    pe.wait_ge(s_p, h * NT + 1)
                    if more is not None:
                        pe.wait_ge(s_pv, h * NT + 1)
                    for a_ in range(2):
                        for i in range(NT):
                            bank = (4 if a_ == 0 else 0) + i // 4
                            last = pe.transpose(ps[0:AUG, bank, (i % 4) * P:(i % 4 + 1) * P], qk[:, i, a_],
                                                c["ident"][:, :])
                        last.then_inc(s_qkt, 1)
                    pe.wait_ge(s_kT, h + 1)
                    pe.wait_ge(s_qT, 2 * h + 2)
                    score(0, h)
                    for i in range(NT):
                        if more:
                            project_next(i, h)
                        if i < NT - 1:
                            score(i + 1, h)
                        turn(i, h)
                        if i:
                            values(i - 1, h)
                    ada(h)
                    values(NT - 1, h)

                def project_next(i, h):
                    pe.wait_ge(s_w, 48 * h + 96)
                    pe.wait_ge(s_cp, h * NT + NT + i)
                    pe.wait_ge(s_pje, h * NT + NT + i)
                    if i == 0:
                        pe.wait_ge(s_adae, h + 1)
                    for k in range(KD):
                        last = pe.matmul(ps[:, 7, 0:3 * DH], c["hT"][:, k, i * P:(i + 1) * P],
                                         wq[:, k].rearrange("p a d -> p (a d)"), start=(k == 0), stop=(k == KD - 1))
                    last.then_inc(s_pj, 1)

                pe.nop().then_inc(s_adae, 1)
                for i in range(NT):
                    project(i, 0)
                with pe.Fori(0, AH - 1) as h:
                    head(h, True)
                head(AH - 1, False)


A_STEPS = 21


def project_out(nc, a, c, ps):
    with ExitStack() as m:
        def sb(name, shape, dt=F32):
            return m.enter_context(nc.sbuf_tensor(name, shape, dt))

        def sem(name):
            return m.enter_context(nc.semaphore(name))

        wo = sb("wo", [P, KD, D])
        cat, catT = sb("cat", [P, D]), sb("catT", [P, KD, P])
        xt, x1, sq, h2 = sb("oxt", [P, D]), sb("x1", [P, D]), sb("osqr", [P, D]), sb("h2", [P, D])
        h2T = sb("h2T", [P, KD, P])
        g2 = sb("g2", [P, D])
        wr = sb("wr", [P, KD, NR])
        ss, rs = sb("oss2", [P, 1]), sb("ors", [P, 1])
        s_wo, s_k, s_x, s_cat, s_ct, s_cte, s_mm = (sem(f"o_{n}") for n in ("wo", "k", "x", "cat", "ct", "cte", "mm"))
        s_x1, s_sq, s_h2, s_st, s_ht, s_hte, s_r, s_re, s_v, s_y, s_c0 = (
            sem(f"o_{n}") for n in ("x1", "sq", "h2", "st", "ht", "hte", "r", "re", "v", "y", "c0"))
        s_rt = sem("o_rt")
        x3 = a["x"].rearrange("b s d -> (b s) d")

        with nc.Block() as block:
            @block.sync
            def _(sp):
                sp.dma_start(wo[:, :, :], a["w_out"][0].rearrange("(k p) n -> p k n", p=P)).then_inc(s_wo, 16)
                sp.dma_start(wr[:, :, 0:G], a["w_router_group"][0].rearrange("(k p) n -> p k n", p=P)).then_inc(s_k, 16)
                sp.dma_start(wr[:, :, G:NR], a["w_router_expert"][0].rearrange("(k p) n -> p k n", p=P)).then_inc(s_k, 16)
                sp.dma_start(g2[:, :], a["norm2_g"][0].partition_broadcast(P)).then_inc(s_k, 16)
                sp.dma_start(c["brt"][:, 0:G], a["b_router_group"][0].partition_broadcast(P)).then_inc(s_k, 16)
                sp.dma_start(c["brt"][:, G:NR], a["b_router_expert"][0].partition_broadcast(P)).then_inc(s_k, 16)

                def stores(i):
                    sp.wait_ge(s_h2, i + 1)
                    sp.dma_start(a["x1_dram"][ds(i * P, P), :], x1[:, :]).then_inc(s_st, 16)
                    sp.dma_start(a["h2_dram"][ds(i * P, P), :], h2[:, :]).then_inc(s_st, 16)

                sp.dma_start(xt[:, :], x3[0:P, :]).then_inc(s_x, 16)
                with sp.Fori(1, NT) as i:
                    sp.wait_ge(s_x1, i)
                    sp.dma_start(xt[:, :], x3[ds(i * P, P), :]).then_inc(s_x, 16)
                    stores(i - 1)
                stores(NT - 1)
                sp.wait_ge(s_st, 32 * NT)

            @block.gpsimd
            def _(pool):
                def concat(i):
                    pool.tensor_copy(cat[:, 0:AW], c["ao"][:, i]).then_inc(s_cat, 1)
                    pool.tensor_copy(cat[:, AW:], c["ho"][:, i]).then_inc(s_cat, 1)
                concat(0)
                with pool.Fori(1, NT) as i:
                    pool.wait_ge(s_ct, 2 * i)
                    pool.tensor_copy(cat[:, 0:AW], flat(c["ao"][:, ds(i, 1)])).then_inc(s_cat, 1)
                    pool.tensor_copy(cat[:, AW:], flat(c["ho"][:, ds(i, 1)])).then_inc(s_cat, 1)

            @block.scalar
            def _(act):
                def cat_out(i):
                    for b in range(2):
                        act.wait_ge(s_ct, 2 * i + b + 1)
                        if not (isinstance(i, int) and i == 0):
                            act.wait_ge(s_mm, 2 * i)
                        act.copy(catT[:, 4 * b:4 * b + 4].rearrange("p k t -> p (k t)"), ps[:, b]).then_inc(s_cte, 1)

                def h_out(i):
                    for b in range(2):
                        act.wait_ge(s_ht, 2 * i + b + 1)
                        act.wait_ge(s_r, i + 1)
                        act.copy(h2T[:, 4 * b:4 * b + 4].rearrange("p k t -> p (k t)"), ps[:, 4 + b]).then_inc(s_hte, 1)

                def square(i):
                    act.wait_ge(s_x1, i + 1)
                    act.activation(sq[:, :], x1[:, :], ACT.Square, accum_out=ss[:, :]).then_inc(s_sq, 1)
                    act.wait_ge(s_sq, i + 1)
                    act.activation(rs[:, :], ss[:, :], ACT.Sqrt, scale=1.0 / D, bias=c["eps"][:, :]).then_inc(s_rt, 1)

                cat_out(0)
                cat_out(1)
                square(0)
                with act.Fori(1, NT - 1) as i:
                    cat_out(i + 1)
                    h_out(i - 1)
                    square(i)
                h_out(NT - 2)
                square(NT - 1)
                h_out(NT - 1)

            @block.vector
            def _(dve):
                v = Steps(dve, s_v)
                dve.wait_ge(s_k, 80)
                v.then(dve.scalar_tensor_tensor(g2[:, :], c["mod"][:, 2], 1.0, g2[:, :], ALU.add, ALU.mult))
                start = v.n

                def logits(i):
                    dve.wait_ge(s_r, i + 2)
                    dve.tensor_tensor(c["lg"][:, ds(i, 1)], ps[:, 6:7, 0:NR], c["brt"][:, :].unsqueeze(1),
                                      ALU.add).then_inc(s_re, 1)

                def tile(i, first):
                    v.base, v.n = start + 4 * i, 0
                    dve.wait_ge(s_x, 16 * i + 16)
                    if not first:
                        dve.wait_ge(s_st, 32 * i)
                    for b in range(2):
                        dve.wait_ge(s_mm, 2 * i + b + 1)
                        cols = slice(b * HALF, (b + 1) * HALF)
                        v.did(dve.tensor_tensor(x1[:, cols], ps[:, 2 + b], c["mod"][:, 0, cols], ALU.mult))
                    v.done()
                    dve.nop().then_inc(s_y, 1)
                    dve.tensor_tensor(x1[:, :], x1[:, :], xt[:, :], ALU.add).then_inc(s_x1, 1)
                    if not first:
                        logits(i - 1)
                    dve.wait_ge(s_rt, i + 1)
                    v.then(dve.reciprocal(rs[:, :], rs[:, :]))
                    if not first:
                        dve.wait_ge(s_ht, 2 * i)
                    v.then(dve.scalar_tensor_tensor(h2[:, :], x1[:, :], rs[:, :], g2[:, :], ALU.mult, ALU.mult))
                    dve.tensor_tensor(h2[:, :], h2[:, :], c["mod"][:, 1], ALU.add).then_inc(s_h2, 1)

                tile(0, True)
                with dve.Fori(1, NT) as i:
                    tile(i, False)
                logits(NT - 1)

            @block.tensor
            def _(pe):
                def turn_cat(i):
                    pe.wait_ge(s_cat, 2 * i + 2)
                    for b in range(2):
                        if not (isinstance(i, int) and i == 0):
                            pe.wait_ge(s_cte, 2 * i - 1 + b)
                        for k in range(4):
                            last = pe.transpose(ps[:, b, k * P:(k + 1) * P],
                                                cat[:, (4 * b + k) * P:(4 * b + k + 1) * P], c["ident"][:, :])
                        last.then_inc(s_ct, 1)

                def product(i):
                    pe.wait_ge(s_cte, 2 * i + 2)
                    if not (isinstance(i, int) and i == 0):
                        pe.wait_ge(s_y, i)
                    for b in range(2):
                        for k in range(KD):
                            last = pe.matmul(ps[:, 2 + b], catT[:, k], wo[:, k, b * HALF:(b + 1) * HALF],
                                             start=(k == 0), stop=(k == KD - 1))
                        last.then_inc(s_mm, 1)

                def route(i):
                    pe.wait_ge(s_h2, i + 1)
                    for b in range(2):
                        pe.wait_ge(s_hte, 2 * i + 1 + b)
                        for k in range(4):
                            last = pe.transpose(ps[:, 4 + b, k * P:(k + 1) * P],
                                                h2[:, (4 * b + k) * P:(4 * b + k + 1) * P], c["ident"][:, :])
                        last.then_inc(s_ht, 1)
                    pe.wait_ge(s_hte, 2 * i + 4)
                    pe.wait_ge(s_re, i + 1)
                    for k in range(KD):
                        last = pe.matmul(ps[:, 6, 0:NR], h2T[:, k], wr[:, k], start=(k == 0), stop=(k == KD - 1))
                    last.then_inc(s_r, 1)

                for s, n in ((s_hte, 2), (s_re, 1), (s_r, 1)):
                    for _ in range(n):
                        pe.nop().then_inc(s, 1)
                turn_cat(0)
                pe.wait_ge(s_wo, 16)
                pe.wait_ge(s_k, 80)
                product(0)
                turn_cat(1)
                with pe.Fori(1, NT - 1) as i:
                    product(i)
                    turn_cat(i + 1)
                    route(i - 1)
                product(NT - 1)
                route(NT - 2)
                route(NT - 1)


def flat(ap):
    return ap.rearrange("p a n -> p (a n)")


def experts(nc, a, c, ps):
    with ExitStack() as m:
        def sb(name, shape, dt=F32):
            return m.enter_context(nc.sbuf_tensor(name, shape, dt))

        def sem(name):
            return m.enter_context(nc.semaphore(name))

        slot = sb("slot", [P, 2, NT], I32)
        wts = sb("wts", [P, 2, NT])
        wg = sb("wg", [P, 2, 2, KD, F])
        wd = sb("wd", [P, 2, KF, D])
        tok = sb("tok", [P, TS], I32)
        tile_e = sb("tile_e", [P, TS], I32)
        starts = sb("starts", [P, NE], I32)
        end = sb("end", [P, 1], I32)
        s_wg, s_wd = sem("e_wg"), sem("e_wd")
        w_gate = a["w_gate"][0].rearrange("e (k p) n -> e p k n", p=P)
        w_up = a["w_up"][0].rearrange("e (k p) n -> e p k n", p=P)
        w_down = a["w_down"][0].rearrange("e (k p) n -> e p k n", p=P)

        def load_gate(sp, e, slot_):
            w = w_gate[e:e + 1] if isinstance(e, int) else w_gate[ds(e, 1)]
            u = w_up[e:e + 1] if isinstance(e, int) else w_up[ds(e, 1)]
            for n, x in enumerate((w, u)):
                sp.dma_start(wg[:, slot_, n], x.rearrange("e p k n -> p (e k) n")).then_inc(s_wg, 16)

        def load_down(sp, e, slot_):
            w = w_down[e:e + 1] if isinstance(e, int) else w_down[ds(e, 1)]
            sp.dma_start(wd[:, slot_], w.rearrange("e p k n -> p (e k) n")).then_inc(s_wd, 16)

        with ExitStack() as r:
            def rb(name, shape, dt=F32):
                return r.enter_context(nc.sbuf_tensor(name, shape, dt))

            T4 = [P, NT, G]
            io4, io16, io32 = rb("io4", [P, G], I32), rb("io16", [P, NE], I32), rb("io32", [P, TS], I32)
            f4, f8, f32_ = rb("f4", [P, G]), rb("f8", [P, NT + 1]), rb("f32_", [P, TS])
            tokid = rb("tokid", [P, NT], I32)
            zero = rb("zero", [P, TS], I32)
            mx, sm, idx = rb("mx", [P, NT]), rb("sm", [P, NT]), rb("idx", [P, NT])
            t1, t2, w1 = rb("t1", [P, NT]), rb("t2", [P, NT]), rb("w1", [P, NT])
            d4, eq, ohg, oh1, oh2, ing = (rb(n, T4) for n in ("d4", "eq", "ohg", "oh1", "oh2", "ing"))
            prod = rb("prod", [P, NT, EG, G])
            o1, o2, mm, pm, rk = (rb(n, [P, NT, NE]) for n in ("o1", "o2", "mm_", "pm", "rk"))
            cnt, nt_, inc, exc = (rb(n, [P, NE]) for n in ("cnt", "nt_", "inc", "exc"))
            cmp8, cmpt = rb("cmp8", [P, NE, NT]), rb("cmpt", [P, TS, NE])
            posn, lane, div = rb("posn", [P, NT]), rb("lane", [P, NT], I32), rb("div", [P, NT], I32)
            where = rb("where", [P, 2, NT], I32)
            ef = rb("ef", [P, TS])
            s_v, s_po, s_ex, s_exd, s_tot, s_cnt, s_z, s_slot, s_sc, s_tab, s_d4 = (
                r.enter_context(nc.semaphore(f"r_{n}")) for n in
                ("v", "po", "ex", "exd", "tot", "cnt", "z", "slot", "sc", "tab", "d4"))
            L = c["lg"]

            with nc.Block() as block:
                @block.sync
                def _(sp):
                    sp.wait_ge(s_po, 5)
                    sp.dma_start(a["tok_dram"].rearrange("(p t) o -> p (t o)", t=TS), zero[:, :]).then_inc(s_z, 16)
                    for e in range(2):
                        load_gate(sp, e, e)
                        load_down(sp, e, e)
                    sp.wait_ge(s_sc, 16 * 2 * NT)
                    sp.dma_start(tok[:, :], a["tok_dram"].rearrange("(p t) o -> p (t o)", t=TS)).then_inc(s_tab, 16)
                    sp.wait_ge(s_tab, 16)
                    sp.wait_ge(s_wg, 64)
                    sp.wait_ge(s_wd, 32)

                @block.gpsimd
                def _(pool):
                    pool.iota(io4[:, :], [[1, G]], base=0, channel_multiplier=0).then_inc(s_po, 1)
                    pool.iota(io16[:, 0:NT + 1], [[P, NT + 1]], base=0, channel_multiplier=0).then_inc(s_po, 1)
                    pool.iota(io32[:, :], [[1, TS]], base=0, channel_multiplier=0).then_inc(s_po, 1)
                    pool.iota(tokid[:, :], [[P, NT]], base=0, channel_multiplier=1).then_inc(s_po, 1)
                    pool.memset(zero[:, :], 0).then_inc(s_po, 1)
                    pool.wait_ge(s_po, 5)
                    pool.wait_ge(s_z, 16)
                    pool.wait_ge(s_slot, 1)
                    for n in range(2):
                        for i in range(NT):
                            pool.indirect_dma_start(a["tok_dram"], bass.IndirectOffsetOnAxis(where[:, n, i:i + 1], 0),
                                                    tokid[:, i:i + 1], None).then_inc(s_sc, 16)

                @block.scalar
                def _(act):
                    act.wait_ge(s_d4, 1)
                    act.activation(d4[:, :, :], d4[:, :, :], ACT.Exp).then_inc(s_ex, 1)
                    act.wait_ge(s_exd, 1)
                    act.activation(w1[:, :], w1[:, :], ACT.Exp).then_inc(s_ex, 1)

                @block.vector
                def _(dve):
                    v = Steps(dve, s_v)

                    def choose(onehot, values, top):
                        v.then(dve.tensor_reduce(top[:, :], values[:, :, :], X, ALU.max))
                        v.then(dve.tensor_tensor(eq[:, :, :], values[:, :, :], over(top[:, :], 2, T4), ALU.is_equal))
                        v.then(dve.tensor_scalar(eq[:, :, :], eq[:, :, :], -float(G), float(G), ALU.mult, ALU.add))
                        v.then(dve.tensor_tensor(eq[:, :, :], eq[:, :, :], over(f4[:, :], 1, T4), ALU.add))
                        v.then(dve.tensor_reduce(idx[:, :], eq[:, :, :], X, ALU.min))
                        v.then(dve.tensor_tensor(onehot[:, :, :], eq[:, :, :], over(idx[:, :], 2, T4), ALU.is_equal))

                    dve.wait_ge(s_po, 5)
                    v.did(dve.tensor_copy(f4[:, :], io4[:, :]))
                    v.did(dve.tensor_copy(f8[:, :], io16[:, 0:NT + 1]))
                    v.did(dve.tensor_copy(f32_[:, :], io32[:, :]))
                    v.done()
                    gl = L[:, :, 0:G]
                    choose(ohg, gl, mx)
                    v.did(dve.tensor_tensor(d4[:, :, :], gl, over(mx[:, :], 2, T4), ALU.subtract))
                    v.done()
                    dve.nop().then_inc(s_d4, 1)
                    v.then(dve.tensor_tensor(prod[:, :, :, :],
                                             L[:, :, G:NR].rearrange("p t (g e) -> p t e g", g=G),
                                             over(ohg[:, :, :], 2, [P, NT, EG, G]), ALU.mult))
                    v.then(dve.tensor_reduce(ing[:, :, :], prod[:, :, :, :], X, ALU.add))
                    choose(oh1, ing, t1)
                    v.then(dve.scalar_tensor_tensor(ing[:, :, :], oh1[:, :, :], -BIG, ing[:, :, :], ALU.mult, ALU.add))
                    choose(oh2, ing, t2)
                    v.then(dve.tensor_tensor(w1[:, :], t2[:, :], t1[:, :], ALU.subtract))
                    dve.nop().then_inc(s_exd, 1)
                    for o, oh in ((o1, oh1), (o2, oh2)):
                        v.did(dve.tensor_tensor(o[:, :, :].rearrange("p t (g e) -> p t g e", g=G),
                                                over(ohg[:, :, :], 3, [P, NT, G, EG]),
                                                over(oh[:, :, :], 2, [P, NT, G, EG]), ALU.mult))
                    v.did(dve.memset(pm[:, 0], 0.0))
                    v.done()
                    v.then(dve.tensor_tensor(mm[:, :, :], o1[:, :, :], o2[:, :, :], ALU.add))
                    for i in range(1, NT):
                        v.then(dve.tensor_tensor(pm[:, i], pm[:, i - 1], mm[:, i - 1], ALU.add))
                    v.then(dve.tensor_tensor(cnt[:, :], pm[:, NT - 1], mm[:, NT - 1], ALU.add))
                    dve.nop().then_inc(s_tot, 1)
                    dve.wait_ge(s_ex, 2)
                    v.then(dve.tensor_reduce(sm[:, :], d4[:, :, :], X, ALU.add))
                    v.then(dve.reciprocal(sm[:, :], sm[:, :]))
                    v.then(dve.tensor_scalar(t1[:, :], w1[:, :], 1.0, None, ALU.add))
                    v.then(dve.reciprocal(t1[:, :], t1[:, :]))
                    v.then(dve.tensor_tensor(wts[:, 0], t1[:, :], sm[:, :], ALU.mult))
                    v.then(dve.tensor_tensor(wts[:, 1], wts[:, 0], w1[:, :], ALU.mult))
                    dve.wait_ge(s_cnt, 1)
                    v.did(dve.tensor_copy(rk[:, :, :], ps[:, 0, 0:NT * NE].rearrange("p (t e) -> p t e", e=NE)))
                    v.then(dve.tensor_tensor(cmp8[:, :, :], over(ps[:, 1, 0:NE], 2, [P, NE, NT]),
                                             over(f8[:, 0:NT], 1, [P, NE, NT]), ALU.is_gt))
                    v.then(dve.tensor_reduce(nt_[:, :], cmp8[:, :, :], X, ALU.add))
                    v.then(dve.tensor_tensor_scan(inc[:, :], c["ones"][:, 0:NE], nt_[:, :], 0.0, ALU.mult, ALU.add))
                    v.then(dve.tensor_tensor(exc[:, :], inc[:, :], nt_[:, :], ALU.subtract))
                    v.did(dve.tensor_copy(starts[:, :], exc[:, :]))
                    v.did(dve.tensor_scalar(end[:, :], inc[:, NE - 1:NE], -1.0, None, ALU.add))
                    v.then(dve.tensor_tensor(cmpt[:, :, :], over(inc[:, :], 1, [P, TS, NE]),
                                             over(f32_[:, :], 2, [P, TS, NE]), ALU.is_le))
                    v.then(dve.tensor_reduce(ef[:, :], cmpt[:, :, :], X, ALU.add))
                    v.did(dve.tensor_scalar(tile_e[:, :], ef[:, :], float(NE - 1), None, ALU.min))
                    v.then(dve.tensor_scalar(exc[:, :], exc[:, :], float(P), None, ALU.mult))
                    v.then(dve.tensor_tensor(rk[:, :, :], rk[:, :, :], over(exc[:, :], 1, [P, NT, NE]), ALU.add))
                    for n, o in enumerate((o1, o2)):
                        v.then(dve.tensor_tensor(o[:, :, :], o[:, :, :], rk[:, :, :], ALU.mult))
                        v.then(dve.tensor_reduce(posn[:, :], o[:, :, :], X, ALU.add))
                        v.then(dve.tensor_copy(slot[:, n], posn[:, :]))
                        v.did(dve.tensor_scalar(lane[:, :], slot[:, n], P - 1, TS.bit_length() - 1, ALU.bitwise_and,
                                                ALU.logical_shift_left))
                        v.then(dve.tensor_scalar(div[:, :], slot[:, n], P.bit_length() - 1, None,
                                                 ALU.logical_shift_right))
                        v.then(dve.tensor_tensor(where[:, n], lane[:, :], div[:, :], ALU.bitwise_or))
                    dve.nop().then_inc(s_slot, 1)

                @block.tensor
                def _(pe):
                    pe.wait_ge(s_tot, 1)
                    flat3 = "p t e -> p (t e)"
                    pe.matmul(ps[:, 0, 0:NT * NE], c["before"][:, :], mm[:, :, :].rearrange(flat3), start=True, stop=False)
                    pe.matmul(ps[:, 0, 0:NT * NE], c["ones"][:, :], pm[:, :, :].rearrange(flat3), start=False, stop=True)
                    pe.matmul(ps[:, 1, 0:NE], c["ones"][:, :], cnt[:, :], start=True, stop=True).then_inc(s_cnt, 1)

        with ExitStack() as t_:
            def tb(name, shape, dt=F32):
                return t_.enter_context(nc.sbuf_tensor(name, shape, dt))

            rows = tb("rows", [P, 1], I32)
            xg, xT = tb("xg", [P, D]), tb("xT", [P, KD, P])
            sil, act_, aT = tb("sil", [P, F]), tb("act_", [P, F]), tb("aT", [P, KF, P])
            y = tb("y", [P, 2, D])
            (s_rows, s_gat, s_xt, s_xTe, s_gate, s_gud, s_sil, s_act, s_at, s_aTe, s_dnd, s_y0, s_y1, s_yst) = (
                t_.enter_context(nc.semaphore(f"t_{n}")) for n in
                ("rows", "gat", "xt", "xTe", "gate", "gud", "sil", "act", "at", "aTe", "dnd", "y0", "y1", "yst"))
            s_dn0 = t_.enter_context(nc.semaphore("t_dn0"))

            with nc.Block() as block:
                @block.sync
                def _(sp):
                    with sp.Fori(2, NE) as e:
                        n = sp.value_load(starts[0:1, ds(e - 1, 1)], min_val=0, max_val=MAXT)
                        sp.wait_ge(s_gud, n + 1)
                        load_gate(sp, e, e % 2)
                        sp.wait_ge(s_dnd, n + 1)
                        load_down(sp, e, e % 2)
                        wait_alone(sp, s_wg, e * 32 + 32)
                        wait_alone(sp, s_wd, e * 16 + 16)

                @block.gpsimd
                def _(pool):
                    def fetch(t):
                        pool.tensor_copy(rows[:, :], tok[:, ds(t, 1)]).then_inc(s_rows, 1)
                        wait_alone(pool, s_rows, t + 1)
                        pool.indirect_dma_start(xg[:, :], None, a["h2_dram"],
                                                bass.IndirectOffsetOnAxis(rows[:, :], 0)).then_inc(s_gat, 16)

                    end_t = pool.value_load(end[0:1, 0:1], min_val=1, max_val=MAXT - 1)
                    fetch(0)
                    with pool.Fori(1, end_t + 2) as t:
                        pool.wait_ge(s_xt, t)
                        fetch(t)

                @block.scalar
                def _(act):
                    end_t = act.value_load(end[0:1, 0:1], min_val=1, max_val=MAXT - 1)
                    for s in (s_y0, s_yst):
                        act.nop().then_inc(s, 1)

                    def x_out(t):
                        for b in range(2):
                            act.wait_ge(s_xt, t + 1)
                            act.copy(xT[:, 4 * b:4 * b + 4].rearrange("p k t -> p (k t)"), ps[:, 4 + b]).then_inc(s_xTe, 1)

                    def gate_out(t):
                        act.wait_ge(s_gate, t + 1)
                        act.activation(sil[:, :], ps[:, 0], ACT.Silu).then_inc(s_sil, 1)

                    def a_out(t):
                        act.wait_ge(s_at, t + 1)
                        act.copy(aT[:, :, :].rearrange("p k t -> p (k t)"), ps[:, 6]).then_inc(s_aTe, 1)

                    def y_out(t):
                        act.wait_ge(s_dn0, t + 1)
                        act.copy(y[:, t % 2, 0:HALF], ps[:, 2]).then_inc(s_y0, 1)

                    def store(t):
                        act.wait_ge(s_y0, t + 2)
                        act.wait_ge(s_y1, t + 2)
                        act.wait_ge(s_yst, t * 16 + 1)
                        act.dma_start(a["y_dram"][ds(t * P, P), :], y[:, t % 2]).then_inc(s_yst, 16)

                    x_out(0)
                    gate_out(0)
                    act.wait_ge(s_gud, 2)
                    x_out(1)
                    a_out(0)
                    with act.Fori(1, end_t + 1) as t:
                        act.wait_ge(s_act, t)
                        gate_out(t)
                        act.wait_ge(s_gud, t + 2)
                        x_out(t + 1)
                        y_out(t - 1)
                        a_out(t)
                        store(t - 1)
                    y_out(end_t)
                    store(end_t)
                    wait_alone(act, s_yst, end_t * 16 + 17)

                @block.vector
                def _(dve):
                    end_t = dve.value_load(end[0:1, 0:1], min_val=1, max_val=MAXT - 1)
                    dve.nop().then_inc(s_y1, 1)

                    def gated(t):
                        dve.wait_ge(s_sil, t + 1)
                        dve.wait_ge(s_gud, t + 2)
                        dve.tensor_tensor(act_[:, :], sil[:, :], ps[:, 1], ALU.mult).then_inc(s_act, 1)

                    def y_out(t):
                        dve.wait_ge(s_dnd, t + 2)
                        dve.wait_ge(s_yst, t * 16 + 1)
                        dve.tensor_copy(y[:, t % 2, HALF:], ps[:, 3]).then_inc(s_y1, 1)

                    gated(0)
                    with dve.Fori(1, end_t + 1) as t:
                        dve.wait_ge(s_at, t)
                        gated(t)
                        y_out(t - 1)
                    y_out(end_t)

                @block.tensor
                def _(pe):
                    end_t = pe.value_load(end[0:1, 0:1], min_val=1, max_val=MAXT - 1)
                    for s in (s_gud, s_dnd):
                        pe.nop().then_inc(s, 1)

                    def turn_x(t):
                        pe.wait_ge(s_gat, 16 * t + 16)
                        for k in range(KD):
                            last = pe.transpose(ps[:, 4 + k // 4, (k % 4) * P:(k % 4 + 1) * P],
                                                xg[:, k * P:(k + 1) * P], c["ident"][:, :])
                        last.then_inc(s_xt, 1)

                    def gate_up(t):
                        e = pe.value_load(tile_e[0:1, ds(t, 1)], min_val=0, max_val=NE - 1)
                        pe.wait_ge(s_wg, e * 32 + 32)
                        pe.wait_ge(s_xTe, 2 * t + 2)
                        if not isinstance(t, int):
                            pe.wait_ge(s_act, t)
                        w = pe.snap(e % 2)
                        for g, done in ((0, s_gate), (1, s_gud)):
                            for k in range(KD):
                                last = pe.matmul(ps[:, g], xT[:, k], wg[:, ds(w, 1), g, k].rearrange("p a n -> p (a n)"),
                                                 start=(k == 0), stop=(k == KD - 1))
                            last.then_inc(done, 1)

                    def down(t):
                        e = pe.value_load(tile_e[0:1, ds(t, 1)], min_val=0, max_val=NE - 1)
                        pe.wait_ge(s_wd, e * 16 + 16)
                        pe.wait_ge(s_aTe, t + 1)
                        pe.wait_ge(s_y0, t + 1)
                        pe.wait_ge(s_y1, t + 1)
                        w = pe.snap(e % 2)
                        for b, done in ((0, s_dn0), (1, s_dnd)):
                            for k in range(KF):
                                last = pe.matmul(ps[:, 2 + b], aT[:, k],
                                                 wd[:, ds(w, 1), k, b * HALF:(b + 1) * HALF].rearrange("p a n -> p (a n)"),
                                                 start=(k == 0), stop=(k == KF - 1))
                            last.then_inc(done, 1)

                    def turn_a(t):
                        pe.wait_ge(s_act, t + 1)
                        for k in range(KF):
                            last = pe.transpose(ps[:, 6, k * P:(k + 1) * P], act_[:, k * P:(k + 1) * P], c["ident"][:, :])
                        last.then_inc(s_at, 1)

                    turn_x(0)
                    gate_up(0)
                    turn_x(1)
                    turn_a(0)
                    with pe.Fori(1, end_t + 1) as t:
                        gate_up(t)
                        turn_x(t + 1)
                        down(t - 1)
                        turn_a(t)
                    down(end_t)

        with ExitStack() as t_:
            def tb(name, shape, dt=F32):
                return t_.enter_context(nc.sbuf_tensor(name, shape, dt))

            y1, y2, xo, ro = (tb(n, [P, 2, D]) for n in ("cy1", "cy2", "cx", "cr"))
            s_y1, s_y1b, s_x, s_xb, s_v, s_out, s_done, s_ro = (
                t_.enter_context(nc.semaphore(f"c_{n}")) for n in ("y1", "y1b", "x", "xb", "v", "out", "done", "ro"))
            y_sem, x_sem = [s_y1, s_y1b], [s_x, s_xb]
            out = a["out"].rearrange("b s d -> (b s) d")
            with nc.Block() as block:
                @block.gpsimd
                def _(pool):
                    for i in range(NT):
                        if i >= 2:
                            pool.wait_ge(s_done, i - 1)
                        for n, yy in enumerate((y1, y2)):
                            pool.indirect_dma_start(yy[:, i % 2], None, a["y_dram"],
                                                    bass.IndirectOffsetOnAxis(slot[:, n, i:i + 1], 0)).then_inc(y_sem[i % 2], 16)

                @block.sync
                def _(sp):
                    for i in range(NT):
                        if i >= 2:
                            sp.wait_ge(s_ro, i - 1)
                        sp.dma_start(xo[:, i % 2], a["x1_dram"][i * P:(i + 1) * P, :]).then_inc(x_sem[i % 2], 16)

                @block.scalar
                def _(act):
                    for i in range(NT):
                        act.wait_ge(s_ro, i + 1)
                        act.dma_start(out[i * P:(i + 1) * P, :], ro[:, i % 2]).then_inc(s_out, 16)
                        act.wait_ge(s_out, 16 * i + 16)

                @block.vector
                def _(dve):
                    v = Steps(dve, s_v)
                    for i in range(NT):
                        j = i % 2
                        r_ = ro[:, j]
                        dve.wait_ge(y_sem[j], 32 * (i // 2 + 1))
                        if i >= 2:
                            dve.wait_ge(s_out, 16 * (i - 1))
                        v.then(dve.tensor_scalar(r_, y1[:, j], wts[:, 0, i:i + 1], None, ALU.mult))
                        dve.scalar_tensor_tensor(r_, y2[:, j], wts[:, 1, i:i + 1], r_, ALU.mult,
                                                 ALU.add).then_inc(s_done, 1)
                        dve.wait_ge(s_done, i + 1)
                        v.then(dve.tensor_tensor(r_, r_, c["mod"][:, 3], ALU.mult))
                        dve.wait_ge(x_sem[j], 16 * (i // 2 + 1))
                        dve.tensor_tensor(r_, r_, xo[:, j], ALU.add).then_inc(s_ro, 1)


_INS = ["x", "c", "w_ada", "b_ada", "norm1_g", "w_in", "b_fox", "q_norm_g", "k_norm_g", "attn_out_g",
        "hgrn_lb", "hgrn_out_g", "w_out", "norm2_g", "w_router_group", "b_router_group",
        "w_router_expert", "b_router_expert", "w_gate", "w_up", "w_down"]


def kernel(**inputs):
    import numpy as _np
    import concourse.bacc as _bacc
    from concourse import mybir as _mybir
    from concourse.bass_utils import run_bass_kernel_spmd as _run

    nc = _bacc.Bacc("TRN2", target_bir_lowering=False, num_devices=1)
    arrays, args = {}, {}
    for name in _INS:
        arr = _np.ascontiguousarray(inputs[name])
        arrays[f"in_{name}_dram"] = arr
        args[name] = nc.dram_tensor(f"in_{name}_dram", arr.shape, _mybir.dt.from_np(arr.dtype), kind="ExternalInput").ap()
    args["out"] = nc.dram_tensor("out_dram", (1, SEQ, D), _mybir.dt.float32, kind="ExternalOutput").ap()
    for name, shape, dt in (("x1_dram", (SEQ, D), F32), ("h2_dram", (SEQ, D), F32),
                            ("y_dram", (MAXT * P, D), F32), ("tok_dram", (P * TS, 1), I32)):
        args[name] = nc.dram_tensor(name, shape, dt, kind="Internal").ap()
    build(nc, args)
    r = _run(nc, [arrays], core_ids=[0])
    return r.results[0]["out_dram"]
```

```python
from contextlib import ExitStack

import concourse.bass as bass
from concourse import mybir

P = 128
D = 1024
KD = D // P
SEQ = 1024
NT = SEQ // P
HALF = 512
AH, DH = 8, 64
AW = AH * DH
AUG = DH + 2
GH, DK = 4, 128
GW = GH * DK
LEVELS = 7
G, EG = 4, 4
NE = G * EG
NR = G + NE
F = 512
KF = F // P
MINT = 2 * SEQ // P
MAXT = 2 * SEQ // P + NE - 1
TS = 32
EPS = 1e-6
BIG = 3.0e38
FAR = 1.0e30

C_AQ, C_AK, C_AV, C_AF = 0, AW, 2 * AW, 3 * AW
C_HQ = 3 * AW + AH
C_HF, C_HI, C_HG = C_HQ + GW, C_HQ + 2 * GW, C_HQ + 3 * GW

F32 = mybir.dt.float32
F32R = mybir.dt.float32r
I32 = mybir.dt.int32
ALU = mybir.AluOpType
ACT = mybir.ActivationFunctionType
X = mybir.AxisListType.X
ds = bass.ds


class Steps:

    def __init__(self, eng, sem):
        self.eng, self.sem, self.base, self.n = eng, sem, 0, 0

    def did(self, ins):
        ins.then_inc(self.sem, 1)
        self.n += 1

    def done(self):
        self.eng.wait_ge(self.sem, self.base + self.n)

    def then(self, ins):
        self.did(ins)
        self.done()

    def then_alone(self, ins):
        self.did(ins)
        wait_alone(self.eng, self.sem, self.base + self.n)


def wait_alone(eng, sem, value):
    eng.wait_ge(sem, value)
    eng.nop().then_inc(PASSED[0], 1)


PASSED = []


def one(ap, keep=0):
    if len(ap.shape) == 3 + keep:
        return ap.rearrange("p a c t -> p (a c) t" if keep else "p a t -> p (a t)")
    return ap


def over(ap, axis, shape):
    return ap.unsqueeze(axis).broadcast_to(shape)


def build(nc, a):
    with ExitStack() as kernel_memory:
        def keep(name, shape, dt=F32):
            return kernel_memory.enter_context(nc.sbuf_tensor(name, shape, dt))

        PASSED[:] = [kernel_memory.enter_context(nc.semaphore("passed"))]
        ps = kernel_memory.enter_context(nc.psum_tensor("ps", [P, 8, HALF], F32))
        c = {
            "ident": keep("ident", [P, P]),
            "ones": keep("ones", [P, P]),
            "upto": keep("upto", [P, P]),
            "before": keep("before", [P, P]),
            "causal": keep("causal", [P, P]),
            "cum": keep("cum", [P, NT, AH]),
            "ncum": keep("ncum", [P, NT, AH]),
            "eps": keep("eps", [P, 1]),
            "lg": keep("lg", [P, NT, NR]),
            "brt": keep("brt", [P, NR]),
            "mod": keep("mod", [P, 4, D]),
        }
        with ExitStack() as m:
            for n in ("ao", "ho"):
                c[n] = m.enter_context(nc.sbuf_tensor(n, [P, NT, AW], F32))
            with ExitStack() as mh:
                c["hT"] = mh.enter_context(nc.sbuf_tensor("hT", [P, KD, SEQ], F32))
                c["csil"] = mh.enter_context(nc.sbuf_tensor("csil", [P, KD, P], F32))
                normalise(nc, a, c, ps)
                hgrn(nc, a, c, ps)
                attention(nc, a, c, ps)
            project_out(nc, a, c, ps)
        experts(nc, a, c, ps)


def normalise(nc, a, c, ps):
    with ExitStack() as m:
        def sb(name, shape, dt=F32):
            return m.enter_context(nc.sbuf_tensor(name, shape, dt))

        def sem(name):
            return m.enter_context(nc.semaphore(name))

        ccol, cexp, crec = (sb(n, [P, KD]) for n in ("ccol", "cexp", "crec"))
        wada = sb("wada1", [P, 2, KD, HALF])
        brow = sb("brow1", [1, 2, HALF])
        g1 = sb("g1", [P, D])
        sh = sb("sh", [P, 2, D])
        xt = sb("xt", [P, 2, D])
        sq = sb("sq", [P, D])
        h = sb("h", [P, D])
        ss, rs = sb("ss", [P, NT]), sb("rs", [P, NT])
        waf = sb("waf", [P, KD, AH])
        bfox = sb("bfox", [P, AH])
        z, mn, ab, pre = (sb(n, [P, NT, AH]) for n in ("z", "mn", "ab", "pre"))
        lf = sb("lf", [P, NT, AH])

        s_c, s_g, s_w, s_w2, s_x, s_x2, s_af = (sem(f"n_{n}") for n in ("c", "g", "w", "w2", "x", "x2", "af"))
        s_const, s_csil, s_row = (sem(f"n_{n}") for n in ("const", "csil", "row"))
        s_sq, s_h, s_tr, s_ev = (sem(f"n_{n}") for n in ("sq", "h", "tr", "ev"))
        s_cexp, s_v, s_z, s_ab, s_lf, s_cum, s_free, s_pool = (
            sem(f"n_{n}") for n in ("cexp", "v", "z", "ab", "lf", "cum", "free", "pool"))
        s_a, s_eps, s_rt = sem("n_a"), sem("n_eps"), sem("n_rt")
        x3 = a["x"].rearrange("b (t p) d -> (b t) p d", p=P)
        w_ada = a["w_ada"][0].rearrange("(p k) n -> p k n", k=KD)
        w_in = a["w_in"][0].rearrange("(k p) n -> p k n", p=P)
        w_sem = [s_w, s_w2]
        x_sem = [s_x, s_x2]

        with nc.Block() as block:
            @block.sync
            def _(sp):
                sp.dma_start(ccol[:, :], a["c"][0].rearrange("(p k) -> p k", k=KD)).then_inc(s_c, 16)
                for r in range(2):
                    sp.dma_start(wada[:, r], w_ada[:, :, r * HALF:(r + 1) * HALF]).then_inc(w_sem[r], 16)
                    sp.dma_start(brow[:, r], a["b_ada"][0:1, r * HALF:(r + 1) * HALF]).then_inc(w_sem[r], 16)
                for i in range(2):
                    sp.dma_start(xt[:, i], x3[i]).then_inc(x_sem[i], 16)
                sp.dma_start(g1[:, :], a["norm1_g"][0].partition_broadcast(P)).then_inc(s_g, 16)
                for r in range(2, 4):
                    sp.wait_ge(s_row, r - 1)
                    sp.dma_start(wada[:, r % 2], w_ada[:, :, r * HALF:(r + 1) * HALF]).then_inc(w_sem[r % 2], 16)
                    sp.dma_start(brow[:, r % 2], a["b_ada"][0:1, r * HALF:(r + 1) * HALF]).then_inc(w_sem[r % 2], 16)
                sp.dma_start(waf[:, :, :], w_in[:, :, C_AF:C_AF + AH]).then_inc(s_af, 16)
                sp.dma_start(bfox[:, :], a["b_fox"][0].partition_broadcast(P)).then_inc(s_af, 16)
                for i in range(2, NT):
                    sp.wait_ge(s_free, i - 1)
                    sp.dma_start(xt[:, i % 2], x3[i]).then_inc(x_sem[i % 2], 16)

            @block.gpsimd
            def _(pool):
                v = Steps(pool, s_pool)
                v.did(pool.memset(c["ident"][:, :], 0.0))
                v.did(pool.memset(c["ones"][:, :], 1.0))
                pool.memset(c["eps"][:, :], EPS).then_inc(s_eps, 1)
                v.did(pool.memset(c["upto"][:, :], 1.0))
                v.did(pool.memset(c["before"][:, :], 1.0))
                v.then(pool.memset(c["causal"][:, :], 0.0))
                def keep_where(t, op, fill):
                    pool.affine_select(out=t[:, :], in_=t[:, :], compare_op=op, fill=fill, base=0,
                                       pattern=[[1, P]], channel_multiplier=-1).then_inc(s_const, 1)
                keep_where(c["ident"], ALU.not_equal, 1.0)
                keep_where(c["upto"], ALU.is_ge, 0.0)
                keep_where(c["before"], ALU.is_gt, 0.0)
                pool.affine_select(out=c["causal"][:, :], in_=c["causal"][:, :], compare_op=ALU.is_ge, fill=-FAR,
                                   base=0, pattern=[[-1, P]], channel_multiplier=1).then_inc(s_const, 1)

            @block.scalar
            def _(act):
                act.wait_ge(s_c, 16)
                act.activation(cexp[:, :], ccol[:, :], ACT.Exp, scale=-1.0).then_inc(s_cexp, 1)
                for i in range(NT):
                    act.wait_ge(x_sem[i % 2], 16 * (i // 2 + 1))
                    if i:
                        act.wait_ge(s_sq, i)
                    act.activation(sq[:, :], xt[:, i % 2], ACT.Square, accum_out=ss[:, i:i + 1]).then_inc(s_sq, 1)
                    act.wait_ge(s_sq, i + 1)
                    act.wait_ge(s_eps, 1)
                    act.activation(rs[:, i:i + 1], ss[:, i:i + 1], ACT.Sqrt, scale=1.0 / D,
                                   bias=c["eps"][:, :]).then_inc(s_rt, 1)
                    if i:
                        for b in range(2):
                            act.wait_ge(s_tr, 2 * i - 1 + b)
                            act.copy(c["hT"][:, 4 * b:4 * b + 4, (i - 1) * P:i * P],
                                     ps[:, 4 + b].rearrange("p (k t) -> p k t", t=P)).then_inc(s_ev, 1)
                for b in range(2):
                    act.wait_ge(s_tr, 2 * NT - 1 + b)
                    act.copy(c["hT"][:, 4 * b:4 * b + 4, (NT - 1) * P:],
                             ps[:, 4 + b].rearrange("p (k t) -> p k t", t=P)).then_inc(s_ev, 1)
                act.wait_ge(s_ab, 1)
                act.activation(ab[:, :, :], ab[:, :, :], ACT.Exp, scale=-1.0).then_inc(s_a, 1)
                act.wait_ge(s_a, 1)
                act.activation(ab[:, :, :], ab[:, :, :], ACT.Ln, bias=1.0).then_inc(s_lf, 1)

            @block.vector
            def _(dve):
                v = Steps(dve, s_v)
                dve.wait_ge(s_cexp, 1)
                v.then(dve.tensor_scalar(crec[:, :], cexp[:, :], 1.0, None, ALU.add))
                v.then(dve.reciprocal(crec[:, :], crec[:, :]))
                v.then(dve.tensor_tensor(crec[:, :], crec[:, :], ccol[:, :], ALU.mult))
                dve.tensor_copy(c["csil"][:, :, :], over(crec[:, :], 2, [P, KD, P])).then_inc(s_csil, 1)
                for r in range(4):
                    dve.wait_ge(s_row, r + 1)
                    v.did(dve.tensor_copy(sh[:, r // 2, (r % 2) * HALF:(r % 2 + 1) * HALF], ps[:, r % 2]))
                dve.wait_ge(s_g, 16)
                v.done()
                v.then(dve.scalar_tensor_tensor(sh[:, 1], sh[:, 1], 1.0, g1[:, :], ALU.add, ALU.mult))
                for i in range(NT):
                    dve.wait_ge(s_rt, i + 1)
                    v.then(dve.reciprocal(rs[:, i:i + 1], rs[:, i:i + 1]))
                    if i:
                        dve.wait_ge(s_tr, 2 * i)
                    dve.scalar_tensor_tensor(h[:, :], xt[:, i % 2], rs[:, i:i + 1], sh[:, 1],
                                             ALU.mult, ALU.mult).then_inc(s_free, 1)
                    dve.wait_ge(s_free, i + 1)
                    dve.tensor_tensor(h[:, :], h[:, :], sh[:, 0], ALU.add).then_inc(s_h, 1)
                dve.wait_ge(s_af, 32)
                dve.wait_ge(s_z, 1)
                v.then(dve.tensor_tensor(z[:, :, :], ps[:, 6, 0:NT * AH].rearrange("p (t h) -> p t h", h=AH),
                                         over(bfox[:, :], 1, [P, NT, AH]), ALU.add))
                v.did(dve.tensor_scalar(mn[:, :, :], z[:, :, :], 0.0, None, ALU.min))
                dve.scalar_tensor_tensor(ab[:, :, :], z[:, :, :], -1.0, z[:, :, :], ALU.mult, ALU.max).then_inc(s_ab, 1)
                dve.wait_ge(s_lf, 1)
                v.done()
                v.did(dve.memset(pre[:, 0, :], 0.0))
                v.then(dve.tensor_tensor(lf[:, :, :], mn[:, :, :], ab[:, :, :], ALU.subtract))
                for i in range(1, NT):
                    v.then(dve.tensor_tensor(pre[:, i], pre[:, i - 1], lf[:, i - 1], ALU.add))
                dve.nop().then_inc(s_cum, 1)
                dve.wait_ge(s_z, 2)
                cm = ps[:, 7, 0:NT * AH].rearrange("p (t h) -> p t h", h=AH)
                v.did(dve.tensor_copy(c["cum"][:, :, :], cm))
                v.then(dve.tensor_scalar(c["ncum"][:, :, :], cm, -1.0, None, ALU.mult))

            @block.tensor
            def _(pe):
                pe.wait_ge(s_const, 4)
                pe.wait_ge(s_csil, 1)
                for r in range(4):
                    pe.wait_ge(w_sem[r % 2], 32 * (r // 2 + 1))
                    if r >= 2:
                        pe.wait_ge(s_v, 3 + r - 1)
                    for k in range(KD):
                        pe.matmul(ps[:, r % 2], c["csil"][:, k], wada[:, r % 2, k], start=(k == 0), stop=False)
                    pe.matmul(ps[:, r % 2], c["ones"][0:1, :], brow[0:1, r % 2], start=False,
                              stop=True).then_inc(s_row, 1)
                for i in range(NT):
                    pe.wait_ge(s_h, i + 1)
                    for b in range(2):
                        if i:
                            pe.wait_ge(s_ev, 2 * i - 1 + b)
                        for k in range(4):
                            last = pe.transpose(ps[:, 4 + b, k * P:(k + 1) * P],
                                                h[:, (4 * b + k) * P:(4 * b + k + 1) * P], c["ident"][:, :])
                        last.then_inc(s_tr, 1)
                pe.wait_ge(s_ev, 2 * NT)
                pe.wait_ge(s_af, 32)
                for i in range(NT):
                    for k in range(KD):
                        last = pe.matmul(ps[:, 6, i * AH:(i + 1) * AH], c["hT"][:, k, i * P:(i + 1) * P],
                                         waf[:, k], start=(k == 0), stop=(k == KD - 1))
                last.then_inc(s_z, 1)
                pe.wait_ge(s_cum, 1)
                pe.matmul(ps[:, 7, 0:NT * AH], c["upto"][:, :], lf[:, :, :].rearrange("p t h -> p (t h)"),
                          start=True, stop=False)
                pe.matmul(ps[:, 7, 0:NT * AH], c["ones"][:, :], pre[:, :, :].rearrange("p t h -> p (t h)"),
                          start=False, stop=True).then_inc(s_z, 1)


def hgrn(nc, a, c, ps):
    with ExitStack() as m:
        def sb(name, shape, dt=F32):
            return m.enter_context(nc.sbuf_tensor(name, shape, dt))

        def sem(name):
            return m.enter_context(nc.semaphore(name))

        wt = sb("wt", [P, KD, 2, DK])
        wv = sb("wv", [P, KD, 2, DK])
        uf = sb("uf", [P, 2, SEQ])
        uq = sb("uq", [P, 2, SEQ])
        xq = sb("xq", [P, 2, SEQ])
        xv = sb("xv", [P, 2, NT, 2 * DK])
        ug = sb("ug", [P, 2, NT, DK])
        kend = sb("kend", [P, SEQ])
        qe = sb("qe", [P, SEQ])
        ecum = sb("ecum", [P, SEQ])
        lev = sb("lev", [P, LB, SEQ])
        sc = sb("sc", [P, NT, P])
        kx = sb("kx", [P, NT, P])
        st = sb("st", [P, NT, DK])
        masks = sb("masks", [P, LEVELS, P], I32)
        ti, si = sb("ti", [P, P], I32), sb("si", [P, P], I32)
        tf, ge = sb("tf", [P, P]), sb("ge", [P, LEVELS + 1, P])
        reset = sb("reset", [P, SEQ], mybir.dt.bfloat16)
        lbx, lbw, lb, oml = sb("lbx", [P, 2, GH]), sb("lbw", [P, 2, GH]), sb("lb", [P, GH]), sb("oml", [P, GH])
        gout = sb("gout", [P, GW])
        ss, rs = sb("hss", [P, NT]), sb("hrs", [P, NT])

        s_wt, s_wv, s_k = sem("h_wt"), sem("h_wv"), sem("h_k")
        s_pj, s_pje = sem("h_pj"), sem("h_pje")
        s_tri, s_e = sem("h_tri"), sem("h_e")
        s_v, s_a, s_ka = sem("h_v"), sem("h_a"), sem("h_ka")
        s_f, s_lf, s_dk, s_ek, s_ec = (sem(f"h_{n}") for n in ("f", "lf", "dk", "ek", "ec"))
        s_d, s_x, s_l = (sem(f"h_{n}") for n in ("d", "x", "l"))
        s_kend, s_kt, s_kte, s_u, s_st = (sem(f"h_{n}") for n in ("kend", "kt", "kte", "u", "st"))
        s_g, s_ge, s_o, s_os, s_oe, s_qk, s_po = (sem(f"h_{n}") for n in ("g", "ge", "o", "os", "oe", "qk", "po"))
        s_kc = sem("h_kc")
        s_sub, s_raw, s_ss, s_rt = sem("h_sub"), sem("h_raw"), sem("h_ss"), sem("h_rt")
        w_in = a["w_in"][0].rearrange("(k p) n -> p k n", p=P)
        UNITS = 4 + NT
        GR = [0, 2]

        with nc.Block() as block:
            @block.sync
            def _(sp):
                sp.dma_start(lbx[:, :, :], a["hgrn_lb"].rearrange("l (h p) -> p l h", p=P),
                             allow_slow_non_contiguous=True).then_inc(s_k, 16)
                sp.dma_start(gout[:, :], a["hgrn_out_g"][0].partition_broadcast(P)).then_inc(s_k, 16)

                def load_t(h):
                    sp.dma_start(wt[:, :, 0], w_in[:, :, ds(h * DK + C_HF, DK)]).then_inc(s_wt, 16)
                    sp.dma_start(wt[:, :, 1], w_in[:, :, ds(h * DK + C_HQ, DK)]).then_inc(s_wt, 16)

                def load_v(h):
                    sp.dma_start(wv[:, :, 0], w_in[:, :, ds(h * DK + C_HI, DK)]).then_inc(s_wv, 16)
                    sp.dma_start(wv[:, :, 1], w_in[:, :, ds(h * DK + C_HG, DK)]).then_inc(s_wv, 16)

                load_t(0)
                load_v(0)
                with sp.Fori(1, GH) as h:
                    sp.wait_ge(s_pj, h * UNITS - UNITS + 4)
                    load_t(h)
                    sp.wait_ge(s_pj, h * UNITS)
                    load_v(h)

            @block.gpsimd
            def _(pool):
                pool.iota(ti[:, :], [[1, P]], base=0, channel_multiplier=0).then_inc(s_po, 1)
                pool.iota(si[:, :], [[0, P]], base=0, channel_multiplier=1).then_inc(s_po, 1)
                pool.memset(reset[:, :], 1.0).then_inc(s_po, 1)
                pool.wait_ge(s_po, 3)
                pool.memset(reset[:, :].rearrange("p (c t) -> p c t", t=P)[:, :, 0:1], 0.0).then_inc(s_po, 1)

            @block.scalar
            def _(act):
                act.wait_ge(s_k, 32)
                act.wait_ge(s_sub, 1)
                act.activation(lbw[:, :, :], lbw[:, :, :], ACT.Exp).then_inc(s_a, 1)

                def copy_out(u, h, par):
                    act.wait_ge(s_pj, h * UNITS + u + 1)
                    bank = ps[:, 6 + u % 2]
                    if u == 0:
                        act.wait_ge(s_raw, h + 1)
                    if u < 2:
                        act.activation(uf[:, par, u * HALF:(u + 1) * HALF], bank, ACT.Exp,
                                       scale=-1.0).then_inc(s_pje, 1)
                    elif u < 4:
                        b = u - 2
                        act.copy(xq[:, par, b * HALF:(b + 1) * HALF], bank).then_inc(s_e, 1)
                        act.activation(uq[:, par, b * HALF:(b + 1) * HALF], bank, ACT.Exp,
                                       scale=-1.0).then_inc(s_pje, 1)
                    else:
                        act.copy(xv[:, par, u - 4], bank[:, 0:2 * DK]).then_inc(s_e, 1)
                        act.activation(ug[:, par, u - 4], bank[:, DK:2 * DK], ACT.Exp,
                                       scale=-1.0).then_inc(s_pje, 1)

                def factor(l, h):
                    act.wait_ge(s_d, h * LEVELS + l + 1)
                    act.activation(lev[:, l % LB], lev[:, l % LB], ACT.Exp).then_inc(s_x, 1)

                def log_f(h):
                    act.wait_ge(s_f, h + 1)
                    act.activation(kend[:, :], kend[:, :], ACT.Ln).then_inc(s_lf, 1)

                def decays(h):
                    act.wait_ge(s_dk, h + 1)
                    act.activation(kend[:, :], kend[:, :], ACT.Exp).then_inc(s_ek, 1)
                    act.activation(ecum[:, :], one(uf[:, h % 2]), ACT.Exp).then_inc(s_ec, 1)

                def head(h, more):
                    nxt = (h + 1) % 2

                    def units(*us):
                        for u in us:
                            if more:
                                copy_out(u, h + 1, nxt)

                    for b in range(2):
                        act.wait_ge(s_kt, 2 * h + b + 1)
                        act.copy(kx[:, 4 * b:4 * b + 4], ps[:, b].rearrange("p (c t) -> p c t", t=P)).then_inc(s_kte, 1)
                    units(0)
                    for l in range(2, LEVELS):
                        factor(l, h)
                        units(*COPY_AFTER[l])
                        if l == 4 and more:
                            log_f(h + 1)
                    if more:
                        decays(h + 1)
                        units(10, 11)
                        factor(0, h + 1)
                        factor(1, h + 1)
                    for b in range(2):
                        act.wait_ge(s_o, 2 * h + b + 1)
                        act.activation(sc[:, 4 * b:4 * b + 4], ps[:, 4 + b].rearrange("p (c t) -> p c t", t=P),
                                       ACT.Square).then_inc(s_os, 1)
                    act.wait_ge(s_ss, h + 1)
                    act.activation(rs[:, :], ss[:, :], ACT.Sqrt, scale=1.0 / DK, bias=c["eps"][:, :]).then_inc(s_rt, 1)

                for u in range(UNITS):
                    copy_out(u, 0, 0)
                log_f(0)
                decays(0)
                factor(0, 0)
                factor(1, 0)
                with act.Fori(0, GH - 1) as h:
                    head(h, True)
                head(GH - 1, False)

            @block.vector
            def _(dve):
                dve.wait_ge(s_k, 32)
                v = Steps(dve, s_v)
                v.then(dve.tensor_tensor(lb[:, :], lbx[:, 0], lbx[:, 1], ALU.max))
                dve.tensor_tensor(lbw[:, :, :], lbx[:, :, :], over(lb[:, :], 1, [P, 2, GH]),
                                  ALU.subtract).then_inc(s_sub, 1)
                dve.wait_ge(s_a, 1)
                v.then(dve.tensor_tensor(oml[:, :], lbw[:, 0], lbw[:, 1], ALU.add))
                v.then(dve.reciprocal(oml[:, :], oml[:, :]))
                v.did(dve.tensor_tensor(lb[:, :], lbw[:, 0], oml[:, :], ALU.mult))
                v.then(dve.tensor_tensor(oml[:, :], lbw[:, 1], oml[:, :], ALU.mult))
                dve.wait_ge(s_po, 4)
                v.then(dve.tensor_tensor(ti[:, :], ti[:, :], si[:, :], ALU.bitwise_xor))
                v.then(dve.tensor_copy(tf[:, :], ti[:, :]))
                v.then(dve.tensor_tensor(tf[:, :], tf[:, :], c["before"][:, :], ALU.mult))
                for l in range(LEVELS + 1):
                    v.did(dve.tensor_scalar(ge[:, l], tf[:, :], float(1 << l), None, ALU.is_ge))
                v.done()
                v.did(dve.tensor_tensor(masks[:, :, :], ge[:, 0:LEVELS], ge[:, 1:], ALU.subtract))
                v.did(dve.memset(st[:, 0], 0.0))
                v.done()

                def sigmoid_f(h):
                    dve.wait_ge(s_pje, h * UNITS + 2)
                    u = one(uf[:, h % 2])
                    v.then_alone(dve.tensor_scalar(u, u, 1.0, None, ALU.add))
                    v.did(dve.reciprocal(u, u))

                def gates(h):
                    q, u, k = one(xq[:, h % 2]), one(uf[:, h % 2]), one(uq[:, h % 2])
                    dve.wait_ge(s_pje, h * UNITS + 4)
                    dve.wait_ge(s_e, h * (UNITS - 2) + 2)
                    v.then_alone(dve.tensor_scalar(k, k, 1.0, None, ALU.add))
                    v.then_alone(dve.reciprocal(k, k))
                    v.then(dve.tensor_tensor(q, q, k, ALU.mult))
                    v.then(dve.tensor_scalar(kend[:, :], u, oml[:, ds(h, 1)], lb[:, ds(h, 1)], ALU.mult, ALU.add))
                    v.then(dve.tensor_scalar(k, kend[:, :], -1.0, 1.0, ALU.mult, ALU.add))
                    dve.nop().then_inc(s_f, 1)

                def running_sums(h):
                    cum = one(uf[:, h % 2])
                    dve.wait_ge(s_lf, h + 1)
                    v.then(dve.tensor_tensor_scan(cum, reset[:, :], kend[:, :], 0.0, ALU.mult, ALU.add))
                    cc = cum.rearrange("p (c t) -> p c t", t=P)
                    ke = kend[:, :].rearrange("p (c t) -> p c t", t=P)
                    dve.tensor_tensor(ke, cc[:, :, P - 1:P].broadcast_to([P, NT, P]), cc,
                                      ALU.subtract).then_inc(s_dk, 1)

                def keys_to_end(h):
                    dve.wait_ge(s_ek, h + 1)
                    dve.tensor_tensor(kend[:, :], kend[:, :], one(uq[:, h % 2]), ALU.mult).then_inc(s_kend, 1)

                def exponents(l, h):
                    half = 1 << l
                    cb = one(uf[:, h % 2]).rearrange("p (b w) -> p b w", w=2 * half)
                    lv = lev[:, l % LB].rearrange("p (b w) -> p b w", w=2 * half)
                    mid = cb[:, :, half - 1:half].broadcast_to([P, SEQ // (2 * half), half])
                    v.did(dve.tensor_tensor(lv[:, :, half:], cb[:, :, half:], mid, ALU.subtract))
                    dve.tensor_tensor(lv[:, :, 0:half], mid, cb[:, :, 0:half], ALU.subtract).then_inc(s_d, 1)
                    v.done()

                def factors(l, h):
                    half = 1 << l
                    lv, qb, kb = (t.rearrange("p (b w) -> p b w", w=2 * half)
                                  for t in (lev[:, l % LB], one(xq[:, h % 2]), one(uq[:, h % 2])))
                    dve.wait_ge(s_x, h * LEVELS + l + 1)
                    v.did(dve.tensor_tensor(lv[:, :, half:], lv[:, :, half:], qb[:, :, half:], ALU.mult))
                    v.then(dve.tensor_tensor(lv[:, :, 0:half], lv[:, :, 0:half], kb[:, :, 0:half], ALU.mult))
                    dve.nop().then_inc(s_l, 1)

                def take_scores(l, h):
                    wait_alone(dve, s_g, h * (LEVELS + 1) + l + 2)
                    for b in range(2):
                        v.did(dve.copy_predicated(
                            sc[:, 4 * b:4 * b + 4], over(masks[:, l], 1, [P, 4, P]),
                            ps[:, GR[(l + 1) % 2] + b].rearrange("p (c t) -> p c t", t=P)))
                    v.done()
                    dve.nop().then_inc(s_ge, 1)

                def first_buffers(h):
                    exponents(0, h)
                    exponents(1, h)
                    v.then(dve.tensor_scalar(lev[:, LB - 1], one(uq[:, h % 2]), 1.0, None, ALU.mult))
                    dve.nop().then_inc(s_kc, 1)

                def output_gate(h):
                    g, hg = one(ug[:, h % 2], 1), one(xv[:, h % 2], 1)
                    dve.wait_ge(s_pje, h * UNITS + UNITS)
                    dve.wait_ge(s_e, (h + 1) * (UNITS - 2))
                    v.then_alone(dve.tensor_scalar(g, g, 1.0, None, ALU.add))
                    v.then_alone(dve.reciprocal(g, g))
                    v.then(dve.tensor_tensor(g, g, hg[:, :, DK:], ALU.mult))
                    v.then(dve.tensor_tensor(g, g, over(gout[:, ds(h * DK, DK)], 1, [P, NT, DK]), ALU.mult))

                def output(h):
                    g = one(ug[:, h % 2], 1)
                    dve.wait_ge(s_os, 2 * h + 2)
                    dve.tensor_reduce(ss[:, :], sc[:, :, :], X, ALU.add).then_inc(s_ss, 1)
                    dve.wait_ge(s_rt, h + 1)
                    v.then(dve.reciprocal(rs[:, :], rs[:, :]))
                    v.then(dve.tensor_tensor(g, g, over(rs[:, :], 2, [P, NT, DK]), ALU.mult))
                    for b in range(2):
                        v.did(dve.tensor_tensor(c["ho"][:, 4 * b:4 * b + 4, ds(h * DK, DK)],
                                                ps[:, 4 + b].rearrange("p (c t) -> p c t", t=P),
                                                g[:, 4 * b:4 * b + 4], ALU.mult))
                    v.done()
                    dve.nop().then_inc(s_oe, 1)
                    dve.nop().then_inc(s_raw, 1)

                def head(h, more):
                    v.base, v.n = before_heads + h * V_STEPS, 0
                    factors(0, h)
                    exponents(2, h)
                    factors(1, h)
                    wait_alone(dve, s_g, h * (LEVELS + 1) + 1)
                    for b in range(2):
                        v.did(dve.tensor_tensor(sc[:, 4 * b:4 * b + 4], ps[:, GR[0] + b].rearrange("p (c t) -> p c t", t=P),
                                                over(c["ident"][:, :], 1, [P, 4, P]), ALU.mult))
                    v.done()
                    dve.nop().then_inc(s_ge, 1)
                    exponents(3, h)
                    factors(2, h)
                    dve.wait_ge(s_ec, h + 1)
                    dve.wait_ge(s_u, h + 1)
                    for i in range(NT - 1):
                        v.then(dve.scalar_tensor_tensor(
                            st[:, i + 1], st[:, i], ecum[:, i * P + P - 1:i * P + P],
                            ps[:, 4 + i // 4, (i % 4) * P:(i % 4 + 1) * P], ALU.mult, ALU.add))
                    dve.nop().then_inc(s_st, 1)
                    take_scores(0, h)
                    exponents(4, h)
                    factors(3, h)
                    v.did(dve.tensor_tensor(qe[:, :], ecum[:, :], one(xq[:, h % 2]), ALU.mult))
                    if more:
                        sigmoid_f(h + 1)
                    take_scores(1, h)
                    exponents(5, h)
                    factors(4, h)
                    if more:
                        gates(h + 1)
                    take_scores(2, h)
                    exponents(6, h)
                    factors(5, h)
                    output_gate(h)
                    take_scores(3, h)
                    factors(6, h)
                    if more:
                        running_sums(h + 1)
                    take_scores(4, h)
                    take_scores(5, h)
                    if more:
                        keys_to_end(h + 1)
                        first_buffers(h + 1)
                    take_scores(6, h)
                    output(h)
                    assert v.n == V_STEPS or not more, v.n

                dve.nop().then_inc(s_raw, 1)
                dve.nop().then_inc(s_raw, 1)
                dve.nop().then_inc(s_ge, 1)
                dve.nop().then_inc(s_ge, 1)
                sigmoid_f(0)
                gates(0)
                running_sums(0)
                keys_to_end(0)
                first_buffers(0)
                before_heads = v.n
                with dve.Fori(0, GH - 1) as h:
                    head(h, True)
                head(GH - 1, False)

            @block.tensor
            def _(pe):
                def unit(u, h, ahead):
                    out = ps[:, 6 + u % 2]
                    if u == 0:
                        pe.wait_ge(s_wt, h * 32 + 32 * ahead + 32)
                    if u == 4:
                        pe.wait_ge(s_wv, h * 32 + 32 * ahead + 32)
                    if ahead or u >= 2:
                        pe.wait_ge(s_pje, h * UNITS + (ahead * UNITS + u - 1))
                    for k in range(KD):
                        if u < 4:
                            last = pe.matmul(out, wt[:, k, u // 2], c["hT"][:, k, (u % 2) * HALF:(u % 2 + 1) * HALF],
                                             start=(k == 0), stop=(k == KD - 1))
                        else:
                            last = pe.matmul(out[:, 0:2 * DK], c["hT"][:, k, (u - 4) * P:(u - 3) * P],
                                             wv[:, k].rearrange("p a b -> p (a b)"),
                                             start=(k == 0), stop=(k == KD - 1))
                    last.then_inc(s_pj, 1)

                def gram(n, h):
                    if n == 0:
                        pe.wait_ge(s_kte, 2 * h + 2)
                        pe.wait_ge(s_ge, h * (LEVELS + 1) + 1)
                        pe.wait_ge(s_kc, h + 1)
                    else:
                        pe.wait_ge(s_l, h * LEVELS + n)
                        pe.wait_ge(s_ge, h * (LEVELS + 1) + n + 1)
                    for i in range(NT):
                        out = ps[:, GR[n % 2] + i // 4, (i % 4) * P:(i % 4 + 1) * P]
                        if n == 0:
                            last = pe.matmul(out, lev[:, LB - 1, i * P:(i + 1) * P], one(xq[:, h % 2])[:, i * P:(i + 1) * P],
                                             start=True, stop=True)
                        else:
                            s = lev[:, (n - 1) % LB, i * P:(i + 1) * P]
                            last = pe.matmul(out, s, s, start=True, stop=True)
                    last.then_inc(s_g, 1)

                def head(h, more):
                    def units(*us):
                        for u in us:
                            if more:
                                unit(u, h, 1)
                    v = one(xv[:, h % 2], 1)
                    pe.wait_ge(s_kend, h + 1)
                    pe.wait_ge(s_ge, h * (LEVELS + 1) + 1)
                    for b in range(2):
                        for i in range(4 * b, 4 * b + 4):
                            last = pe.transpose(ps[:, b, (i % 4) * P:(i % 4 + 1) * P], kend[:, i * P:(i + 1) * P],
                                                c["ident"][:, :])
                        last.then_inc(s_kt, 1)
                    units(0)
                    gram(0, h)
                    pe.wait_ge(s_oe, h + 1)
                    pe.wait_ge(s_e, (h + 1) * (UNITS - 2))
                    for i in range(NT):
                        last = pe.matmul(ps[:, 4 + i // 4, (i % 4) * P:(i % 4 + 1) * P], kx[:, i], v[:, i, 0:DK],
                                         start=True, stop=True)
                    last.then_inc(s_u, 1)
                    units(1)
                    for l in range(LEVELS):
                        gram(l + 1, h)
                        units(*UNIT_AFTER[l])
                    pe.wait_ge(s_st, h + 1)
                    for b in range(2):
                        pe.wait_ge(s_ge, (h + 1) * (LEVELS + 1) + 2)
                        for i in range(4 * b, 4 * b + 4):
                            out = ps[:, 4 + b, (i % 4) * P:(i % 4 + 1) * P]
                            pe.matmul(out, sc[:, i], v[:, i, 0:DK], start=True, stop=False)
                            last = pe.matmul(out, qe[:, i * P:(i + 1) * P], st[:, i], start=False, stop=True)
                        last.then_inc(s_o, 1)

                pe.nop().then_inc(s_oe, 1)
                for u in range(UNITS):
                    unit(u, 0, 0)
                with pe.Fori(0, GH - 1) as h:
                    head(h, True)
                head(GH - 1, False)


UNIT_AFTER = [(2,), (3,), (4, 5), (6, 7), (8, 9), (10, 11), ()]
COPY_AFTER = {2: (1,), 3: (2,), 4: (3,), 5: (4, 5), 6: (6, 7, 8, 9)}
LB = 4
V_STEPS = 62


def attention(nc, a, c, ps):
    with ExitStack() as m:
        def sb(name, shape, dt=F32):
            return m.enter_context(nc.sbuf_tensor(name, shape, dt))

        def sem(name):
            return m.enter_context(nc.semaphore(name))

        wq = sb("wq", [P, KD, 3, DH])
        raw = sb("raw", [P, 2, NT, 3 * DH])
        sqr = sb("sqr", [P, NT, 2 * DH])
        qk = sb("qk", [P, NT, 2, AUG])
        qT, kT = sb("qT", [AUG, SEQ]), sb("kT", [AUG, SEQ])
        p = sb("p", [P, 2, SEQ])
        pT = sb("pT", [P, 4, 4, P])
        o = sb("o", [P, NT, DH])
        osq = sb("osq", [P, NT, DH])
        nm, rsum = sb("nm", [P, NT]), sb("rsum", [P, NT])
        rin, oss = sb("rin", [P, NT]), sb("oss", [P, NT])
        ss = sb("ass", [P, NT, 2])
        gqk = sb("gqk", [P, 2, DH])
        gatt = sb("gatt", [P, AW])
        wada = sb("wada2", [P, KD, HALF])
        blank = sb("blank", [P, D])
        brow = sb("brow2", [1, HALF])

        s_k, s_w, s_ada_w = sem("a_k"), sem("a_w"), sem("a_adaw")
        s_pj, s_cp, s_pje, s_norm, s_qkt, s_qT, s_kT = (
            sem(f"a_{n}") for n in ("pj", "cp", "pje", "norm", "qkt", "qT", "kT"))
        s_s, s_nm, s_p, s_t, s_te0, s_te1, s_pv, s_o1 = (
            sem(f"a_{n}") for n in ("s", "nm", "p", "t", "te0", "te1", "pv", "o1"))
        s_ada, s_adae, s_v = sem("a_ada"), sem("a_adae"), sem("a_v")
        s_blank, s_bl = sem("a_blank"), sem("a_bl")
        s_ss, s_rt, s_oss, s_ort = sem("a_ss"), sem("a_rt"), sem("a_oss"), sem("a_ort")
        w_in = a["w_in"][0].rearrange("(k p) n -> p k n", p=P)
        w_ada = a["w_ada"][0].rearrange("(p k) n -> p k n", k=KD)
        mod = c["mod"][:, :, :].rearrange("p a (b n) -> p (a b) n", n=HALF)

        groups = [[(g, min(4, qi + 1 - 4 * g)) for g in range(qi // 4 + 1)] for qi in range(NT)]
        first = [sum(len(x) for x in groups[:qi]) for qi in range(NT)]
        NG = sum(len(x) for x in groups)
        tile_of = [qi for qi in range(NT) for _ in groups[qi]]
        assert NG % 4 == 0

        def scores(qi):
            return ps[:, 2 * (qi % 2):2 * (qi % 2) + 2].rearrange("p b n -> p (b n)")

        def copy_group(eng, copy, q, size, h, done):
            eng.wait_ge(s_t, h * NG + q + 2)
            eng.wait_ge(s_pv, h * NT + (tile_of[q - 4] + 1 if q >= 4 else 0) + 1)
            copy(pT[:, q % 4, 0:size].rearrange("p b q -> p (b q)"), ps[:, 4 + q % 2, 0:size * P]).then_inc(done, 1)

        with nc.Block() as block:
            @block.sync
            def _(sp):
                sp.dma_start(gqk[:, 0], a["q_norm_g"][0].partition_broadcast(P)).then_inc(s_k, 16)
                sp.dma_start(gqk[:, 1], a["k_norm_g"][0].partition_broadcast(P)).then_inc(s_k, 16)
                sp.dma_start(gatt[:, :], a["attn_out_g"][0].partition_broadcast(P)).then_inc(s_k, 16)

                def head_weights(h):
                    for n, col in enumerate((C_AQ, C_AK, C_AV)):
                        sp.dma_start(wq[:, :, n], w_in[:, :, ds(h * DH + col, DH)]).then_inc(s_w, 16)

                def ada_weights(h):
                    sp.dma_start(wada[:, :, :], w_ada[:, :, ds(h * HALF + 2 * D, HALF)]).then_inc(s_ada_w, 16)
                    sp.dma_start(brow[:, :], a["b_ada"][0:1, ds(h * HALF + 2 * D, HALF)]).then_inc(s_ada_w, 16)

                head_weights(0)
                ada_weights(0)
                with sp.Fori(1, AH) as h:
                    sp.wait_ge(s_pj, h * NT)
                    head_weights(h)
                    sp.wait_ge(s_ada, h)
                    ada_weights(h)

            @block.gpsimd
            def _(pool):
                pool.memset(blank[:, :], 0.0).then_inc(s_blank, 1)
                pool.wait_ge(s_blank, 1)
                with pool.Fori(MINT, MAXT) as t:
                    pool.dma_start(a["y_dram"][ds(t * P, P), :], blank[:, :]).then_inc(s_bl, 16)
                pool.wait_ge(s_bl, 16 * (MAXT - MINT))

            @block.scalar
            def _(act):
                def copy_out(i, h, par):
                    act.wait_ge(s_pj, h * NT + i + 1)
                    if i == 0 and not (isinstance(h, int) and h == 0):
                        act.wait_ge(s_pv, (h - 1) * NT + 1)
                        act.wait_ge(s_norm, h)
                    act.copy(raw[:, par, i], ps[:, 7, 0:3 * DH]).then_inc(s_cp, 1)
                    act.activation(sqr[:, i], ps[:, 7, 0:2 * DH], ACT.Square).then_inc(s_pje, 1)

                def head(h, more):
                    for b in range(2):
                        act.wait_ge(s_qkt, 2 * h + 1)
                        act.copy(qT[:, b * HALF:(b + 1) * HALF], ps[0:AUG, 4 + b]).then_inc(s_qT, 1)
                    for i in range(NT):
                        act.wait_ge(s_nm, h * NT + i + 1)
                        act.wait_ge(s_t, h * NG + (first[i - 1] if i >= 2 else 0) + 1)
                        act.activation(p[:, i % 2, 0:(i + 1) * P], scores(i)[:, 0:(i + 1) * P], ACT.Exp,
                                       bias=nm[:, i:i + 1], accum_out=rsum[:, i:i + 1]).then_inc(s_p, 1)
                        if more:
                            copy_out(i, h + 1, (h + 1) % 2)
                        for n, (g, size) in enumerate(groups[i]):
                            q = first[i] + n
                            if q % 2 == 0:
                                copy_group(act, act.copy, q, size, h, s_te0)
                    if more:
                        qk_root(h + 1)
                    act.wait_ge(s_oss, h + 1)
                    act.activation(oss[:, :], oss[:, :], ACT.Sqrt, scale=1.0 / DH, bias=c["eps"][:, :]).then_inc(s_ort, 1)

                def qk_root(h):
                    act.wait_ge(s_ss, h + 1)
                    act.activation(ss[:, :, :], ss[:, :, :], ACT.Sqrt, scale=1.0 / DH, bias=c["eps"][:, :]).then_inc(s_rt, 1)

                for i in range(NT):
                    copy_out(i, 0, 0)
                qk_root(0)
                with act.Fori(0, AH - 1) as h:
                    head(h, True)
                head(AH - 1, False)

            @block.vector
            def _(dve):
                v = Steps(dve, s_v)
                dve.wait_ge(s_k, 48)
                v.did(dve.memset(qk[:, :, 0, AUG - 1:AUG], 1.0))
                v.did(dve.memset(qk[:, :, 1, AUG - 2:AUG - 1], 1.0))
                v.then(dve.tensor_scalar(gqk[:, 0], gqk[:, 0], DH ** -0.5, None, ALU.mult))

                def norm(h):
                    dve.wait_ge(s_pje, h * NT + NT)
                    dve.wait_ge(s_cp, h * NT + NT)
                    r = raw[:, h % 2]
                    if len(r.shape) == 4:
                        r = r.rearrange("p a t n -> p (a t) n")
                    dve.tensor_reduce(ss[:, :, :], sqr[:, :, :].rearrange("p t (a d) -> p t a d", a=2), X,
                                      ALU.add).then_inc(s_ss, 1)
                    dve.wait_ge(s_rt, h + 1)
                    v.then(dve.reciprocal(ss[:, :, :], ss[:, :, :]))
                    v.then(dve.tensor_tensor(qk[:, :, :, 0:DH], r[:, :, 0:2 * DH].rearrange("p t (a d) -> p t a d", a=2),
                                             over(ss[:, :, :], 3, [P, NT, 2, DH]), ALU.mult))
                    v.did(dve.tensor_tensor(qk[:, :, :, 0:DH], qk[:, :, :, 0:DH],
                                            over(gqk[:, :, :], 1, [P, NT, 2, DH]), ALU.mult))
                    v.did(dve.tensor_copy(qk[:, :, 0, DH:DH + 1], c["cum"][:, :, ds(h, 1)]))
                    v.did(dve.tensor_copy(qk[:, :, 1, DH + 1:DH + 2], c["ncum"][:, :, ds(h, 1)]))
                    v.done()
                    dve.nop().then_inc(s_norm, 1)

                def odd_groups(i, h):
                    for n, (g, size) in enumerate(groups[i]):
                        q = first[i] + n
                        if q % 2:
                            copy_group(dve, dve.tensor_copy, q, size, h, s_te1)

                def head(h, more):
                    v.base, v.n = before_heads + h * A_STEPS, 0
                    for b in range(2):
                        dve.wait_ge(s_qkt, 2 * h + 2)
                        v.did(dve.tensor_copy(kT[:, b * HALF:(b + 1) * HALF], ps[0:AUG, b]))
                    v.done()
                    dve.nop().then_inc(s_kT, 1)
                    for i in range(NT):
                        dve.wait_ge(s_s, h * NT + i + 1)
                        d = scores(i)[:, i * P:(i + 1) * P]
                        v.then(dve.tensor_tensor(d, d, c["causal"][:, :], ALU.add))
                        dve.tensor_reduce(nm[:, i:i + 1], scores(i)[:, 0:(i + 1) * P], X, ALU.max,
                                          negate=True).then_inc(s_nm, 1)
                        if i:
                            odd_groups(i - 1, h)
                    odd_groups(NT - 1, h)
                    if more:
                        norm(h + 1)
                    dve.wait_ge(s_ada, h + 1)
                    dve.tensor_copy(mod[:, ds(h, 1)], ps[:, 7:8]).then_inc(s_adae, 1)
                    dve.wait_ge(s_p, h * NT + NT + 1)
                    v.then(dve.reciprocal(rin[:, :], rsum[:, :]))
                    dve.wait_ge(s_pv, h * NT + NT + 1)
                    v.then(dve.tensor_tensor(o[:, :, :], ps[:, 6].rearrange("p (t d) -> p t d", d=DH),
                                             over(rin[:, :], 2, [P, NT, DH]), ALU.mult))
                    dve.nop().then_inc(s_o1, 1)
                    v.then(dve.tensor_tensor(osq[:, :, :], o[:, :, :], o[:, :, :], ALU.mult))
                    dve.tensor_reduce(oss[:, :], osq[:, :, :], X, ALU.add).then_inc(s_oss, 1)
                    dve.wait_ge(s_ort, h + 1)
                    v.then(dve.reciprocal(oss[:, :], oss[:, :]))
                    v.then(dve.tensor_tensor(o[:, :, :], o[:, :, :], over(oss[:, :], 2, [P, NT, DH]), ALU.mult))
                    v.then(dve.tensor_tensor(c["ao"][:, :, ds(h * DH, DH)], o[:, :, :],
                                             over(gatt[:, ds(h * DH, DH)], 1, [P, NT, DH]), ALU.mult))
                    assert v.n == A_STEPS or not more, v.n

                norm(0)
                before_heads = v.n
                with dve.Fori(0, AH - 1) as h:
                    head(h, True)
                head(AH - 1, False)

            @block.tensor
            def _(pe):
                for s in (s_p, s_t, s_pv, s_o1):
                    pe.nop().then_inc(s, 1)

                def project(i, h):
                    if i == 0:
                        pe.wait_ge(s_w, 48 * h + 48)
                    if not (isinstance(h, int) and h == 0):
                        pe.wait_ge(s_cp, h * NT + i)
                        pe.wait_ge(s_pje, h * NT + i)
                        if i == 0 and not (isinstance(h, int) and h == 1):
                            pe.wait_ge(s_adae, h - 1)
                    elif i:
                        pe.wait_ge(s_cp, i)
                        pe.wait_ge(s_pje, i)
                    for k in range(KD):
                        last = pe.matmul(ps[:, 7, 0:3 * DH], c["hT"][:, k, i * P:(i + 1) * P],
                                         wq[:, k].rearrange("p a d -> p (a d)"), start=(k == 0), stop=(k == KD - 1))
                    last.then_inc(s_pj, 1)

                def score(i, h):
                    pe.wait_ge(s_p, h * NT + (i - 1 if i else 0) + 1)
                    for n0 in range(0, (i + 1) * P, HALF):
                        n1 = min(n0 + HALF, (i + 1) * P)
                        last = pe.matmul(scores(i)[:, n0:n1], qT[:, i * P:(i + 1) * P], kT[:, n0:n1],
                                         start=True, stop=True)
                    last.then_inc(s_s, 1)

                def turn(i, h):
                    pe.wait_ge(s_p, h * NT + i + 2)
                    for n, (g, size) in enumerate(groups[i]):
                        q = first[i] + n
                        if q >= 2:
                            pe.wait_ge((s_te0, s_te1)[q % 2], h * (NG // 2) + q // 2)
                        for b in range(size):
                            kb = 4 * g + b
                            last = pe.transpose(ps[:, 4 + q % 2, b * P:(b + 1) * P],
                                                p[:, i % 2, kb * P:(kb + 1) * P], c["ident"][:, :])
                        last.then_inc(s_t, 1)

                def values(i, h):
                    if i == 0:
                        pe.wait_ge(s_o1, h + 1)
                    v = raw[:, h % 2]
                    if len(v.shape) == 4:
                        v = v.rearrange("p a t n -> p (a t) n")
                    last_q = first[i] + len(groups[i]) - 1
                    pe.wait_ge(s_te0, h * (NG // 2) + last_q // 2 + 1)
                    if last_q:
                        pe.wait_ge(s_te1, h * (NG // 2) + (last_q + 1) // 2)
                    for kb in range(i + 1):
                        q = first[i] + kb // 4
                        last = pe.matmul(ps[:, 6, i * DH:(i + 1) * DH], pT[:, q % 4, kb % 4],
                                         v[:, kb, 2 * DH:3 * DH], start=(kb == 0), stop=(kb == i))
                    last.then_inc(s_pv, 1)

                def ada(h):
                    pe.wait_ge(s_ada_w, 32 * h + 32)
                    if not (isinstance(h, int) and h == AH - 1):
                        pe.wait_ge(s_cp, h * NT + 2 * NT)
                        pe.wait_ge(s_pje, h * NT + 2 * NT)
                    else:
                        pe.wait_ge(s_adae, h)
                    for k in range(KD):
                        pe.matmul(ps[:, 7], c["csil"][:, k], wada[:, k], start=(k == 0), stop=False)
                    pe.matmul(ps[:, 7], c["ones"][0:1, :], brow[0:1, :], start=False, stop=True).then_inc(s_ada, 1)

                def head(h, more):
                    pe.wait_ge(s_norm, h + 1)
                    pe.wait_ge(s_p, h * NT + 1)
                    if more is not None:
                        pe.wait_ge(s_pv, h * NT + 1)
                    for a_ in range(2):
                        for i in range(NT):
                            bank = (4 if a_ == 0 else 0) + i // 4
                            last = pe.transpose(ps[0:AUG, bank, (i % 4) * P:(i % 4 + 1) * P], qk[:, i, a_],
                                                c["ident"][:, :])
                        last.then_inc(s_qkt, 1)
                    pe.wait_ge(s_kT, h + 1)
                    pe.wait_ge(s_qT, 2 * h + 2)
                    score(0, h)
                    for i in range(NT):
                        if more:
                            project_next(i, h)
                        if i < NT - 1:
                            score(i + 1, h)
                        turn(i, h)
                        if i:
                            values(i - 1, h)
                    ada(h)
                    values(NT - 1, h)

                def project_next(i, h):
                    pe.wait_ge(s_w, 48 * h + 96)
                    pe.wait_ge(s_cp, h * NT + NT + i)
                    pe.wait_ge(s_pje, h * NT + NT + i)
                    if i == 0:
                        pe.wait_ge(s_adae, h + 1)
                    for k in range(KD):
                        last = pe.matmul(ps[:, 7, 0:3 * DH], c["hT"][:, k, i * P:(i + 1) * P],
                                         wq[:, k].rearrange("p a d -> p (a d)"), start=(k == 0), stop=(k == KD - 1))
                    last.then_inc(s_pj, 1)

                pe.nop().then_inc(s_adae, 1)
                for i in range(NT):
                    project(i, 0)
                with pe.Fori(0, AH - 1) as h:
                    head(h, True)
                head(AH - 1, False)


A_STEPS = 21


def project_out(nc, a, c, ps):
    with ExitStack() as m:
        def sb(name, shape, dt=F32):
            return m.enter_context(nc.sbuf_tensor(name, shape, dt))

        def sem(name):
            return m.enter_context(nc.semaphore(name))

        wo = sb("wo", [P, KD, D])
        cat, catT = sb("cat", [P, D]), sb("catT", [P, KD, P])
        xt, x1, sq, h2 = sb("oxt", [P, D]), sb("x1", [P, D]), sb("osqr", [P, D]), sb("h2", [P, D])
        h2T = sb("h2T", [P, KD, P])
        g2 = sb("g2", [P, D])
        wr = sb("wr", [P, KD, NR])
        ss, rs = sb("oss2", [P, 1]), sb("ors", [P, 1])
        s_wo, s_k, s_x, s_cat, s_ct, s_cte, s_mm = (sem(f"o_{n}") for n in ("wo", "k", "x", "cat", "ct", "cte", "mm"))
        s_x1, s_sq, s_h2, s_st, s_ht, s_hte, s_r, s_re, s_v, s_y, s_c0 = (
            sem(f"o_{n}") for n in ("x1", "sq", "h2", "st", "ht", "hte", "r", "re", "v", "y", "c0"))
        s_rt = sem("o_rt")
        x3 = a["x"].rearrange("b s d -> (b s) d")

        with nc.Block() as block:
            @block.sync
            def _(sp):
                sp.dma_start(wo[:, :, :], a["w_out"][0].rearrange("(k p) n -> p k n", p=P)).then_inc(s_wo, 16)
                sp.dma_start(wr[:, :, 0:G], a["w_router_group"][0].rearrange("(k p) n -> p k n", p=P)).then_inc(s_k, 16)
                sp.dma_start(wr[:, :, G:NR], a["w_router_expert"][0].rearrange("(k p) n -> p k n", p=P)).then_inc(s_k, 16)
                sp.dma_start(g2[:, :], a["norm2_g"][0].partition_broadcast(P)).then_inc(s_k, 16)
                sp.dma_start(c["brt"][:, 0:G], a["b_router_group"][0].partition_broadcast(P)).then_inc(s_k, 16)
                sp.dma_start(c["brt"][:, G:NR], a["b_router_expert"][0].partition_broadcast(P)).then_inc(s_k, 16)

                def stores(i):
                    sp.wait_ge(s_h2, i + 1)
                    sp.dma_start(a["x1_dram"][ds(i * P, P), :], x1[:, :]).then_inc(s_st, 16)
                    sp.dma_start(a["h2_dram"][ds(i * P, P), :], h2[:, :]).then_inc(s_st, 16)

                sp.dma_start(xt[:, :], x3[0:P, :]).then_inc(s_x, 16)
                with sp.Fori(1, NT) as i:
                    sp.wait_ge(s_x1, i)
                    sp.dma_start(xt[:, :], x3[ds(i * P, P), :]).then_inc(s_x, 16)
                    stores(i - 1)
                stores(NT - 1)
                sp.wait_ge(s_st, 32 * NT)

            @block.gpsimd
            def _(pool):
                def concat(i):
                    pool.tensor_copy(cat[:, 0:AW], c["ao"][:, i]).then_inc(s_cat, 1)
                    pool.tensor_copy(cat[:, AW:], c["ho"][:, i]).then_inc(s_cat, 1)
                concat(0)
                with pool.Fori(1, NT) as i:
                    pool.wait_ge(s_ct, 2 * i)
                    pool.tensor_copy(cat[:, 0:AW], flat(c["ao"][:, ds(i, 1)])).then_inc(s_cat, 1)
                    pool.tensor_copy(cat[:, AW:], flat(c["ho"][:, ds(i, 1)])).then_inc(s_cat, 1)

            @block.scalar
            def _(act):
                def cat_out(i):
                    for b in range(2):
                        act.wait_ge(s_ct, 2 * i + b + 1)
                        if not (isinstance(i, int) and i == 0):
                            act.wait_ge(s_mm, 2 * i)
                        act.copy(catT[:, 4 * b:4 * b + 4].rearrange("p k t -> p (k t)"), ps[:, b]).then_inc(s_cte, 1)

                def h_out(i):
                    for b in range(2):
                        act.wait_ge(s_ht, 2 * i + b + 1)
                        act.wait_ge(s_r, i + 1)
                        act.copy(h2T[:, 4 * b:4 * b + 4].rearrange("p k t -> p (k t)"), ps[:, 4 + b]).then_inc(s_hte, 1)

                def square(i):
                    act.wait_ge(s_x1, i + 1)
                    act.activation(sq[:, :], x1[:, :], ACT.Square, accum_out=ss[:, :]).then_inc(s_sq, 1)
                    act.wait_ge(s_sq, i + 1)
                    act.activation(rs[:, :], ss[:, :], ACT.Sqrt, scale=1.0 / D, bias=c["eps"][:, :]).then_inc(s_rt, 1)

                cat_out(0)
                cat_out(1)
                square(0)
                with act.Fori(1, NT - 1) as i:
                    cat_out(i + 1)
                    h_out(i - 1)
                    square(i)
                h_out(NT - 2)
                square(NT - 1)
                h_out(NT - 1)

            @block.vector
            def _(dve):
                v = Steps(dve, s_v)
                dve.wait_ge(s_k, 80)
                v.then(dve.scalar_tensor_tensor(g2[:, :], c["mod"][:, 2], 1.0, g2[:, :], ALU.add, ALU.mult))
                start = v.n

                def logits(i):
                    dve.wait_ge(s_r, i + 2)
                    dve.tensor_tensor(c["lg"][:, ds(i, 1)], ps[:, 6:7, 0:NR], c["brt"][:, :].unsqueeze(1),
                                      ALU.add).then_inc(s_re, 1)

                def tile(i, first):
                    v.base, v.n = start + 4 * i, 0
                    dve.wait_ge(s_x, 16 * i + 16)
                    if not first:
                        dve.wait_ge(s_st, 32 * i)
                    for b in range(2):
                        dve.wait_ge(s_mm, 2 * i + b + 1)
                        cols = slice(b * HALF, (b + 1) * HALF)
                        v.did(dve.tensor_tensor(x1[:, cols], ps[:, 2 + b], c["mod"][:, 0, cols], ALU.mult))
                    v.done()
                    dve.nop().then_inc(s_y, 1)
                    dve.tensor_tensor(x1[:, :], x1[:, :], xt[:, :], ALU.add).then_inc(s_x1, 1)
                    if not first:
                        logits(i - 1)
                    dve.wait_ge(s_rt, i + 1)
                    v.then(dve.reciprocal(rs[:, :], rs[:, :]))
                    if not first:
                        dve.wait_ge(s_ht, 2 * i)
                    v.then(dve.scalar_tensor_tensor(h2[:, :], x1[:, :], rs[:, :], g2[:, :], ALU.mult, ALU.mult))
                    dve.tensor_tensor(h2[:, :], h2[:, :], c["mod"][:, 1], ALU.add).then_inc(s_h2, 1)

                tile(0, True)
                with dve.Fori(1, NT) as i:
                    tile(i, False)
                logits(NT - 1)

            @block.tensor
            def _(pe):
                def turn_cat(i):
                    pe.wait_ge(s_cat, 2 * i + 2)
                    for b in range(2):
                        if not (isinstance(i, int) and i == 0):
                            pe.wait_ge(s_cte, 2 * i - 1 + b)
                        for k in range(4):
                            last = pe.transpose(ps[:, b, k * P:(k + 1) * P],
                                                cat[:, (4 * b + k) * P:(4 * b + k + 1) * P], c["ident"][:, :])
                        last.then_inc(s_ct, 1)

                def product(i):
                    pe.wait_ge(s_cte, 2 * i + 2)
                    if not (isinstance(i, int) and i == 0):
                        pe.wait_ge(s_y, i)
                    for b in range(2):
                        for k in range(KD):
                            last = pe.matmul(ps[:, 2 + b], catT[:, k], wo[:, k, b * HALF:(b + 1) * HALF],
                                             start=(k == 0), stop=(k == KD - 1))
                        last.then_inc(s_mm, 1)

                def route(i):
                    pe.wait_ge(s_h2, i + 1)
                    for b in range(2):
                        pe.wait_ge(s_hte, 2 * i + 1 + b)
                        for k in range(4):
                            last = pe.transpose(ps[:, 4 + b, k * P:(k + 1) * P],
                                                h2[:, (4 * b + k) * P:(4 * b + k + 1) * P], c["ident"][:, :])
                        last.then_inc(s_ht, 1)
                    pe.wait_ge(s_hte, 2 * i + 4)
                    pe.wait_ge(s_re, i + 1)
                    for k in range(KD):
                        last = pe.matmul(ps[:, 6, 0:NR], h2T[:, k], wr[:, k], start=(k == 0), stop=(k == KD - 1))
                    last.then_inc(s_r, 1)

                for s, n in ((s_hte, 2), (s_re, 1), (s_r, 1)):
                    for _ in range(n):
                        pe.nop().then_inc(s, 1)
                turn_cat(0)
                pe.wait_ge(s_wo, 16)
                pe.wait_ge(s_k, 80)
                product(0)
                turn_cat(1)
                with pe.Fori(1, NT - 1) as i:
                    product(i)
                    turn_cat(i + 1)
                    route(i - 1)
                product(NT - 1)
                route(NT - 2)
                route(NT - 1)


def flat(ap):
    return ap.rearrange("p a n -> p (a n)")


def experts(nc, a, c, ps):
    with ExitStack() as m:
        def sb(name, shape, dt=F32):
            return m.enter_context(nc.sbuf_tensor(name, shape, dt))

        def sem(name):
            return m.enter_context(nc.semaphore(name))

        slot = sb("slot", [P, 2, NT], I32)
        wts = sb("wts", [P, 2, NT])
        raw = [sb("raw_g", [P, KD, F]), sb("raw_u", [P, KD, F]), sb("raw_d", [P, KF, D])]
        high = [sb("high_g", [P, KD, F], F32R), sb("high_u", [P, KD, F], F32R), sb("high_d", [P, KF, D], F32R)]
        low = [sb("low_g", [P, KD, F], F32R), sb("low_u", [P, KD, F], F32R), sb("low_d", [P, KF, D], F32R)]
        tok = sb("tok", [P, TS], I32)
        rank = sb("rank", [P, TS], I32)
        fresh = sb("fresh", [P, TS], I32)
        expert = sb("expert", [P, TS], I32)
        end = sb("end", [P, 1], I32)
        n_exp = sb("n_exp", [P, 1], I32)
        s_raw = [sem(f"e_raw{n}") for n in "gud"]
        s_hi = [sem(f"e_hi{n}") for n in "gud"]
        s_lo = [sem(f"e_lo{n}") for n in "gud"]
        weights = [a[n][0].rearrange("e (k p) n -> e p k n", p=P) for n in ("w_gate", "w_up", "w_down")]
        CH = 4
        LEAD = 2 * CH

        def chunk(t, j):
            k = t.shape[1] // CH
            return t[:, j * k:(j + 1) * k].rearrange("p k n -> p (k n)")

        def load(sp, part, e):
            sp.dma_start(raw[part][:, :, :], weights[part][ds(e, 1)].rearrange("e p k n -> p (e k) n")
                         ).then_inc(s_raw[part], 16)

        def round_high(act, part, r):
            act.wait_ge(s_raw[part], r * 16 + 16)
            for j in range(CH):
                act.copy(chunk(high[part], j), chunk(raw[part], j)).then_inc(s_hi[part], 1)

        def take_low(dve, part, r):
            for j in range(CH):
                dve.wait_ge(s_hi[part], r * CH + j + 1)
                dve.tensor_tensor(chunk(low[part], j), chunk(raw[part], j), chunk(high[part], j).bitcast(F32),
                                  ALU.subtract).then_inc(s_lo[part], 1)

        with ExitStack() as r:
            def rb(name, shape, dt=F32):
                return r.enter_context(nc.sbuf_tensor(name, shape, dt))

            T4 = [P, NT, G]
            io4, io16, io32 = rb("io4", [P, G], I32), rb("io16", [P, NE], I32), rb("io32", [P, TS], I32)
            f4, f8, f32_ = rb("f4", [P, G]), rb("f8", [P, NT + 1]), rb("f32_", [P, TS])
            tokid = rb("tokid", [P, NT], I32)
            zero = rb("zero", [P, TS], I32)
            mx, sm, idx = rb("mx", [P, NT]), rb("sm", [P, NT]), rb("idx", [P, NT])
            t1, t2, w1 = rb("t1", [P, NT]), rb("t2", [P, NT]), rb("w1", [P, NT])
            d4, eq, ohg, oh1, oh2, ing = (rb(n, T4) for n in ("d4", "eq", "ohg", "oh1", "oh2", "ing"))
            prod = rb("prod", [P, NT, EG, G])
            o1, o2, mm, pm, rk = (rb(n, [P, NT, NE]) for n in ("o1", "o2", "mm_", "pm", "rk"))
            cnt, nt_, inc, exc = (rb(n, [P, NE]) for n in ("cnt", "nt_", "inc", "exc"))
            cmp8, cmpt = rb("cmp8", [P, NE, NT]), rb("cmpt", [P, TS, NE])
            posn, lane, div = rb("posn", [P, NT]), rb("lane", [P, NT], I32), rb("div", [P, NT], I32)
            where = rb("where", [P, 2, NT], I32)
            ef, enf = rb("ef", [P, TS]), rb("enf", [P, TS])
            has, prk, exq = (rb(n, [P, NE]) for n in ("has", "prk", "exq"))
            f16 = rb("f16", [P, NE])
            s_tables = r.enter_context(nc.semaphore("r_tables"))
            s_v, s_po, s_ex, s_exd, s_tot, s_cnt, s_z, s_slot, s_sc, s_tab, s_d4 = (
                r.enter_context(nc.semaphore(f"r_{n}")) for n in
                ("v", "po", "ex", "exd", "tot", "cnt", "z", "slot", "sc", "tab", "d4"))
            L = c["lg"]

            with nc.Block() as block:
                @block.sync
                def _(sp):
                    sp.wait_ge(s_po, 5)
                    sp.dma_start(a["tok_dram"].rearrange("(p t) o -> p (t o)", t=TS), zero[:, :]).then_inc(s_z, 16)
                    for s in s_lo:
                        sp.nop().then_inc(s, LEAD)
                    sp.wait_ge(s_tables, 1)
                    e0 = sp.value_load(expert[0:1, 0:1], min_val=0, max_val=NE - 1)
                    for part in range(3):
                        load(sp, part, e0)
                    sp.wait_ge(s_sc, 16 * 2 * NT)
                    sp.dma_start(tok[:, :], a["tok_dram"].rearrange("(p t) o -> p (t o)", t=TS)).then_inc(s_tab, 16)
                    sp.wait_ge(s_tab, 16)

                @block.gpsimd
                def _(pool):
                    pool.iota(io4[:, :], [[1, G]], base=0, channel_multiplier=0).then_inc(s_po, 1)
                    pool.iota(io16[:, 0:NT + 1], [[P, NT + 1]], base=0, channel_multiplier=0).then_inc(s_po, 1)
                    pool.iota(io32[:, :], [[1, TS]], base=0, channel_multiplier=0).then_inc(s_po, 1)
                    pool.iota(tokid[:, :], [[P, NT]], base=0, channel_multiplier=1).then_inc(s_po, 1)
                    pool.memset(zero[:, :], 0).then_inc(s_po, 1)
                    pool.wait_ge(s_po, 5)
                    pool.wait_ge(s_z, 16)
                    for n in range(2):
                        pool.wait_ge(s_slot, n + 1)
                        for i in range(NT):
                            pool.indirect_dma_start(a["tok_dram"], bass.IndirectOffsetOnAxis(where[:, n, i:i + 1], 0),
                                                    tokid[:, i:i + 1], None).then_inc(s_sc, 16)

                @block.scalar
                def _(act):
                    act.wait_ge(s_d4, 1)
                    act.activation(d4[:, :, :], d4[:, :, :], ACT.Exp).then_inc(s_ex, 1)
                    act.wait_ge(s_exd, 1)
                    act.activation(w1[:, :], w1[:, :], ACT.Exp).then_inc(s_ex, 1)
                    for part in range(3):
                        round_high(act, part, 0)

                @block.vector
                def _(dve):
                    v = Steps(dve, s_v)

                    def choose(onehot, values, top):
                        v.then(dve.tensor_reduce(top[:, :], values[:, :, :], X, ALU.max))
                        v.then(dve.tensor_tensor(eq[:, :, :], values[:, :, :], over(top[:, :], 2, T4), ALU.is_equal))
                        v.then(dve.tensor_scalar(eq[:, :, :], eq[:, :, :], -float(G), float(G), ALU.mult, ALU.add))
                        v.then(dve.tensor_tensor(eq[:, :, :], eq[:, :, :], over(f4[:, :], 1, T4), ALU.add))
                        v.then(dve.tensor_reduce(idx[:, :], eq[:, :, :], X, ALU.min))
                        v.then(dve.tensor_tensor(onehot[:, :, :], eq[:, :, :], over(idx[:, :], 2, T4), ALU.is_equal))

                    dve.wait_ge(s_po, 5)
                    v.did(dve.tensor_copy(f4[:, :], io4[:, :]))
                    v.did(dve.tensor_copy(f8[:, :], io16[:, 0:NT + 1]))
                    v.did(dve.tensor_copy(f32_[:, :], io32[:, :]))
                    v.done()
                    gl = L[:, :, 0:G]
                    choose(ohg, gl, mx)
                    v.did(dve.tensor_tensor(d4[:, :, :], gl, over(mx[:, :], 2, T4), ALU.subtract))
                    v.done()
                    dve.nop().then_inc(s_d4, 1)
                    v.then(dve.tensor_tensor(prod[:, :, :, :],
                                             L[:, :, G:NR].rearrange("p t (g e) -> p t e g", g=G),
                                             over(ohg[:, :, :], 2, [P, NT, EG, G]), ALU.mult))
                    v.then(dve.tensor_reduce(ing[:, :, :], prod[:, :, :, :], X, ALU.add))
                    choose(oh1, ing, t1)
                    v.then(dve.scalar_tensor_tensor(ing[:, :, :], oh1[:, :, :], -BIG, ing[:, :, :], ALU.mult, ALU.add))
                    choose(oh2, ing, t2)
                    v.then(dve.tensor_tensor(w1[:, :], t2[:, :], t1[:, :], ALU.subtract))
                    dve.nop().then_inc(s_exd, 1)
                    for o, oh in ((o1, oh1), (o2, oh2)):
                        v.did(dve.tensor_tensor(o[:, :, :].rearrange("p t (g e) -> p t g e", g=G),
                                                over(ohg[:, :, :], 3, [P, NT, G, EG]),
                                                over(oh[:, :, :], 2, [P, NT, G, EG]), ALU.mult))
                    v.did(dve.memset(pm[:, 0], 0.0))
                    v.done()
                    v.then(dve.tensor_tensor(mm[:, :, :], o1[:, :, :], o2[:, :, :], ALU.add))
                    for i in range(1, NT):
                        v.then(dve.tensor_tensor(pm[:, i], pm[:, i - 1], mm[:, i - 1], ALU.add))
                    v.then(dve.tensor_tensor(cnt[:, :], pm[:, NT - 1], mm[:, NT - 1], ALU.add))
                    dve.nop().then_inc(s_tot, 1)
                    dve.wait_ge(s_cnt, 1)
                    v.did(dve.tensor_copy(rk[:, :, :], ps[:, 0, 0:NT * NE].rearrange("p (t e) -> p t e", e=NE)))
                    v.then(dve.tensor_tensor(cmp8[:, :, :], over(ps[:, 1, 0:NE], 2, [P, NE, NT]),
                                             over(f8[:, 0:NT], 1, [P, NE, NT]), ALU.is_gt))
                    v.then(dve.tensor_reduce(nt_[:, :], cmp8[:, :, :], X, ALU.add))
                    v.did(dve.tensor_scalar(has[:, :], nt_[:, :], 0.0, None, ALU.is_gt))
                    v.then(dve.tensor_tensor_scan(inc[:, :], c["ones"][:, 0:NE], nt_[:, :], 0.0, ALU.mult, ALU.add))
                    v.did(dve.tensor_tensor_scan(prk[:, :], c["ones"][:, 0:NE], has[:, :], 0.0, ALU.mult, ALU.add))
                    v.then(dve.tensor_tensor(exc[:, :], inc[:, :], nt_[:, :], ALU.subtract))
                    v.did(dve.tensor_scalar(end[:, :], inc[:, NE - 1:NE], -1.0, None, ALU.add))
                    v.did(dve.tensor_copy(n_exp[:, :], prk[:, NE - 1:NE]))
                    v.then(dve.tensor_tensor(cmpt[:, :, :], over(prk[:, :], 1, [P, TS, NE]),
                                             over(f32_[:, :], 2, [P, TS, NE]), ALU.is_le))
                    v.then(dve.tensor_reduce(ef[:, :], cmpt[:, :, :], X, ALU.add))
                    v.then(dve.tensor_scalar(expert[:, :], ef[:, :], float(NE - 1), None, ALU.min))
                    dve.nop().then_inc(s_tables, 1)
                    v.then(dve.tensor_scalar(exq[:, :], has[:, :], -float(P), float(P), ALU.mult, ALU.add))
                    v.then(dve.tensor_tensor(exq[:, :], exq[:, :], exc[:, :], ALU.add))
                    v.then(dve.tensor_tensor(cmpt[:, :, :], over(exq[:, :], 1, [P, TS, NE]),
                                             over(f32_[:, :], 2, [P, TS, NE]), ALU.is_equal))
                    v.then(dve.tensor_reduce(ef[:, :], cmpt[:, :, :], X, ALU.add))
                    v.then(dve.memset(ef[:, 0:1], 0.0))
                    v.did(dve.tensor_copy(fresh[:, :], ef[:, :]))
                    v.then(dve.tensor_tensor_scan(enf[:, :], c["ones"][:, 0:TS], ef[:, :], 0.0, ALU.mult, ALU.add))
                    v.did(dve.tensor_copy(rank[:, :], enf[:, :]))
                    v.then(dve.tensor_scalar(exc[:, :], exc[:, :], float(P), None, ALU.mult))
                    v.then(dve.tensor_tensor(rk[:, :, :], rk[:, :, :], over(exc[:, :], 1, [P, NT, NE]), ALU.add))
                    for n, o in enumerate((o1, o2)):
                        v.then(dve.tensor_tensor(o[:, :, :], o[:, :, :], rk[:, :, :], ALU.mult))
                        v.then(dve.tensor_reduce(posn[:, :], o[:, :, :], X, ALU.add))
                        v.then(dve.tensor_copy(slot[:, n], posn[:, :]))
                        v.did(dve.tensor_scalar(lane[:, :], slot[:, n], P - 1, TS.bit_length() - 1, ALU.bitwise_and,
                                                ALU.logical_shift_left))
                        v.then(dve.tensor_scalar(div[:, :], slot[:, n], P.bit_length() - 1, None,
                                                 ALU.logical_shift_right))
                        v.then(dve.tensor_tensor(where[:, n], lane[:, :], div[:, :], ALU.bitwise_or))
                        dve.nop().then_inc(s_slot, 1)
                    dve.wait_ge(s_ex, 2)
                    v.then(dve.tensor_reduce(sm[:, :], d4[:, :, :], X, ALU.add))
                    v.then(dve.reciprocal(sm[:, :], sm[:, :]))
                    v.then(dve.tensor_scalar(t1[:, :], w1[:, :], 1.0, None, ALU.add))
                    v.then(dve.reciprocal(t1[:, :], t1[:, :]))
                    v.then(dve.tensor_tensor(wts[:, 0], t1[:, :], sm[:, :], ALU.mult))
                    v.then(dve.tensor_tensor(wts[:, 1], wts[:, 0], w1[:, :], ALU.mult))
                    for part in range(3):
                        take_low(dve, part, 0)

                @block.tensor
                def _(pe):
                    pe.wait_ge(s_tot, 1)
                    flat3 = "p t e -> p (t e)"
                    pe.matmul(ps[:, 0, 0:NT * NE], c["before"][:, :], mm[:, :, :].rearrange(flat3), start=True, stop=False)
                    pe.matmul(ps[:, 0, 0:NT * NE], c["ones"][:, :], pm[:, :, :].rearrange(flat3), start=False, stop=True)
                    pe.matmul(ps[:, 1, 0:NE], c["ones"][:, :], cnt[:, :], start=True, stop=True).then_inc(s_cnt, 1)

        with ExitStack() as t_:
            def tb(name, shape, dt=F32):
                return t_.enter_context(nc.sbuf_tensor(name, shape, dt))

            rows = tb("rows", [P, 1], I32)
            xg = tb("xg", [P, D])
            xh, xl = tb("xh", [P, KD, P], F32R), tb("xl", [P, KD, P], F32R)
            sil, act_ = tb("sil", [P, F]), tb("act_", [P, F])
            ah, al = tb("ah", [P, KF, P], F32R), tb("al", [P, KF, P], F32R)
            y = tb("y", [P, 2, D])
            (s_rows, s_gat, s_xt, s_xh, s_xl, s_gmm, s_umm, s_dmm, s_sil, s_act, s_at, s_ah, s_al, s_y0, s_y1, s_yst) = (
                t_.enter_context(nc.semaphore(f"t_{n}")) for n in
                ("rows", "gat", "xt", "xh", "xl", "gmm", "umm", "dmm", "sil", "act", "at", "ah", "al", "y0", "y1", "yst"))
            used = [s_gmm, s_umm, s_dmm]

            with nc.Block() as block:
                @block.sync
                def _(sp):
                    m_ = sp.value_load(n_exp[0:1, 0:1], min_val=2, max_val=NE)

                    def expert_of(r):
                        return sp.value_load(expert[0:1, ds(r, 1)], min_val=0, max_val=NE - 1)

                    def load_gate_up(r):
                        e = expert_of(r)
                        for part in range(2):
                            wait_alone(sp, s_lo[part], r * CH + LEAD)
                            load(sp, part, e)

                    def load_down(r):
                        wait_alone(sp, s_lo[2], r * CH + LEAD)
                        load(sp, 2, expert_of(r))

                    load_gate_up(1)
                    with sp.Fori(2, m_) as r:
                        load_gate_up(r)
                        load_down(r - 1)
                    load_down(m_ - 1)

                @block.gpsimd
                def _(pool):
                    def fetch(t):
                        pool.tensor_copy(rows[:, :], tok[:, ds(t, 1)]).then_inc(s_rows, 1)
                        wait_alone(pool, s_rows, t + 1)
                        pool.indirect_dma_start(xg[:, :], None, a["h2_dram"],
                                                bass.IndirectOffsetOnAxis(rows[:, :], 0)).then_inc(s_gat, 16)

                    end_t = pool.value_load(end[0:1, 0:1], min_val=1, max_val=MAXT - 1)
                    fetch(0)
                    with pool.Fori(1, end_t + 2) as t:
                        pool.wait_ge(s_xt, t)
                        fetch(t)

                @block.scalar
                def _(act):
                    end_t = act.value_load(end[0:1, 0:1], min_val=1, max_val=MAXT - 1)
                    for s in (s_y0, s_yst):
                        act.nop().then_inc(s, 1)

                    def table(t, tab, hi):
                        return act.value_load(tab[0:1, ds(t, 1)], min_val=0, max_val=hi)

                    def x_out(t):
                        act.wait_ge(s_xt, t + 1)
                        for b in range(2):
                            act.copy(xh[:, 4 * b:4 * b + 4].rearrange("p k t -> p (k t)"), ps[:, 4 + b]).then_inc(s_xh, 1)

                    def gate_out(t):
                        act.wait_ge(s_gmm, t * CH + CH)
                        act.activation(sil[:, :], ps[:, 0], ACT.Silu).then_inc(s_sil, 1)

                    def a_out(t):
                        act.wait_ge(s_at, t + 1)
                        act.copy(ah[:, :, :].rearrange("p k t -> p (k t)"), ps[:, 6]).then_inc(s_ah, 1)

                    def y_out(t):
                        act.wait_ge(s_dmm, t * CH + CH)
                        act.copy(y[:, t % 2, 0:HALF], ps[:, 2]).then_inc(s_y0, 1)

                    def store(t):
                        act.wait_ge(s_y0, t + 2)
                        act.wait_ge(s_y1, t + 2)
                        act.wait_ge(s_yst, t * 16 + 1)
                        act.dma_start(a["y_dram"][ds(t * P, P), :], y[:, t % 2]).then_inc(s_yst, 16)

                    def renew(part, t, to, new):
                        with act.If(new > 0):
                            r = table(to, rank, NE - 1)
                            wait_alone(act, used[part], t * CH + CH)
                            round_high(act, part, r)

                    def tile(t, first):
                        if not first:
                            act.wait_ge(s_act, t)
                        gate_out(t)
                        new = table(t + 1, fresh, 1)
                        renew(0, t, t + 1, new)
                        act.wait_ge(s_umm, t * CH + CH)
                        x_out(t + 1)
                        renew(1, t, t + 1, new)
                        if not first:
                            y_out(t - 1)
                        a_out(t)
                        if not first:
                            store(t - 1)
                            renew(2, t - 1, t, table(t, fresh, 1))

                    x_out(0)
                    tile(0, True)
                    with act.Fori(1, end_t + 1) as t:
                        tile(t, False)
                    y_out(end_t)
                    store(end_t)
                    wait_alone(act, s_yst, end_t * 16 + 17)

                @block.vector
                def _(dve):
                    end_t = dve.value_load(end[0:1, 0:1], min_val=1, max_val=MAXT - 1)
                    dve.nop().then_inc(s_y1, 1)

                    def table(t, tab, hi):
                        return dve.value_load(tab[0:1, ds(t, 1)], min_val=0, max_val=hi)

                    def gated(t):
                        dve.wait_ge(s_sil, t + 1)
                        dve.wait_ge(s_umm, t * CH + CH)
                        dve.tensor_tensor(act_[:, :], sil[:, :], ps[:, 1], ALU.mult).then_inc(s_act, 1)

                    def x_low(t):
                        for b in range(2):
                            dve.wait_ge(s_xh, 2 * t + b + 1)
                            x_ = slice(4 * b, 4 * b + 4)
                            dve.tensor_tensor(xl[:, x_].rearrange("p k t -> p (k t)"), ps[:, 4 + b],
                                              xh[:, x_].rearrange("p k t -> p (k t)").bitcast(F32),
                                              ALU.subtract).then_inc(s_xl, 1)

                    def a_low(t):
                        dve.wait_ge(s_ah, t + 1)
                        dve.tensor_tensor(al[:, :, :].rearrange("p k t -> p (k t)"), ps[:, 6],
                                          ah[:, :, :].rearrange("p k t -> p (k t)").bitcast(F32),
                                          ALU.subtract).then_inc(s_al, 1)

                    def y_out(t):
                        dve.wait_ge(s_dmm, t * CH + CH)
                        dve.wait_ge(s_yst, t * 16 + 1)
                        dve.tensor_copy(y[:, t % 2, HALF:], ps[:, 3]).then_inc(s_y1, 1)

                    def renew(part, to, new):
                        with dve.If(new > 0):
                            take_low(dve, part, table(to, rank, NE - 1))

                    def tile(t, first):
                        new = table(t + 1, fresh, 1)
                        renew(0, t + 1, new)
                        if not first:
                            dve.wait_ge(s_at, t)
                        gated(t)
                        x_low(t + 1)
                        renew(1, t + 1, new)
                        if not first:
                            y_out(t - 1)
                        a_low(t)
                        if not first:
                            renew(2, t, table(t, fresh, 1))

                    x_low(0)
                    tile(0, True)
                    with dve.Fori(1, end_t + 1) as t:
                        tile(t, False)
                    y_out(end_t)

                @block.tensor
                def _(pe):
                    end_t = pe.value_load(end[0:1, 0:1], min_val=1, max_val=MAXT - 1)

                    def product(out, xs, k, part, cols, first, last_):
                        (h_, l_), wh, wl = xs, high[part][:, k, cols], low[part][:, k, cols]
                        pe.matmul(out, h_[:, k], wh, start=first, stop=False)
                        pe.matmul(out, h_[:, k], wl, start=False, stop=False)
                        return pe.matmul(out, l_[:, k], wh, start=False, stop=last_)

                    def turn_x(t):
                        pe.wait_ge(s_gat, 16 * t + 16)
                        for k in range(KD):
                            last = pe.transpose(ps[:, 4 + k // 4, (k % 4) * P:(k % 4 + 1) * P],
                                                xg[:, k * P:(k + 1) * P], c["ident"][:, :])
                        last.then_inc(s_xt, 1)

                    def gate_up(t, r):
                        pe.wait_ge(s_xl, 2 * t + 2)
                        if not isinstance(t, int):
                            pe.wait_ge(s_act, t)
                        for part in range(2):
                            for k in range(KD):
                                if k % 2 == 0:
                                    pe.wait_ge(s_lo[part], r * CH + LEAD + k // 2 + 1)
                                last = product(ps[:, part], (xh, xl), k, part, slice(0, F), k == 0, k == KD - 1)
                                if k % 2:
                                    last.then_inc(used[part], 1)

                    def down(t, r):
                        pe.wait_ge(s_al, t + 1)
                        pe.wait_ge(s_y0, t + 1)
                        pe.wait_ge(s_y1, t + 1)
                        for k in range(KF):
                            pe.wait_ge(s_lo[2], r * CH + LEAD + k + 1)
                            for b in range(2):
                                last = product(ps[:, 2 + b], (ah, al), k, 2, slice(b * HALF, (b + 1) * HALF),
                                               k == 0, k == KF - 1)
                            last.then_inc(s_dmm, 1)

                    def turn_a(t):
                        pe.wait_ge(s_act, t + 1)
                        for k in range(KF):
                            last = pe.transpose(ps[:, 6, k * P:(k + 1) * P], act_[:, k * P:(k + 1) * P], c["ident"][:, :])
                        last.then_inc(s_at, 1)

                    def rank_of(t):
                        return pe.value_load(rank[0:1, ds(t, 1)], min_val=0, max_val=NE - 1)

                    turn_x(0)
                    gate_up(0, 0)
                    turn_x(1)
                    turn_a(0)
                    with pe.Fori(1, end_t + 1) as t:
                        gate_up(t, rank_of(t))
                        turn_x(t + 1)
                        down(t - 1, rank_of(t - 1))
                        turn_a(t)
                    down(end_t, rank_of(end_t))

        with ExitStack() as t_:
            def tb(name, shape, dt=F32):
                return t_.enter_context(nc.sbuf_tensor(name, shape, dt))

            y1, y2, xo, ro = (tb(n, [P, 2, D]) for n in ("cy1", "cy2", "cx", "cr"))
            s_y1, s_y1b, s_x, s_xb, s_v, s_out, s_done, s_ro = (
                t_.enter_context(nc.semaphore(f"c_{n}")) for n in ("y1", "y1b", "x", "xb", "v", "out", "done", "ro"))
            y_sem, x_sem = [s_y1, s_y1b], [s_x, s_xb]
            out = a["out"].rearrange("b s d -> (b s) d")
            with nc.Block() as block:
                @block.gpsimd
                def _(pool):
                    for i in range(NT):
                        if i >= 2:
                            pool.wait_ge(s_done, i - 1)
                        for n, yy in enumerate((y1, y2)):
                            pool.indirect_dma_start(yy[:, i % 2], None, a["y_dram"],
                                                    bass.IndirectOffsetOnAxis(slot[:, n, i:i + 1], 0)).then_inc(y_sem[i % 2], 16)

                @block.sync
                def _(sp):
                    for i in range(NT):
                        if i >= 2:
                            sp.wait_ge(s_ro, i - 1)
                        sp.dma_start(xo[:, i % 2], a["x1_dram"][i * P:(i + 1) * P, :]).then_inc(x_sem[i % 2], 16)

                @block.scalar
                def _(act):
                    for i in range(NT):
                        act.wait_ge(s_ro, i + 1)
                        act.dma_start(out[i * P:(i + 1) * P, :], ro[:, i % 2]).then_inc(s_out, 16)
                        act.wait_ge(s_out, 16 * i + 16)

                @block.vector
                def _(dve):
                    v = Steps(dve, s_v)
                    for i in range(NT):
                        j = i % 2
                        r_ = ro[:, j]
                        dve.wait_ge(y_sem[j], 32 * (i // 2 + 1))
                        if i >= 2:
                            dve.wait_ge(s_out, 16 * (i - 1))
                        v.then(dve.tensor_scalar(r_, y1[:, j], wts[:, 0, i:i + 1], None, ALU.mult))
                        dve.scalar_tensor_tensor(r_, y2[:, j], wts[:, 1, i:i + 1], r_, ALU.mult,
                                                 ALU.add).then_inc(s_done, 1)
                        dve.wait_ge(s_done, i + 1)
                        v.then(dve.tensor_tensor(r_, r_, c["mod"][:, 3], ALU.mult))
                        dve.wait_ge(x_sem[j], 16 * (i // 2 + 1))
                        dve.tensor_tensor(r_, r_, xo[:, j], ALU.add).then_inc(s_ro, 1)


_INS = ["x", "c", "w_ada", "b_ada", "norm1_g", "w_in", "b_fox", "q_norm_g", "k_norm_g", "attn_out_g",
        "hgrn_lb", "hgrn_out_g", "w_out", "norm2_g", "w_router_group", "b_router_group",
        "w_router_expert", "b_router_expert", "w_gate", "w_up", "w_down"]


def kernel(**inputs):
    import numpy as _np
    import concourse.bacc as _bacc
    from concourse import mybir as _mybir
    from concourse.bass_utils import run_bass_kernel_spmd as _run

    nc = _bacc.Bacc("TRN2", target_bir_lowering=False, num_devices=1)
    arrays, args = {}, {}
    for name in _INS:
        arr = _np.ascontiguousarray(inputs[name])
        arrays[f"in_{name}_dram"] = arr
        args[name] = nc.dram_tensor(f"in_{name}_dram", arr.shape, _mybir.dt.from_np(arr.dtype), kind="ExternalInput").ap()
    args["out"] = nc.dram_tensor("out_dram", (1, SEQ, D), _mybir.dt.float32, kind="ExternalOutput").ap()
    for name, shape, dt in (("x1_dram", (SEQ, D), F32), ("h2_dram", (SEQ, D), F32),
                            ("y_dram", (MAXT * P, D), F32), ("tok_dram", (P * TS, 1), I32)):
        args[name] = nc.dram_tensor(name, shape, dt, kind="Internal").ap()
    build(nc, args)
    r = _run(nc, [arrays], core_ids=[0])
    return r.results[0]["out_dram"]
```

```python
from contextlib import ExitStack

import concourse.bass as bass
from concourse import mybir

P = 128
D = 1024
KD = D // P
SEQ = 1024
NT = SEQ // P
HALF = 512
AH, DH = 8, 64
AW = AH * DH
AUG = DH + 2
GH, DK = 4, 128
GW = GH * DK
LEVELS = 7
G, EG = 4, 4
NE = G * EG
NR = G + NE
F = 512
KF = F // P
MINT = 2 * SEQ // P
MAXT = 2 * SEQ // P + NE - 1
TS = 32
EPS = 1e-6
BIG = 3.0e38
FAR = 1.0e30

C_AQ, C_AK, C_AV, C_AF = 0, AW, 2 * AW, 3 * AW
C_HQ = 3 * AW + AH
C_HF, C_HI, C_HG = C_HQ + GW, C_HQ + 2 * GW, C_HQ + 3 * GW

F32 = mybir.dt.float32
F32R = mybir.dt.float32r
I32 = mybir.dt.int32
ALU = mybir.AluOpType
ACT = mybir.ActivationFunctionType
X = mybir.AxisListType.X
ds = bass.ds


class Steps:

    def __init__(self, eng, sem):
        self.eng, self.sem, self.base, self.n = eng, sem, 0, 0

    def did(self, ins):
        ins.then_inc(self.sem, 1)
        self.n += 1

    def done(self):
        self.eng.wait_ge(self.sem, self.base + self.n)

    def then(self, ins):
        self.did(ins)
        self.done()

    def then_alone(self, ins):
        self.did(ins)
        wait_alone(self.eng, self.sem, self.base + self.n)


def wait_alone(eng, sem, value):
    eng.wait_ge(sem, value)
    eng.nop().then_inc(PASSED[0], 1)


PASSED = []


def one(ap, keep=0):
    if len(ap.shape) == 3 + keep:
        return ap.rearrange("p a c t -> p (a c) t" if keep else "p a t -> p (a t)")
    return ap


def over(ap, axis, shape):
    return ap.unsqueeze(axis).broadcast_to(shape)


def build(nc, a):
    with ExitStack() as kernel_memory:
        def keep(name, shape, dt=F32):
            return kernel_memory.enter_context(nc.sbuf_tensor(name, shape, dt))

        PASSED[:] = [kernel_memory.enter_context(nc.semaphore("passed"))]
        ps = kernel_memory.enter_context(nc.psum_tensor("ps", [P, 8, HALF], F32))
        c = {
            "ident": keep("ident", [P, P]),
            "ones": keep("ones", [P, P]),
            "upto": keep("upto", [P, P]),
            "before": keep("before", [P, P]),
            "causal": keep("causal", [P, P]),
            "scol": keep("scol", [P, KD]),
            "bfox": keep("bfox", [P, AH]),
            "z": keep("z", [P, NT, AH]),
            "cum": keep("cum", [P, NT, AH]),
            "ncum": keep("ncum", [P, NT, AH]),
            "eps": keep("eps", [P, 1]),
            "lg": keep("lg", [P, NT, NR]),
            "brt": keep("brt", [P, NR]),
            "mod": keep("mod", [P, 4, D]),
        }
        with ExitStack() as m:
            for n in ("ao", "ho"):
                c[n] = m.enter_context(nc.sbuf_tensor(n, [P, NT, AW], F32))
            with ExitStack() as mh:
                c["hT"] = mh.enter_context(nc.sbuf_tensor("hT", [P, KD, SEQ], F32))
                for n in ("s_wt", "s_wv", "s_wq", "s_wo", "s_apj", "s_acp"):
                    c[n] = kernel_memory.enter_context(nc.semaphore(n))
                c["wq"] = mh.enter_context(nc.sbuf_tensor("wq", [P, KD, 3, DH], F32))
                with ExitStack() as mw:
                    cols = mw.enter_context(nc.sbuf_tensor("cols", [P, KD * (4 * DK + AH)], F32))
                    c["wt"] = cols[:, 0:2 * KD * DK].rearrange("p (k a n) -> p k a n", k=KD, a=2)
                    c["wv"] = cols[:, 2 * KD * DK:].rearrange("p (k n) -> p k n", k=KD)
                    c["raw"] = cols[:, 0:2 * NT * 3 * DH].rearrange("p (a t n) -> p a t n", a=2, t=NT)
                    normalise(nc, a, c, ps)
                    hgrn(nc, a, c, ps)
                    attention(nc, a, c, ps)
                project_out(nc, a, c, ps)
        experts(nc, a, c, ps)


def load_head_t(sp, a, c, h):
    w_in = a["w_in"][0].rearrange("(k p) n -> p k n", p=P)
    sp.dma_start(c["wt"][:, :, 0], w_in[:, :, ds(h * DK + C_HF, DK)]).then_inc(c["s_wt"], 16)
    sp.dma_start(c["wt"][:, :, 1], w_in[:, :, ds(h * DK + C_HQ, DK)]).then_inc(c["s_wt"], 16)


def load_head_v(sp, a, c, h):
    w_in = a["w_in"][0].rearrange("(k p) n -> p k n", p=P)
    sp.dma_start(c["wv"][:, :, 0:DK], w_in[:, :, ds(h * DK + C_HI, DK)]).then_inc(c["s_wv"], 16)
    sp.dma_start(c["wv"][:, :, DK:2 * DK], w_in[:, :, ds(h * DK + C_HG, DK)]).then_inc(c["s_wv"], 16)


def load_attention_head(sp, a, c, h):
    w_in = a["w_in"][0].rearrange("(k p) n -> p k n", p=P)
    for n, col in enumerate((C_AQ, C_AK, C_AV)):
        sp.dma_start(c["wq"][:, :, n], w_in[:, :, ds(h * DH + col, DH)]).then_inc(c["s_wq"], 16)


def project(pe, c, ps, i, bank):
    for k in range(KD):
        last = pe.matmul(ps[:, bank, 0:3 * DH], c["hT"][:, k, i * P:(i + 1) * P],
                         c["wq"][:, k].rearrange("p a d -> p (a d)"), start=(k == 0), stop=(k == KD - 1))
    last.then_inc(c["s_apj"], 1)


def normalise(nc, a, c, ps):
    with ExitStack() as m:
        def sb(name, shape, dt=F32):
            return m.enter_context(nc.sbuf_tensor(name, shape, dt))

        def sem(name):
            return m.enter_context(nc.semaphore(name))

        ccol, cexp = sb("ccol", [P, KD]), sb("cexp", [P, KD])
        csil = sb("csil", [P, KD, P])
        wada = sb("wada1", [P, 3, KD, HALF])
        xt = sb("xt", [P, NT, D])
        sq = sb("sq", [P, D])
        h = sb("h", [P, 2, D])
        row = sb("row", [P, 2, HALF])
        ss, rs = sb("ss", [P, NT]), sb("rs", [P, NT])
        bg = sb("bg", [3 * KD, P])
        bgT = sb("bgT", [P, 3 * KD])
        col = sb("col", [P, 2 * KD])

        s_c, s_bg, s_const, s_csil, s_eps = (sem(f"n_{n}") for n in ("c", "bg", "const", "csil", "eps"))
        s_w, s_x = [sem(f"n_w{r}") for r in range(4)], [sem(f"n_x{i}") for i in range(NT // 2)]
        s_cexp, s_v, s_sq, s_rt, s_h, s_tr, s_ev0, s_ev1 = (
            sem(f"n_{n}") for n in ("cexp", "v", "sq", "rt", "h", "tr", "ev0", "ev1"))
        s_row, s_rc, s_rt4, s_bt, s_col, s_pool = (
            sem(f"n_{n}") for n in ("row", "rc", "rt4", "bt", "col", "pool"))
        pairs = a["x"][0].rearrange("(j t p) d -> j p t d", t=2, p=P)
        w_ada = a["w_ada"][0].rearrange("(p k) n -> p k n", k=KD)
        order = (0, 2, 1, 3)

        with nc.Block() as block:
            @block.sync
            def _(sp):
                sp.dma_start(ccol[:, :], a["c"][0].rearrange("(p k) -> p k", k=KD)).then_inc(s_c, 16)
                sp.dma_start(bg[0:2 * KD, :], a["b_ada"][0, 0:2 * D].rearrange("(k p) -> k p", p=P)).then_inc(s_bg, 16)
                sp.dma_start(bg[2 * KD:, :], a["norm1_g"][0].rearrange("(k p) -> k p", p=P)).then_inc(s_bg, 16)
                for n, r in enumerate(order):
                    sp.dma_start(xt[:, 2 * n:2 * n + 2], pairs[n]).then_inc(s_x[n], 16)
                    if n == 3:
                        sp.wait_ge(s_row, 1)
                    sp.dma_start(wada[:, n % 3], w_ada[:, :, r * HALF:(r + 1) * HALF]).then_inc(s_w[r], 16)
                load_head_t(sp, a, c, 0)
                load_head_v(sp, a, c, 0)

            @block.gpsimd
            def _(pool):
                v = Steps(pool, s_pool)
                v.did(pool.memset(c["ident"][:, :], 0.0))
                v.did(pool.memset(c["ones"][:, :], 1.0))
                pool.memset(c["eps"][:, :], EPS).then_inc(s_eps, 1)
                v.did(pool.memset(c["upto"][:, :], 1.0))
                v.did(pool.memset(c["before"][:, :], 1.0))
                v.then(pool.memset(c["causal"][:, :], 0.0))
                def keep_where(t, op, fill):
                    pool.affine_select(out=t[:, :], in_=t[:, :], compare_op=op, fill=fill, base=0,
                                       pattern=[[1, P]], channel_multiplier=-1).then_inc(s_const, 1)
                keep_where(c["ident"], ALU.not_equal, 1.0)
                keep_where(c["upto"], ALU.is_ge, 0.0)
                keep_where(c["before"], ALU.is_gt, 0.0)
                pool.affine_select(out=c["causal"][:, :], in_=c["causal"][:, :], compare_op=ALU.is_ge, fill=-FAR,
                                   base=0, pattern=[[-1, P]], channel_multiplier=1).then_inc(s_const, 1)

            @block.scalar
            def _(act):
                def h_out(i):
                    act.wait_ge(s_tr, 2 * i + 1)
                    act.copy(c["hT"][:, 0:4, i * P:(i + 1) * P],
                             ps[:, 4 + 2 * (i % 2)].rearrange("p (k t) -> p k t", t=P)).then_inc(s_ev0, 1)

                act.wait_ge(s_c, 16)
                act.activation(cexp[:, :], ccol[:, :], ACT.Exp, scale=-1.0).then_inc(s_cexp, 1)
                act.wait_ge(s_eps, 1)
                for i in range(NT):
                    act.wait_ge(s_x[i // 2], 16)
                    if i:
                        act.wait_ge(s_sq, i)
                    act.activation(sq[:, :], xt[:, i], ACT.Square, accum_out=ss[:, i:i + 1]).then_inc(s_sq, 1)
                    act.wait_ge(s_sq, i + 1)
                    act.activation(rs[:, i:i + 1], ss[:, i:i + 1], ACT.Sqrt, scale=1.0 / D,
                                   bias=c["eps"][:, :]).then_inc(s_rt, 1)
                    if i:
                        h_out(i - 1)
                h_out(NT - 1)
                act.wait_ge(s_ev0, NT)
                act.wait_ge(s_ev1, NT)
                for n in range(2):
                    act.wait_ge(s_col, n + 1)
                    for k in range(4 * n + 1, 4 * n + 4, 2):
                        act.activation(c["hT"][:, k], c["hT"][:, k], ACT.Identity, scale=col[:, KD + k:KD + k + 1],
                                       bias=col[:, k:k + 1])

            @block.vector
            def _(dve):
                v = Steps(dve, s_v)
                dve.wait_ge(s_cexp, 1)
                v.then(dve.tensor_scalar(cexp[:, :], cexp[:, :], 1.0, None, ALU.add))
                v.then(dve.reciprocal(cexp[:, :], cexp[:, :]))
                v.then(dve.tensor_tensor(c["scol"][:, :], cexp[:, :], ccol[:, :], ALU.mult))
                dve.tensor_copy(csil[:, :, :], over(c["scol"][:, :], 2, [P, KD, P])).then_inc(s_csil, 1)

                def h_out(i):
                    dve.wait_ge(s_tr, 2 * i + 2)
                    dve.tensor_copy(c["hT"][:, 4:8, i * P:(i + 1) * P],
                                    ps[:, 5 + 2 * (i % 2)].rearrange("p (k t) -> p k t", t=P)).then_inc(s_ev1, 1)

                def row_out(n):
                    dve.wait_ge(s_row, n + 1)
                    dve.tensor_copy(row[:, n % 2], ps[:, n % 2]).then_inc(s_rc, 1)

                for i in range(NT):
                    dve.wait_ge(s_rt, i + 1)
                    v.then(dve.reciprocal(rs[:, i:i + 1], rs[:, i:i + 1]))
                    if i >= 2:
                        dve.wait_ge(s_tr, 2 * i - 2)
                    dve.tensor_scalar(h[:, i % 2], xt[:, i], rs[:, i:i + 1], None, ALU.mult).then_inc(s_h, 1)
                    if i:
                        h_out(i - 1)
                    if i == ADA_AT[0]:
                        row_out(0)
                    if i == ADA_AT[1]:
                        row_out(1)
                h_out(NT - 1)
                dve.wait_ge(s_bt, 1)
                v.then(dve.tensor_copy(bgT[:, :], ps[:, 4, 0:3 * KD]))

                def columns(n):
                    dve.wait_ge(s_rt4, 2 * n + 2)
                    turned = ps[:, 2:4].rearrange("p b (k t) -> p b k t", t=P)
                    sh, sc = (slice(o + 4 * n, o + 4 * n + 4) for o in (0, KD))
                    v.did(dve.tensor_tensor(col[:, sh].unsqueeze(2), turned[:, 0, :, 0:1], bgT[:, sh].unsqueeze(2), ALU.add))
                    v.then(dve.tensor_tensor(col[:, sc].unsqueeze(2), turned[:, 1, :, 0:1], bgT[:, sc].unsqueeze(2), ALU.add))
                    v.then(dve.scalar_tensor_tensor(col[:, sc], col[:, sc], 1.0, bgT[:, 2 * KD + 4 * n:2 * KD + 4 * n + 4],
                                                    ALU.add, ALU.mult))
                    dve.nop().then_inc(s_col, 1)

                def modulate(n):
                    for k in range(4 * n, 4 * n + 4, 2):
                        v.did(dve.tensor_scalar(c["hT"][:, k], c["hT"][:, k], col[:, KD + k:KD + k + 1],
                                                col[:, k:k + 1], ALU.mult, ALU.add))

                dve.wait_ge(s_ev0, NT)
                dve.wait_ge(s_ev1, NT)
                columns(0)
                row_out(2)
                modulate(0)
                row_out(3)
                columns(1)
                modulate(1)

            @block.tensor
            def _(pe):
                def product(n):
                    r = order[n]
                    pe.wait_ge(s_w[r], 16)
                    if n >= 2:
                        pe.wait_ge(s_rc, n - 1)
                    for k in range(KD):
                        last = pe.matmul(ps[:, n % 2], csil[:, k], wada[:, n % 3, k], start=(k == 0), stop=(k == KD - 1))
                    last.then_inc(s_row, 1)

                def turn_row(n):
                    pe.wait_ge(s_rc, n + 1)
                    if n >= 2:
                        pe.wait_ge(s_col, 1)
                    for k in range(4):
                        last = pe.transpose(ps[:, 2 + n % 2, k * P:(k + 1) * P], row[:, n % 2, k * P:(k + 1) * P],
                                            c["ident"][:, :])
                    last.then_inc(s_rt4, 1)

                pe.wait_ge(s_const, 4)
                pe.wait_ge(s_csil, 1)
                for i in range(NT):
                    pe.wait_ge(s_h, i + 1)
                    for b in range(2):
                        if i >= 2:
                            pe.wait_ge((s_ev0, s_ev1)[b], i - 1)
                        for k in range(4):
                            last = pe.transpose(ps[:, 4 + 2 * (i % 2) + b, k * P:(k + 1) * P],
                                                h[:, i % 2, (4 * b + k) * P:(4 * b + k + 1) * P], c["ident"][:, :])
                        last.then_inc(s_tr, 1)
                    for n in range(2):
                        if i == ADA_AT[n]:
                            product(n)
                pe.wait_ge(s_ev0, NT - 1)
                pe.wait_ge(s_bg, 32)
                pe.transpose(ps[:, 4, 0:3 * KD], bg[:, :], c["ident"][0:3 * KD, 0:3 * KD]).then_inc(s_bt, 1)
                turn_row(0)
                turn_row(1)
                product(2)
                product(3)
                turn_row(2)
                turn_row(3)


ADA_AT = (3, 6)


def hgrn(nc, a, c, ps):
    with ExitStack() as m:
        def sb(name, shape, dt=F32):
            return m.enter_context(nc.sbuf_tensor(name, shape, dt))

        def sem(name):
            return m.enter_context(nc.semaphore(name))

        wt, wv = c["wt"], c["wv"]
        uf = sb("uf", [P, 2, SEQ])
        uq = sb("uq", [P, 2, SEQ])
        xq = sb("xq", [P, 2, SEQ])
        xv = sb("xv", [P, 2, NT, 2 * DK])
        ug = sb("ug", [P, 2, NT, DK])
        kend = sb("kend", [P, SEQ])
        qe = sb("qe", [P, SEQ])
        ecum = sb("ecum", [P, SEQ])
        lev = sb("lev", [P, LB, SEQ])
        sc = sb("sc", [P, NT, P])
        kx = sb("kx", [P, NT, P])
        st = sb("st", [P, NT, DK])
        masks = sb("masks", [P, LEVELS, P], I32)
        ti, si = sb("ti", [P, P], I32), sb("si", [P, P], I32)
        tf, ge = sb("tf", [P, P]), sb("ge", [P, LEVELS + 1, P])
        reset = sb("reset", [P, SEQ], mybir.dt.bfloat16)
        lbx, lbw, lb, oml = sb("lbx", [P, 2, GH]), sb("lbw", [P, 2, GH]), sb("lb", [P, GH]), sb("oml", [P, GH])
        gout = sb("gout", [P, GW])
        ss, rs = sb("hss", [P, NT]), sb("hrs", [P, NT])

        s_wt, s_wv, s_k = c["s_wt"], c["s_wv"], sem("h_k")
        s_pj, s_pje = sem("h_pj"), sem("h_pje")
        s_e = sem("h_e")
        s_v, s_a = sem("h_v"), sem("h_a")
        s_f, s_lf, s_dk, s_ek, s_ec = (sem(f"h_{n}") for n in ("f", "lf", "dk", "ek", "ec"))
        s_d, s_x, s_l = (sem(f"h_{n}") for n in ("d", "x", "l"))
        s_kend, s_kt, s_kte, s_u, s_st = (sem(f"h_{n}") for n in ("kend", "kt", "kte", "u", "st"))
        s_g, s_ge, s_o, s_os, s_oe, s_po = (sem(f"h_{n}") for n in ("g", "ge", "o", "os", "oe", "po"))
        s_kc = sem("h_kc")
        s_sub, s_raw, s_ss, s_rt = sem("h_sub"), sem("h_raw"), sem("h_ss"), sem("h_rt")
        w_in = a["w_in"][0].rearrange("(k p) n -> p k n", p=P)
        UNITS = 4 + NT
        GR = [0, 2]

        with nc.Block() as block:
            @block.sync
            def _(sp):
                sp.dma_start(lbx[:, :, :], a["hgrn_lb"].rearrange("l (h p) -> p l h", p=P),
                             allow_slow_non_contiguous=True).then_inc(s_k, 16)
                sp.dma_start(gout[:, :], a["hgrn_out_g"][0].partition_broadcast(P)).then_inc(s_k, 16)

                sp.dma_start(wv[:, :, 2 * DK:], w_in[:, :, C_AF:C_AF + AH]).then_inc(s_k, 16)
                sp.dma_start(c["bfox"][:, :], a["b_fox"][0].partition_broadcast(P)).then_inc(s_k, 16)
                load_attention_head(sp, a, c, 0)
                with sp.Fori(1, GH) as h:
                    sp.wait_ge(s_pj, h * UNITS - UNITS + 4)
                    load_head_t(sp, a, c, h)
                    sp.wait_ge(s_pj, h * UNITS)
                    load_head_v(sp, a, c, h)

            @block.gpsimd
            def _(pool):
                pool.iota(ti[:, :], [[1, P]], base=0, channel_multiplier=0).then_inc(s_po, 1)
                pool.iota(si[:, :], [[0, P]], base=0, channel_multiplier=1).then_inc(s_po, 1)
                pool.memset(reset[:, :], 1.0).then_inc(s_po, 1)
                pool.wait_ge(s_po, 3)
                pool.memset(reset[:, :].rearrange("p (c t) -> p c t", t=P)[:, :, 0:1], 0.0).then_inc(s_po, 1)

            @block.scalar
            def _(act):
                act.wait_ge(s_k, 64)
                act.wait_ge(s_sub, 1)
                act.activation(lbw[:, :, :], lbw[:, :, :], ACT.Exp).then_inc(s_a, 1)

                def copy_out(u, h, par):
                    act.wait_ge(s_pj, h * UNITS + u + 1)
                    bank = ps[:, 6 + u % 2]
                    if u == 0:
                        act.wait_ge(s_raw, h + 1)
                    if u < 2:
                        act.activation(uf[:, par, u * HALF:(u + 1) * HALF], bank, ACT.Exp,
                                       scale=-1.0).then_inc(s_pje, 1)
                    elif u < 4:
                        b = u - 2
                        act.copy(xq[:, par, b * HALF:(b + 1) * HALF], bank).then_inc(s_e, 1)
                        act.activation(uq[:, par, b * HALF:(b + 1) * HALF], bank, ACT.Exp,
                                       scale=-1.0).then_inc(s_pje, 1)
                    else:
                        act.copy(xv[:, par, u - 4], bank[:, 0:2 * DK]).then_inc(s_e, 1)
                        if isinstance(h, int):
                            act.copy(c["z"][:, u - 4], bank[:, 2 * DK:2 * DK + AH])
                        act.activation(ug[:, par, u - 4], bank[:, DK:2 * DK], ACT.Exp,
                                       scale=-1.0).then_inc(s_pje, 1)

                def factor(l, h):
                    act.wait_ge(s_d, h * LEVELS + l + 1)
                    act.activation(lev[:, l % LB], lev[:, l % LB], ACT.Exp).then_inc(s_x, 1)

                def log_f(h):
                    act.wait_ge(s_f, h + 1)
                    act.activation(kend[:, :], kend[:, :], ACT.Ln).then_inc(s_lf, 1)

                def decays(h):
                    act.wait_ge(s_dk, h + 1)
                    act.activation(kend[:, :], kend[:, :], ACT.Exp).then_inc(s_ek, 1)
                    act.activation(ecum[:, :], one(uf[:, h % 2]), ACT.Exp).then_inc(s_ec, 1)

                def head(h, more):
                    nxt = (h + 1) % 2

                    def units(*us):
                        for u in us:
                            if more:
                                copy_out(u, h + 1, nxt)
                            elif u < NT:
                                act.wait_ge(c["s_apj"], u + 1)
                                act.copy(c["raw"][:, 0, u], ps[:, 6 + u % 2, 0:3 * DH]).then_inc(c["s_acp"], 1)

                    for b in range(2):
                        act.wait_ge(s_kt, 2 * h + b + 1)
                        act.copy(kx[:, 4 * b:4 * b + 4], ps[:, b].rearrange("p (c t) -> p c t", t=P)).then_inc(s_kte, 1)
                    units(0)
                    for l in range(2, LEVELS):
                        factor(l, h)
                        units(*COPY_AFTER[l])
                        if l == 4 and more:
                            log_f(h + 1)
                    if more:
                        decays(h + 1)
                        units(10, 11)
                        factor(0, h + 1)
                        factor(1, h + 1)
                    for b in range(2):
                        act.wait_ge(s_o, 2 * h + b + 1)
                        act.activation(sc[:, 4 * b:4 * b + 4], ps[:, 4 + b].rearrange("p (c t) -> p c t", t=P),
                                       ACT.Square).then_inc(s_os, 1)
                    act.wait_ge(s_ss, h + 1)
                    act.activation(rs[:, :], ss[:, :], ACT.Sqrt, scale=1.0 / DK, bias=c["eps"][:, :]).then_inc(s_rt, 1)

                for u in range(UNITS):
                    copy_out(u, 0, 0)
                log_f(0)
                decays(0)
                factor(0, 0)
                factor(1, 0)
                with act.Fori(0, GH - 1) as h:
                    head(h, True)
                head(GH - 1, False)

            @block.vector
            def _(dve):
                dve.wait_ge(s_k, 64)
                v = Steps(dve, s_v)
                v.then(dve.tensor_tensor(lb[:, :], lbx[:, 0], lbx[:, 1], ALU.max))
                dve.tensor_tensor(lbw[:, :, :], lbx[:, :, :], over(lb[:, :], 1, [P, 2, GH]),
                                  ALU.subtract).then_inc(s_sub, 1)
                dve.wait_ge(s_a, 1)
                v.then(dve.tensor_tensor(oml[:, :], lbw[:, 0], lbw[:, 1], ALU.add))
                v.then(dve.reciprocal(oml[:, :], oml[:, :]))
                v.did(dve.tensor_tensor(lb[:, :], lbw[:, 0], oml[:, :], ALU.mult))
                v.then(dve.tensor_tensor(oml[:, :], lbw[:, 1], oml[:, :], ALU.mult))
                dve.wait_ge(s_po, 4)
                v.then(dve.tensor_tensor(ti[:, :], ti[:, :], si[:, :], ALU.bitwise_xor))
                v.then(dve.tensor_copy(tf[:, :], ti[:, :]))
                v.then(dve.tensor_tensor(tf[:, :], tf[:, :], c["before"][:, :], ALU.mult))
                for l in range(LEVELS + 1):
                    v.did(dve.tensor_scalar(ge[:, l], tf[:, :], float(1 << l), None, ALU.is_ge))
                v.done()
                v.did(dve.tensor_tensor(masks[:, :, :], ge[:, 0:LEVELS], ge[:, 1:], ALU.subtract))
                v.did(dve.memset(st[:, 0], 0.0))
                v.done()

                def sigmoid_f(h):
                    dve.wait_ge(s_pje, h * UNITS + 2)
                    u = one(uf[:, h % 2])
                    v.then_alone(dve.tensor_scalar(u, u, 1.0, None, ALU.add))
                    v.did(dve.reciprocal(u, u))

                def gates(h):
                    q, u, k = one(xq[:, h % 2]), one(uf[:, h % 2]), one(uq[:, h % 2])
                    dve.wait_ge(s_pje, h * UNITS + 4)
                    dve.wait_ge(s_e, h * (UNITS - 2) + 2)
                    v.then_alone(dve.tensor_scalar(k, k, 1.0, None, ALU.add))
                    v.then_alone(dve.reciprocal(k, k))
                    v.then(dve.tensor_tensor(q, q, k, ALU.mult))
                    v.then(dve.tensor_scalar(kend[:, :], u, oml[:, ds(h, 1)], lb[:, ds(h, 1)], ALU.mult, ALU.add))
                    v.then(dve.tensor_scalar(k, kend[:, :], -1.0, 1.0, ALU.mult, ALU.add))
                    dve.nop().then_inc(s_f, 1)

                def running_sums(h):
                    cum = one(uf[:, h % 2])
                    dve.wait_ge(s_lf, h + 1)
                    v.then(dve.tensor_tensor_scan(cum, reset[:, :], kend[:, :], 0.0, ALU.mult, ALU.add))
                    cc = cum.rearrange("p (c t) -> p c t", t=P)
                    ke = kend[:, :].rearrange("p (c t) -> p c t", t=P)
                    dve.tensor_tensor(ke, cc[:, :, P - 1:P].broadcast_to([P, NT, P]), cc,
                                      ALU.subtract).then_inc(s_dk, 1)

                def keys_to_end(h):
                    dve.wait_ge(s_ek, h + 1)
                    dve.tensor_tensor(kend[:, :], kend[:, :], one(uq[:, h % 2]), ALU.mult).then_inc(s_kend, 1)

                def exponents(l, h):
                    half = 1 << l
                    cb = one(uf[:, h % 2]).rearrange("p (b w) -> p b w", w=2 * half)
                    lv = lev[:, l % LB].rearrange("p (b w) -> p b w", w=2 * half)
                    mid = cb[:, :, half - 1:half].broadcast_to([P, SEQ // (2 * half), half])
                    v.did(dve.tensor_tensor(lv[:, :, half:], cb[:, :, half:], mid, ALU.subtract))
                    dve.tensor_tensor(lv[:, :, 0:half], mid, cb[:, :, 0:half], ALU.subtract).then_inc(s_d, 1)
                    v.done()

                def factors(l, h):
                    half = 1 << l
                    lv, qb, kb = (t.rearrange("p (b w) -> p b w", w=2 * half)
                                  for t in (lev[:, l % LB], one(xq[:, h % 2]), one(uq[:, h % 2])))
                    dve.wait_ge(s_x, h * LEVELS + l + 1)
                    v.did(dve.tensor_tensor(lv[:, :, half:], lv[:, :, half:], qb[:, :, half:], ALU.mult))
                    v.then(dve.tensor_tensor(lv[:, :, 0:half], lv[:, :, 0:half], kb[:, :, 0:half], ALU.mult))
                    dve.nop().then_inc(s_l, 1)

                def take_scores(l, h):
                    wait_alone(dve, s_g, h * (LEVELS + 1) + l + 2)
                    for b in range(2):
                        v.did(dve.copy_predicated(
                            sc[:, 4 * b:4 * b + 4], over(masks[:, l], 1, [P, 4, P]),
                            ps[:, GR[(l + 1) % 2] + b].rearrange("p (c t) -> p c t", t=P)))
                    v.done()
                    dve.nop().then_inc(s_ge, 1)

                def first_buffers(h):
                    exponents(0, h)
                    exponents(1, h)
                    v.then(dve.tensor_scalar(lev[:, LB - 1], one(uq[:, h % 2]), 1.0, None, ALU.mult))
                    dve.nop().then_inc(s_kc, 1)

                def output_gate(h):
                    g, hg = one(ug[:, h % 2], 1), one(xv[:, h % 2], 1)
                    dve.wait_ge(s_pje, h * UNITS + UNITS)
                    dve.wait_ge(s_e, (h + 1) * (UNITS - 2))
                    v.then_alone(dve.tensor_scalar(g, g, 1.0, None, ALU.add))
                    v.then_alone(dve.reciprocal(g, g))
                    v.then(dve.tensor_tensor(g, g, hg[:, :, DK:], ALU.mult))
                    v.then(dve.tensor_tensor(g, g, over(gout[:, ds(h * DK, DK)], 1, [P, NT, DK]), ALU.mult))

                def output(h):
                    g = one(ug[:, h % 2], 1)
                    dve.wait_ge(s_os, 2 * h + 2)
                    dve.tensor_reduce(ss[:, :], sc[:, :, :], X, ALU.add).then_inc(s_ss, 1)
                    dve.wait_ge(s_rt, h + 1)
                    v.then(dve.reciprocal(rs[:, :], rs[:, :]))
                    v.then(dve.tensor_tensor(g, g, over(rs[:, :], 2, [P, NT, DK]), ALU.mult))
                    for b in range(2):
                        v.did(dve.tensor_tensor(c["ho"][:, 4 * b:4 * b + 4, ds(h * DK, DK)],
                                                ps[:, 4 + b].rearrange("p (c t) -> p c t", t=P),
                                                g[:, 4 * b:4 * b + 4], ALU.mult))
                    v.done()
                    dve.nop().then_inc(s_oe, 1)
                    dve.nop().then_inc(s_raw, 1)

                def head(h, more):
                    v.base, v.n = before_heads + h * V_STEPS, 0
                    factors(0, h)
                    exponents(2, h)
                    factors(1, h)
                    wait_alone(dve, s_g, h * (LEVELS + 1) + 1)
                    for b in range(2):
                        v.did(dve.tensor_tensor(sc[:, 4 * b:4 * b + 4], ps[:, GR[0] + b].rearrange("p (c t) -> p c t", t=P),
                                                over(c["ident"][:, :], 1, [P, 4, P]), ALU.mult))
                    v.done()
                    dve.nop().then_inc(s_ge, 1)
                    exponents(3, h)
                    factors(2, h)
                    dve.wait_ge(s_ec, h + 1)
                    dve.wait_ge(s_u, h + 1)
                    for i in range(NT - 1):
                        v.then(dve.scalar_tensor_tensor(
                            st[:, i + 1], st[:, i], ecum[:, i * P + P - 1:i * P + P],
                            ps[:, 4 + i // 4, (i % 4) * P:(i % 4 + 1) * P], ALU.mult, ALU.add))
                    dve.nop().then_inc(s_st, 1)
                    take_scores(0, h)
                    exponents(4, h)
                    factors(3, h)
                    v.did(dve.tensor_tensor(qe[:, :], ecum[:, :], one(xq[:, h % 2]), ALU.mult))
                    if more:
                        sigmoid_f(h + 1)
                    take_scores(1, h)
                    exponents(5, h)
                    factors(4, h)
                    if more:
                        gates(h + 1)
                    take_scores(2, h)
                    exponents(6, h)
                    factors(5, h)
                    output_gate(h)
                    take_scores(3, h)
                    factors(6, h)
                    if more:
                        running_sums(h + 1)
                    take_scores(4, h)
                    take_scores(5, h)
                    if more:
                        keys_to_end(h + 1)
                        first_buffers(h + 1)
                    take_scores(6, h)
                    output(h)
                    assert v.n == V_STEPS or not more, v.n

                dve.nop().then_inc(s_raw, 1)
                dve.nop().then_inc(s_raw, 1)
                dve.nop().then_inc(s_ge, 1)
                dve.nop().then_inc(s_ge, 1)
                sigmoid_f(0)
                gates(0)
                running_sums(0)
                keys_to_end(0)
                first_buffers(0)
                before_heads = v.n
                with dve.Fori(0, GH - 1) as h:
                    head(h, True)
                head(GH - 1, False)

            @block.tensor
            def _(pe):
                def unit(u, h, ahead):
                    out = ps[:, 6 + u % 2]
                    if u == 0:
                        pe.wait_ge(s_wt, h * 32 + 32 * ahead + 32)
                    if u == 4:
                        pe.wait_ge(s_wv, h * 32 + 32 * ahead + 32)
                        if not ahead:
                            pe.wait_ge(s_k, 64)
                    width = 2 * DK if ahead else 2 * DK + AH
                    if ahead or u >= 2:
                        pe.wait_ge(s_pje, h * UNITS + (ahead * UNITS + u - 1))
                    for k in range(KD):
                        if u < 4:
                            last = pe.matmul(out, wt[:, k, u // 2], c["hT"][:, k, (u % 2) * HALF:(u % 2 + 1) * HALF],
                                             start=(k == 0), stop=(k == KD - 1))
                        else:
                            last = pe.matmul(out[:, 0:width], c["hT"][:, k, (u - 4) * P:(u - 3) * P], wv[:, k, 0:width],
                                             start=(k == 0), stop=(k == KD - 1))
                    last.then_inc(s_pj, 1)

                def gram(n, h):
                    if n == 0:
                        pe.wait_ge(s_kte, 2 * h + 2)
                        pe.wait_ge(s_ge, h * (LEVELS + 1) + 1)
                        pe.wait_ge(s_kc, h + 1)
                    else:
                        pe.wait_ge(s_l, h * LEVELS + n)
                        pe.wait_ge(s_ge, h * (LEVELS + 1) + n + 1)
                    for i in range(NT):
                        out = ps[:, GR[n % 2] + i // 4, (i % 4) * P:(i % 4 + 1) * P]
                        if n == 0:
                            last = pe.matmul(out, lev[:, LB - 1, i * P:(i + 1) * P], one(xq[:, h % 2])[:, i * P:(i + 1) * P],
                                             start=True, stop=True)
                        else:
                            s = lev[:, (n - 1) % LB, i * P:(i + 1) * P]
                            last = pe.matmul(out, s, s, start=True, stop=True)
                    last.then_inc(s_g, 1)

                def head(h, more):
                    def units(*us):
                        for u in us:
                            if more:
                                unit(u, h, 1)
                            elif u < NT:
                                if u == 0:
                                    pe.wait_ge(c["s_wq"], 48)
                                    pe.wait_ge(s_pje, GH * UNITS)
                                if u >= 2:
                                    pe.wait_ge(c["s_acp"], u - 1)
                                project(pe, c, ps, u, 6 + u % 2)
                    v = one(xv[:, h % 2], 1)
                    pe.wait_ge(s_kend, h + 1)
                    pe.wait_ge(s_ge, h * (LEVELS + 1) + 1)
                    for b in range(2):
                        for i in range(4 * b, 4 * b + 4):
                            last = pe.transpose(ps[:, b, (i % 4) * P:(i % 4 + 1) * P], kend[:, i * P:(i + 1) * P],
                                                c["ident"][:, :])
                        last.then_inc(s_kt, 1)
                    units(0)
                    gram(0, h)
                    pe.wait_ge(s_oe, h + 1)
                    pe.wait_ge(s_e, (h + 1) * (UNITS - 2))
                    for i in range(NT):
                        last = pe.matmul(ps[:, 4 + i // 4, (i % 4) * P:(i % 4 + 1) * P], kx[:, i], v[:, i, 0:DK],
                                         start=True, stop=True)
                    last.then_inc(s_u, 1)
                    units(1)
                    for l in range(LEVELS):
                        gram(l + 1, h)
                        units(*UNIT_AFTER[l])
                    pe.wait_ge(s_st, h + 1)
                    for b in range(2):
                        pe.wait_ge(s_ge, (h + 1) * (LEVELS + 1) + 2)
                        for i in range(4 * b, 4 * b + 4):
                            out = ps[:, 4 + b, (i % 4) * P:(i % 4 + 1) * P]
                            pe.matmul(out, sc[:, i], v[:, i, 0:DK], start=True, stop=False)
                            last = pe.matmul(out, qe[:, i * P:(i + 1) * P], st[:, i], start=False, stop=True)
                        last.then_inc(s_o, 1)

                pe.nop().then_inc(s_oe, 1)
                for u in range(UNITS):
                    unit(u, 0, 0)
                with pe.Fori(0, GH - 1) as h:
                    head(h, True)
                head(GH - 1, False)


UNIT_AFTER = [(2,), (3,), (4, 5), (6, 7), (8, 9), (10, 11), ()]
COPY_AFTER = {2: (1,), 3: (2,), 4: (3, 4), 5: (5, 6), 6: (7, 8, 9)}
LB = 4
V_STEPS = 62


def attention(nc, a, c, ps):
    with ExitStack() as m:
        def sb(name, shape, dt=F32):
            return m.enter_context(nc.sbuf_tensor(name, shape, dt))

        def sem(name):
            return m.enter_context(nc.semaphore(name))

        wq = c["wq"]
        raw = c["raw"]
        sqr = sb("sqr", [P, NT, 2 * DH])
        qk = sb("qk", [P, NT, 2, AUG])
        qT, kT = sb("qT", [AUG, SEQ]), sb("kT", [AUG, SEQ])
        p = sb("p", [P, 2, SEQ])
        pT = sb("pT", [P, 4, 4, P])
        o = sb("o", [P, NT, DH])
        osq = sb("osq", [P, NT, DH])
        nm, rsum = sb("nm", [P, NT]), sb("rsum", [P, NT])
        rin, oss = sb("rin", [P, NT]), sb("oss", [P, NT])
        ss = sb("ass", [P, NT, 2])
        gqk = sb("gqk", [P, 2, DH])
        gatt = sb("gatt", [P, AW])
        wada = sb("wada2", [P, KD, HALF])
        acc = sb("acc", [P, HALF])
        blank = sb("blank", [P, D])
        brow = sb("brow2", [1, HALF])

        s_k, s_w, s_ada_w = sem("a_k"), c["s_wq"], sem("a_adaw")
        s_pj, s_cp = c["s_apj"], c["s_acp"]
        s_pje, s_norm, s_kt, s_qt, s_qT, s_kT = (sem(f"a_{n}") for n in ("pje", "norm", "kt", "qt", "qT", "kT"))
        s_s, s_nm, s_p, s_t, s_te0, s_te1, s_pv, s_o1 = (
            sem(f"a_{n}") for n in ("s", "nm", "p", "t", "te0", "te1", "pv", "o1"))
        s_acc, s_ada, s_adae, s_v, s_pool = (sem(f"a_{n}") for n in ("acc", "ada", "adae", "v", "pool"))
        s_blank, s_bl = sem("a_blank"), sem("a_bl")
        s_ab, s_lf, s_cum, s_cs, s_sq0 = (sem(f"a_{n}") for n in ("ab", "lf", "cum", "cs", "sq0"))
        bfox, z = c["bfox"], c["z"]
        mn, ab, pre, lf = (sb(n, [P, NT, AH]) for n in ("mn", "ab", "pre", "lf"))
        s_rt, s_oss, s_ort = sem("a_rt"), sem("a_oss"), sem("a_ort")
        w_in = a["w_in"][0].rearrange("(k p) n -> p k n", p=P)
        w_ada = a["w_ada"][0].rearrange("(p k) n -> p k n", k=KD)
        mod = c["mod"][:, :, :].rearrange("p a (b n) -> p (a b) n", n=HALF)

        groups = [[(g, min(4, qi + 1 - 4 * g)) for g in range(qi // 4 + 1)] for qi in range(NT)]
        first = [sum(len(x) for x in groups[:qi]) for qi in range(NT)]
        NG = sum(len(x) for x in groups)
        tile_of = [qi for qi in range(NT) for _ in groups[qi]]
        assert NG % 4 == 0

        def scores(qi):
            return ps[:, 2 * (qi % 2):2 * (qi % 2) + 2].rearrange("p b n -> p (b n)")

        def copy_group(eng, copy, q, size, h, done):
            eng.wait_ge(s_t, h * NG + q + 2)
            eng.wait_ge(s_pv, h * NT + (tile_of[q - 4] + 1 if q >= 4 else 0) + 1)
            copy(pT[:, q % 4, 0:size].rearrange("p b q -> p (b q)"), ps[:, 4 + q % 2, 0:size * P]).then_inc(done, 1)

        with nc.Block() as block:
            @block.sync
            def _(sp):
                sp.dma_start(gqk[:, 0], a["q_norm_g"][0].partition_broadcast(P)).then_inc(s_k, 16)
                sp.dma_start(gqk[:, 1], a["k_norm_g"][0].partition_broadcast(P)).then_inc(s_k, 16)
                sp.dma_start(gatt[:, :], a["attn_out_g"][0].partition_broadcast(P)).then_inc(s_k, 16)

                def ada_weights(h):
                    sp.dma_start(wada[:, :, :], w_ada[:, :, ds(h * HALF + 2 * D, HALF)]).then_inc(s_ada_w, 16)
                    sp.dma_start(brow[:, :], a["b_ada"][0:1, ds(h * HALF + 2 * D, HALF)]).then_inc(s_ada_w, 16)

                sp.wait_ge(s_pj, NT)
                load_attention_head(sp, a, c, 1)
                ada_weights(0)
                sp.wait_ge(s_acc, 1)
                ada_weights(1)
                with sp.Fori(2, AH) as h:
                    sp.wait_ge(s_pj, h * NT)
                    load_attention_head(sp, a, c, h)
                    sp.wait_ge(s_acc, h)
                    ada_weights(h)
                sp.wait_ge(s_pj, AH * NT)
                sp.dma_start(c["hT"][:, :, :], a["w_out"][0].rearrange("(k p) n -> p k n", p=P)).then_inc(c["s_wo"], 16)

            @block.gpsimd
            def _(pool):
                pool.memset(blank[:, :], 0.0).then_inc(s_blank, 1)
                pool.wait_ge(s_blank, 1)
                with pool.Fori(MINT, MAXT) as t:
                    pool.dma_start(a["y_dram"][ds(t * P, P), :], blank[:, :]).then_inc(s_bl, 16)
                v = Steps(pool, s_pool)

                def half(h):
                    v.base, v.n = h * 5, 0
                    pool.wait_ge(s_ada_w, 32 * h + 32)
                    pool.wait_ge(s_ada, h + 1)
                    v.then(pool.tensor_tensor(wada[:, :, :], wada[:, :, :],
                                              over(c["scol"][:, :], 2, [P, KD, HALF]), ALU.mult))
                    v.then(pool.tensor_tensor(wada[:, 0:4], wada[:, 0:4], wada[:, 4:8], ALU.add))
                    v.then(pool.tensor_tensor(wada[:, 0:2], wada[:, 0:2], wada[:, 2:4], ALU.add))
                    v.then(pool.tensor_tensor(acc[:, :], wada[:, 0], wada[:, 1], ALU.add))
                    v.then(pool.tensor_tensor(acc[0:1, :], acc[0:1, :], brow[:, :], ALU.add))
                    pool.nop().then_inc(s_acc, 1)

                with pool.Fori(0, AH) as h:
                    half(h)
                pool.wait_ge(s_bl, 16 * (MAXT - MINT))

            @block.scalar
            def _(act):
                def copy_out(i, h, par):
                    act.wait_ge(s_pj, h * NT + i + 1)
                    if i == 0:
                        act.wait_ge(s_pv, (h - 1) * NT + 1)
                        act.wait_ge(s_norm, h)
                    act.copy(raw[:, par, i], ps[:, 7, 0:3 * DH]).then_inc(s_cp, 1)

                def square(i, h, par):
                    wait_alone(act, s_cp, h * NT + i + 1)
                    for n in range(2):
                        cols = slice(n * DH, (n + 1) * DH)
                        act.activation(sqr[:, i, cols], one(raw[:, par], 1)[:, i, cols], ACT.Square,
                                       accum_out=ss[:, i, n:n + 1]).then_inc(s_pje, 1)

                def q_out(b, h):
                    act.wait_ge(s_qt, 2 * h + b + 1)
                    act.copy(qT[:, b * HALF:(b + 1) * HALF], ps[0:AUG, (7, 0)[b]]).then_inc(s_qT, 1)

                def qk_root(h):
                    act.wait_ge(s_pje, h * 2 * NT + 2 * NT)
                    act.activation(ss[:, :, :], ss[:, :, :], ACT.Sqrt, scale=1.0 / DH, bias=c["eps"][:, :]).then_inc(s_rt, 1)

                def out_root(h):
                    act.wait_ge(s_oss, h + 1)
                    act.activation(oss[:, :], oss[:, :], ACT.Sqrt, scale=1.0 / DH, bias=c["eps"][:, :]).then_inc(s_ort, 1)

                def head(h, prev, more):
                    for i in range(NT):
                        act.wait_ge(s_nm, h * NT + i + 1)
                        act.wait_ge(s_t, h * NG + (first[i - 1] if i >= 2 else 0) + 1)
                        act.activation(p[:, i % 2, 0:(i + 1) * P], scores(i)[:, 0:(i + 1) * P], ACT.Exp,
                                       bias=nm[:, i:i + 1], accum_out=rsum[:, i:i + 1]).then_inc(s_p, 1)
                        if more:
                            for j in PROJECT[i][:1]:
                                copy_out(j, h + 1, (h + 1) % 2)
                            if i == NT - 1:
                                q_out(0, h + 1)
                        for n, (g, size) in enumerate(groups[i]):
                            q = first[i] + n
                            if q % 2 == 0:
                                copy_group(act, act.copy, q, size, h, s_te0)
                        if more:
                            for j in PROJECT[i][1:]:
                                copy_out(j, h + 1, (h + 1) % 2)
                            for j in PROJECT[i]:
                                square(j, h + 1, (h + 1) % 2)
                            if i == 5:
                                qk_root(h + 1)
                        if prev and i == 3:
                            out_root(h - 1)
                    if more:
                        q_out(1, h + 1)

                act.activation(sqr[:, :, :], raw[:, 0, :, 0:2 * DH], ACT.Square).then_inc(s_sq0, 1)
                act.wait_ge(s_ab, 1)
                act.activation(ab[:, :, :], ab[:, :, :], ACT.Exp, scale=-1.0).then_inc(s_lf, 1)
                act.wait_ge(s_lf, 1)
                act.activation(ab[:, :, :], ab[:, :, :], ACT.Ln, bias=1.0).then_inc(s_lf, 1)
                qk_root(0)
                for b in range(2):
                    q_out(b, 0)
                head(0, False, True)
                with act.Fori(1, AH - 1) as h:
                    head(h, True, True)
                head(AH - 1, True, False)
                out_root(AH - 1)

            @block.vector
            def _(dve):
                v = Steps(dve, s_v)
                def norm_a(h):
                    dve.wait_ge(s_cp, h * NT + NT)
                    r = raw[:, h % 2]
                    if len(r.shape) == 4:
                        r = r.rearrange("p a t n -> p (a t) n")
                    dve.wait_ge(s_rt, h + 1)
                    v.then(dve.reciprocal(ss[:, :, :], ss[:, :, :]))
                    v.did(dve.tensor_tensor(qk[:, :, :, 0:DH], r[:, :, 0:2 * DH].rearrange("p t (a d) -> p t a d", a=2),
                                            over(ss[:, :, :], 3, [P, NT, 2, DH]), ALU.mult))

                v.then(dve.tensor_tensor(z[:, :, :], z[:, :, :], over(bfox[:, :], 1, [P, NT, AH]), ALU.add))
                v.did(dve.tensor_scalar(mn[:, :, :], z[:, :, :], 0.0, None, ALU.min))
                dve.scalar_tensor_tensor(ab[:, :, :], z[:, :, :], -1.0, z[:, :, :], ALU.mult, ALU.max).then_inc(s_ab, 1)
                dve.wait_ge(s_sq0, 1)
                dve.tensor_reduce(ss[:, :, :], sqr[:, :, :].rearrange("p t (a d) -> p t a d", a=2), X,
                                  ALU.add).then_inc(s_pje, 2 * NT)
                dve.wait_ge(s_k, 48)
                v.then(dve.scalar_tensor_tensor(gqk[:, 1], gqk[:, 0], DH ** -0.5, gqk[:, 1], ALU.mult, ALU.mult))
                dve.wait_ge(s_lf, 2)
                v.done()
                v.did(dve.memset(pre[:, 0, :], 0.0))
                v.then(dve.tensor_tensor(lf[:, :, :], mn[:, :, :], ab[:, :, :], ALU.subtract))
                for i in range(1, NT):
                    v.then(dve.tensor_tensor(pre[:, i], pre[:, i - 1], lf[:, i - 1], ALU.add))
                dve.nop().then_inc(s_cum, 1)
                norm_a(0)
                dve.wait_ge(s_cs, 1)
                cm = ps[:, 5, 0:NT * AH].rearrange("p (t h) -> p t h", h=AH)
                v.did(dve.tensor_copy(c["cum"][:, :, :], cm))
                v.then(dve.tensor_scalar(c["ncum"][:, :, :], cm, -1.0, None, ALU.mult))
                v.did(dve.memset(qk[:, :, 0, AUG - 1:AUG], 1.0))
                v.did(dve.memset(qk[:, :, 1, AUG - 2:AUG - 1], 1.0))
                def norm_b(h):
                    v.did(dve.tensor_copy(qk[:, :, 0, DH:DH + 1], c["cum"][:, :, ds(h, 1)]))
                    v.did(dve.tensor_copy(qk[:, :, 1, DH + 1:DH + 2], c["ncum"][:, :, ds(h, 1)]))
                    v.done()
                    v.then(dve.tensor_tensor(qk[:, :, 1, 0:DH], qk[:, :, 1, 0:DH],
                                             over(gqk[:, 1], 1, [P, NT, DH]), ALU.mult))
                    dve.nop().then_inc(s_norm, 1)

                def k_out(h):
                    for b in range(2):
                        dve.wait_ge(s_kt, 2 * h + b + 1)
                        dve.tensor_copy(kT[:, b * HALF:(b + 1) * HALF], ps[0:AUG, b]).then_inc(s_kT, 1)

                def divide(h):
                    dve.wait_ge(s_pv, h * NT + NT + 1)
                    v.then(dve.tensor_tensor(o[:, :, :], ps[:, 6].rearrange("p (t d) -> p t d", d=DH),
                                             over(rin[:, :], 2, [P, NT, DH]), ALU.mult))
                    dve.nop().then_inc(s_o1, 1)

                def out_squares(h):
                    v.then(dve.tensor_tensor(osq[:, :, :], o[:, :, :], o[:, :, :], ALU.mult))

                def out_sums(h):
                    dve.tensor_reduce(oss[:, :], osq[:, :, :], X, ALU.add).then_inc(s_oss, 1)

                def out_norm(h):
                    dve.wait_ge(s_ort, h + 1)
                    v.then(dve.reciprocal(oss[:, :], oss[:, :]))
                    v.then(dve.tensor_tensor(o[:, :, :], o[:, :, :], over(oss[:, :], 2, [P, NT, DH]), ALU.mult))
                    v.did(dve.tensor_tensor(c["ao"][:, :, ds(h * DH, DH)], o[:, :, :],
                                            over(gatt[:, ds(h * DH, DH)], 1, [P, NT, DH]), ALU.mult))

                def odd_groups(i, h):
                    for n, (g, size) in enumerate(groups[i]):
                        q = first[i] + n
                        if q % 2:
                            copy_group(dve, dve.tensor_copy, q, size, h, s_te1)

                def head(h, prev, more):
                    for i in range(NT):
                        dve.wait_ge(s_s, h * NT + i + 1)
                        d = scores(i)[:, i * P:(i + 1) * P]
                        v.then(dve.tensor_tensor(d, d, c["causal"][:, :], ALU.add))
                        dve.tensor_reduce(nm[:, i:i + 1], scores(i)[:, 0:(i + 1) * P], X, ALU.max,
                                          negate=True).then_inc(s_nm, 1)
                        if i == 7:
                            dve.wait_ge(s_ada, h + 2)
                            dve.tensor_copy(mod[:, ds(h, 1)], ps[:, 7:8]).then_inc(s_adae, 1)
                        if i:
                            odd_groups(i - 1, h)
                        if prev:
                            for at, part in enumerate((divide, out_squares, out_sums, None, out_norm)):
                                if part and at == i:
                                    part(h - 1)
                        if more and i == 6:
                            norm_a(h + 1)
                            norm_b(h + 1)
                    if more:
                        k_out(h + 1)
                    odd_groups(NT - 1, h)
                    dve.wait_ge(s_p, h * NT + NT + 1)
                    v.then(dve.reciprocal(rin[:, :], rsum[:, :]))

                norm_b(0)
                k_out(0)
                head(0, False, True)
                before_heads = v.n
                with dve.Fori(1, AH - 1) as h:
                    v.base, v.n = before_heads - A_STEPS + h * A_STEPS, 0
                    head(h, True, True)
                    assert v.n == A_STEPS, v.n
                v.base, v.n = before_heads + (AH - 2) * A_STEPS, 0
                head(AH - 1, True, False)
                for part in (divide, out_squares, out_sums, out_norm):
                    part(AH - 1)

            @block.tensor
            def _(pe):
                for s in (s_p, s_t, s_pv, s_o1, s_ada):
                    pe.nop().then_inc(s, 1)

                def score(i, h):
                    pe.wait_ge(s_p, h * NT + (i - 1 if i else 0) + 1)
                    for n0 in range(0, (i + 1) * P, HALF):
                        n1 = min(n0 + HALF, (i + 1) * P)
                        last = pe.matmul(scores(i)[:, n0:n1], qT[:, i * P:(i + 1) * P], kT[:, n0:n1],
                                         start=True, stop=True)
                    last.then_inc(s_s, 1)

                def turn(i, h):
                    pe.wait_ge(s_p, h * NT + i + 2)
                    for n, (g, size) in enumerate(groups[i]):
                        q = first[i] + n
                        if q >= 2:
                            pe.wait_ge((s_te0, s_te1)[q % 2], h * (NG // 2) + q // 2)
                        for b in range(size):
                            kb = 4 * g + b
                            last = pe.transpose(ps[:, 4 + q % 2, b * P:(b + 1) * P],
                                                p[:, i % 2, kb * P:(kb + 1) * P], c["ident"][:, :])
                        last.then_inc(s_t, 1)

                def values(i, h):
                    if i == 0:
                        pe.wait_ge(s_o1, h + 1)
                    v = raw[:, h % 2]
                    if len(v.shape) == 4:
                        v = v.rearrange("p a t n -> p (a t) n")
                    last_q = first[i] + len(groups[i]) - 1
                    pe.wait_ge(s_te0, h * (NG // 2) + last_q // 2 + 1)
                    if last_q:
                        pe.wait_ge(s_te1, h * (NG // 2) + (last_q + 1) // 2)
                    for kb in range(i + 1):
                        q = first[i] + kb // 4
                        last = pe.matmul(ps[:, 6, i * DH:(i + 1) * DH], pT[:, q % 4, kb % 4],
                                         v[:, kb, 2 * DH:3 * DH], start=(kb == 0), stop=(kb == i))
                    last.then_inc(s_pv, 1)

                def ada(h):
                    pe.wait_ge(s_acc, h + 1)
                    pe.matmul(ps[:, 7], c["ones"][:, :], acc[:, :], start=True, stop=True).then_inc(s_ada, 1)

                def turn_k(h):
                    for b in range(2):
                        for i in range(4):
                            last = pe.transpose(ps[0:AUG, b, i * P:(i + 1) * P], qk[:, 4 * b + i, 1], c["ident"][:, :])
                        last.then_inc(s_kt, 1)

                def turn_q(b, h):
                    for i in range(4):
                        last = pe.transpose(ps[0:AUG, (7, 0)[b], i * P:(i + 1) * P], qk[:, 4 * b + i, 0], c["ident"][:, :])
                    last.then_inc(s_qt, 1)

                def project_next(i, h):
                    if i == 0:
                        pe.wait_ge(s_w, 48 * h + 96)
                    pe.wait_ge(s_cp, h * NT + NT + i)
                    project(pe, c, ps, i, 7)

                def head(h, more):
                    pe.wait_ge(s_kT, 2 * h + 2)
                    pe.wait_ge(s_qT, 2 * h + 2)
                    score(0, h)
                    for i in range(NT):
                        if i == 0:
                            score(1, h)
                        if more:
                            for j in PROJECT[i][:1]:
                                project_next(j, h)
                        if 0 < i < NT - 1:
                            score(i + 1, h)
                        if more and i == NT - 1:
                            pe.wait_ge(s_norm, h + 2)
                            pe.wait_ge(s_p, h * NT + i + 1)
                            turn_k(h + 1)
                            pe.wait_ge(s_adae, h + 1)
                            turn_q(0, h + 1)
                        turn(i, h)
                        if more:
                            for j in PROJECT[i][1:]:
                                project_next(j, h)
                            if i == NT - 1:
                                pe.wait_ge(s_kT, 2 * h + 3)
                                turn_q(1, h + 1)
                        if i:
                            values(i - 1, h)
                        if i == 6:
                            if more:
                                pe.wait_ge(s_cp, h * NT + 2 * NT)
                            ada(h)
                    values(NT - 1, h)

                pe.wait_ge(s_cum, 1)
                pe.matmul(ps[:, 5, 0:NT * AH], c["upto"][:, :], lf[:, :, :].rearrange("p t h -> p (t h)"),
                          start=True, stop=False)
                pe.matmul(ps[:, 5, 0:NT * AH], c["ones"][:, :], pre[:, :, :].rearrange("p t h -> p (t h)"),
                          start=False, stop=True).then_inc(s_cs, 1)
                pe.wait_ge(s_norm, 1)
                turn_k(0)
                turn_q(0, 0)
                pe.wait_ge(s_kT, 1)
                turn_q(1, 0)
                head(0, True)
                with pe.Fori(1, AH - 1) as h:
                    head(h, True)
                head(AH - 1, False)


PROJECT = [(0, 1), (2, 3), (4,), (5,), (6,), (7,), (), ()]
A_STEPS = 19


def project_out(nc, a, c, ps):
    with ExitStack() as m:
        def sb(name, shape, dt=F32):
            return m.enter_context(nc.sbuf_tensor(name, shape, dt))

        def sem(name):
            return m.enter_context(nc.semaphore(name))

        wo, s_wo = c["hT"], c["s_wo"]
        wo_high, wo_low = sb("wo_high", [P, KD, D], F32R), sb("wo_low", [P, KD, D], F32R)
        cat = sb("cat", [P, D])
        cat_high, cat_low = sb("cat_high", [P, KD, P], F32R), sb("cat_low", [P, KD, P], F32R)
        xt, x1, sq, h2 = sb("oxt", [P, D]), sb("x1", [P, D]), sb("osqr", [P, D]), sb("h2", [P, D])
        h2T = sb("h2T", [P, KD, P])
        g2 = sb("g2", [P, D])
        wr = sb("wr", [P, KD, NR])
        ss, rs = sb("oss2", [P, 1]), sb("ors", [P, 1])
        s_k, s_x, s_cat, s_ct, s_cte, s_mm = (sem(f"o_{n}") for n in ("k", "x", "cat", "ct", "cte", "mm"))
        s_x1, s_sq, s_h2, s_st, s_ht, s_hte, s_r, s_re, s_v, s_y = (
            sem(f"o_{n}") for n in ("x1", "sq", "h2", "st", "ht", "hte", "r", "re", "v", "y"))
        s_rt, s_wh, s_wl, s_ctl = (sem(f"o_{n}") for n in ("rt", "wh", "wl", "ctl"))
        x3 = a["x"].rearrange("b s d -> (b s) d")

        with nc.Block() as block:
            @block.sync
            def _(sp):
                sp.dma_start(wr[:, :, 0:G], a["w_router_group"][0].rearrange("(k p) n -> p k n", p=P)).then_inc(s_k, 16)
                sp.dma_start(wr[:, :, G:NR], a["w_router_expert"][0].rearrange("(k p) n -> p k n", p=P)).then_inc(s_k, 16)
                sp.dma_start(g2[:, :], a["norm2_g"][0].partition_broadcast(P)).then_inc(s_k, 16)
                sp.dma_start(c["brt"][:, 0:G], a["b_router_group"][0].partition_broadcast(P)).then_inc(s_k, 16)
                sp.dma_start(c["brt"][:, G:NR], a["b_router_expert"][0].partition_broadcast(P)).then_inc(s_k, 16)

                def stores(i):
                    sp.wait_ge(s_h2, i + 1)
                    sp.dma_start(a["x1_dram"][ds(i * P, P), :], x1[:, :]).then_inc(s_st, 16)
                    sp.dma_start(a["h2_dram"][ds(i * P, P), :], h2[:, :]).then_inc(s_st, 16)

                sp.dma_start(xt[:, :], x3[0:P, :]).then_inc(s_x, 16)
                with sp.Fori(1, NT) as i:
                    sp.wait_ge(s_x1, i)
                    sp.dma_start(xt[:, :], x3[ds(i * P, P), :]).then_inc(s_x, 16)
                    stores(i - 1)
                stores(NT - 1)
                sp.wait_ge(s_st, 32 * NT)

            @block.gpsimd
            def _(pool):
                def concat(i):
                    pool.tensor_copy(cat[:, 0:AW], c["ao"][:, i]).then_inc(s_cat, 1)
                    pool.tensor_copy(cat[:, AW:], c["ho"][:, i]).then_inc(s_cat, 1)
                concat(0)
                with pool.Fori(1, NT) as i:
                    pool.wait_ge(s_ct, 2 * i)
                    pool.tensor_copy(cat[:, 0:AW], flat(c["ao"][:, ds(i, 1)])).then_inc(s_cat, 1)
                    pool.tensor_copy(cat[:, AW:], flat(c["ho"][:, ds(i, 1)])).then_inc(s_cat, 1)

            @block.scalar
            def _(act):
                def cat_out(i):
                    for b in range(2):
                        act.wait_ge(s_ct, 2 * i + b + 1)
                        if not (isinstance(i, int) and i == 0):
                            act.wait_ge(s_mm, 2 * i)
                        act.copy(cat_high[:, 4 * b:4 * b + 4].rearrange("p k t -> p (k t)"), ps[:, b]).then_inc(s_cte, 1)

                def h_out(i):
                    for b in range(2):
                        act.wait_ge(s_ht, 2 * i + b + 1)
                        act.wait_ge(s_r, i + 1)
                        act.copy(h2T[:, 4 * b:4 * b + 4].rearrange("p k t -> p (k t)"), ps[:, 4 + b]).then_inc(s_hte, 1)

                def square(i):
                    act.wait_ge(s_x1, i + 1)
                    act.activation(sq[:, :], x1[:, :], ACT.Square, accum_out=ss[:, :]).then_inc(s_sq, 1)
                    act.wait_ge(s_sq, i + 1)
                    act.activation(rs[:, :], ss[:, :], ACT.Sqrt, scale=1.0 / D, bias=c["eps"][:, :]).then_inc(s_rt, 1)

                cat_out(0)
                act.wait_ge(s_wo, 16)
                for k in range(KD):
                    act.copy(wo_high[:, k], wo[:, k]).then_inc(s_wh, 1)
                cat_out(1)
                square(0)
                with act.Fori(1, NT - 1) as i:
                    cat_out(i + 1)
                    h_out(i - 1)
                    square(i)
                h_out(NT - 2)
                square(NT - 1)
                h_out(NT - 1)

            @block.vector
            def _(dve):
                v = Steps(dve, s_v)

                def cat_rest(i):
                    for b in range(2):
                        dve.wait_ge(s_cte, 2 * i + b + 1)
                        half = slice(4 * b, 4 * b + 4)
                        dve.tensor_tensor(cat_low[:, half].rearrange("p k t -> p (k t)"), ps[:, b],
                                          cat_high[:, half].rearrange("p k t -> p (k t)").bitcast(F32),
                                          ALU.subtract).then_inc(s_ctl, 1)

                def logits(i):
                    dve.wait_ge(s_r, i + 2)
                    dve.tensor_tensor(c["lg"][:, ds(i, 1)], ps[:, 6:7, 0:NR], c["brt"][:, :].unsqueeze(1),
                                      ALU.add).then_inc(s_re, 1)

                def tile(i, last=False):
                    first, second = (isinstance(i, int) and i == n for n in range(2))
                    v.base, v.n = start + 4 * i, 0
                    if not last:
                        cat_rest(i + 1)
                    dve.wait_ge(s_x, 16 * i + 16)
                    if not first:
                        dve.wait_ge(s_st, 32 * i)
                    for b in range(2):
                        dve.wait_ge(s_mm, 2 * i + b + 1)
                        cols = slice(b * HALF, (b + 1) * HALF)
                        v.did(dve.tensor_tensor(x1[:, cols], ps[:, 2 + b], c["mod"][:, 0, cols], ALU.mult))
                    v.done()
                    dve.nop().then_inc(s_y, 1)
                    dve.tensor_tensor(x1[:, :], x1[:, :], xt[:, :], ALU.add).then_inc(s_x1, 1)
                    if not (first or second):
                        logits(i - 2)
                    dve.wait_ge(s_rt, i + 1)
                    v.then(dve.reciprocal(rs[:, :], rs[:, :]))
                    if not first:
                        dve.wait_ge(s_ht, 2 * i)
                    v.then(dve.scalar_tensor_tensor(h2[:, :], x1[:, :], rs[:, :], g2[:, :], ALU.mult, ALU.mult))
                    dve.tensor_tensor(h2[:, :], h2[:, :], c["mod"][:, 1], ALU.add).then_inc(s_h2, 1)

                cat_rest(0)
                for k in range(KD):
                    dve.wait_ge(s_wh, k + 1)
                    dve.tensor_tensor(wo_low[:, k], wo[:, k], wo_high[:, k].bitcast(F32), ALU.subtract).then_inc(s_wl, 1)
                dve.wait_ge(s_k, 80)
                v.then(dve.scalar_tensor_tensor(g2[:, :], c["mod"][:, 2], 1.0, g2[:, :], ALU.add, ALU.mult))
                start = v.n
                tile(0)
                tile(1)
                with dve.Fori(2, NT - 1) as i:
                    tile(i)
                tile(NT - 1, True)
                logits(NT - 2)
                logits(NT - 1)

            @block.tensor
            def _(pe):
                def turn_cat(i):
                    pe.wait_ge(s_cat, 2 * i + 2)
                    for b in range(2):
                        if not (isinstance(i, int) and i == 0):
                            pe.wait_ge(s_ctl, 2 * i - 1 + b)
                        for k in range(4):
                            last = pe.transpose(ps[:, b, k * P:(k + 1) * P],
                                                cat[:, (4 * b + k) * P:(4 * b + k + 1) * P], c["ident"][:, :])
                        last.then_inc(s_ct, 1)

                def product(i):
                    pe.wait_ge(s_ctl, 2 * i + 2)
                    first = isinstance(i, int) and i == 0
                    if not first:
                        pe.wait_ge(s_y, i)
                    for k in range(KD):
                        if first:
                            pe.wait_ge(s_wl, k + 1)
                        for b in range(2):
                            cols = slice(b * HALF, (b + 1) * HALF)
                            pe.matmul(ps[:, 2 + b], cat_high[:, k], wo_high[:, k, cols], start=(k == 0), stop=False)
                            pe.matmul(ps[:, 2 + b], cat_high[:, k], wo_low[:, k, cols], start=False, stop=False)
                            last = pe.matmul(ps[:, 2 + b], cat_low[:, k], wo_high[:, k, cols], start=False,
                                             stop=(k == KD - 1))
                            if k == KD - 1:
                                last.then_inc(s_mm, 1)

                def turn_h(i):
                    pe.wait_ge(s_h2, i + 1)
                    for b in range(2):
                        pe.wait_ge(s_hte, 2 * i + 1 + b)
                        for k in range(4):
                            last = pe.transpose(ps[:, 4 + b, k * P:(k + 1) * P],
                                                h2[:, (4 * b + k) * P:(4 * b + k + 1) * P], c["ident"][:, :])
                        last.then_inc(s_ht, 1)

                def route(i):
                    pe.wait_ge(s_hte, 2 * i + 4)
                    pe.wait_ge(s_re, i + 1)
                    for k in range(KD):
                        last = pe.matmul(ps[:, 6, 0:NR], h2T[:, k], wr[:, k], start=(k == 0), stop=(k == KD - 1))
                    last.then_inc(s_r, 1)

                for s, n in ((s_hte, 2), (s_re, 1), (s_r, 1)):
                    for _ in range(n):
                        pe.nop().then_inc(s, 1)
                turn_cat(0)
                product(0)
                turn_cat(1)
                product(1)
                turn_cat(2)
                turn_h(0)
                pe.wait_ge(s_k, 80)
                with pe.Fori(2, NT - 1) as i:
                    product(i)
                    turn_cat(i + 1)
                    route(i - 2)
                    turn_h(i - 1)
                product(NT - 1)
                route(NT - 3)
                turn_h(NT - 2)
                route(NT - 2)
                turn_h(NT - 1)
                route(NT - 1)


def flat(ap):
    return ap.rearrange("p a n -> p (a n)")


def experts(nc, a, c, ps):
    with ExitStack() as m:
        def sb(name, shape, dt=F32):
            return m.enter_context(nc.sbuf_tensor(name, shape, dt))

        def sem(name):
            return m.enter_context(nc.semaphore(name))

        slot = sb("slot", [P, 2, NT], I32)
        wts = sb("wts", [P, 2, NT])
        raw = [sb("raw_g", [P, KD, F]), sb("raw_u", [P, KD, F]), sb("raw_d", [P, KF, D])]
        high = [sb("high_g", [P, KD, F], F32R), sb("high_u", [P, KD, F], F32R), sb("high_d", [P, KF, D], F32R)]
        low = [sb("low_g", [P, KD, F], F32R), sb("low_u", [P, KD, F], F32R), sb("low_d", [P, KF, D], F32R)]
        tok = sb("tok", [P, TS], I32)
        rank = sb("rank", [P, TS], I32)
        fresh = sb("fresh", [P, TS], I32)
        expert = sb("expert", [P, TS], I32)
        end = sb("end", [P, 1], I32)
        n_exp = sb("n_exp", [P, 1], I32)
        s_raw = [sem(f"e_raw{n}") for n in "gud"]
        s_hi = [sem(f"e_hi{n}") for n in "gud"]
        s_lo = [sem(f"e_lo{n}") for n in "gud"]
        weights = [a[n][0].rearrange("e (k p) n -> e p k n", p=P) for n in ("w_gate", "w_up", "w_down")]
        CH = 4
        LEAD = 2 * CH

        x1 = a["x1_dram"].rearrange("(j t p) d -> j p t d", t=NT // 2, p=P)

        def x1_half(part):
            return raw[part][:, :, :].rearrange("p k n -> p (k n)").rearrange("p (t d) -> p t d", d=D)

        def chunk(t, j):
            k = t.shape[1] // CH
            return t[:, j * k:(j + 1) * k].rearrange("p k n -> p (k n)")

        def load(sp, part, e):
            sp.dma_start(raw[part][:, :, :], weights[part][ds(e, 1)].rearrange("e p k n -> p (e k) n")
                         ).then_inc(s_raw[part], 16)

        def round_high(act, part, r):
            act.wait_ge(s_raw[part], r * 16 + 16)
            for j in range(CH):
                act.copy(chunk(high[part], j), chunk(raw[part], j)).then_inc(s_hi[part], 1)

        def take_low(dve, part, r):
            for j in range(CH):
                dve.wait_ge(s_hi[part], r * CH + j + 1)
                dve.tensor_tensor(chunk(low[part], j), chunk(raw[part], j), chunk(high[part], j).bitcast(F32),
                                  ALU.subtract).then_inc(s_lo[part], 1)

        with ExitStack() as r:
            def rb(name, shape, dt=F32):
                return r.enter_context(nc.sbuf_tensor(name, shape, dt))

            T4 = [P, NT, G]
            io4, io16, io32 = rb("io4", [P, G], I32), rb("io16", [P, NE], I32), rb("io32", [P, TS], I32)
            f4, f8, f32_ = rb("f4", [P, G]), rb("f8", [P, NT + 1]), rb("f32_", [P, TS])
            tokid = rb("tokid", [P, NT], I32)
            io128, f128 = rb("io128", [P, P], I32), rb("f128", [P, P])
            tokf = rb("tokf", [P, NT])
            lanef, tilef = rb("lanef", [P, 2, NT]), rb("tilef", [P, 2, NT])
            at_lane, at_tile = rb("at_lane", [P, 2, NT, P]), rb("at_tile", [P, 2, NT, TS])
            mx, sm, idx = rb("mx", [P, NT]), rb("sm", [P, NT]), rb("idx", [P, NT])
            t1, t2, w1 = rb("t1", [P, NT]), rb("t2", [P, NT]), rb("w1", [P, NT])
            d4, eq, ohg, oh1, oh2, ing = (rb(n, T4) for n in ("d4", "eq", "ohg", "oh1", "oh2", "ing"))
            prod = rb("prod", [P, NT, EG, G])
            o1, o2, mm, pm, rk = (rb(n, [P, NT, NE]) for n in ("o1", "o2", "mm_", "pm", "rk"))
            cnt, nt_, inc, exc = (rb(n, [P, NE]) for n in ("cnt", "nt_", "inc", "exc"))
            cmp8, cmpt = rb("cmp8", [P, NE, NT]), rb("cmpt", [P, TS, NE])
            posn, lane, div = rb("posn", [P, NT]), rb("lane", [P, NT], I32), rb("div", [P, NT], I32)
            ef, enf = rb("ef", [P, TS]), rb("enf", [P, TS])
            has, prk, exq = (rb(n, [P, NE]) for n in ("has", "prk", "exq"))
            s_tables = r.enter_context(nc.semaphore("r_tables"))
            s_v, s_po, s_ex, s_exd, s_tot, s_cnt, s_slot, s_tab, s_d4 = (
                r.enter_context(nc.semaphore(f"r_{n}")) for n in
                ("v", "po", "ex", "exd", "tot", "cnt", "slot", "tab", "d4"))
            L = c["lg"]

            with nc.Block() as block:
                @block.sync
                def _(sp):
                    for s in s_lo:
                        sp.nop().then_inc(s, LEAD)
                    sp.wait_ge(s_tables, 1)
                    e0 = sp.value_load(expert[0:1, 0:1], min_val=0, max_val=NE - 1)
                    for part in range(3):
                        load(sp, part, e0)

                @block.gpsimd
                def _(pool):
                    pool.iota(io4[:, :], [[1, G]], base=0, channel_multiplier=0).then_inc(s_po, 1)
                    pool.iota(io16[:, 0:NT + 1], [[P, NT + 1]], base=0, channel_multiplier=0).then_inc(s_po, 1)
                    pool.iota(io32[:, :], [[1, TS]], base=0, channel_multiplier=0).then_inc(s_po, 1)
                    pool.iota(tokid[:, :], [[P, NT]], base=0, channel_multiplier=1).then_inc(s_po, 1)
                    pool.iota(io128[:, :], [[1, P]], base=0, channel_multiplier=0).then_inc(s_po, 1)

                @block.scalar
                def _(act):
                    act.wait_ge(s_d4, 1)
                    act.activation(d4[:, :, :], d4[:, :, :], ACT.Exp).then_inc(s_ex, 1)
                    act.wait_ge(s_exd, 1)
                    act.activation(w1[:, :], w1[:, :], ACT.Exp).then_inc(s_ex, 1)

                @block.vector
                def _(dve):
                    v = Steps(dve, s_v)

                    def choose(onehot, values, top):
                        v.then(dve.tensor_reduce(top[:, :], values[:, :, :], X, ALU.max))
                        v.then(dve.tensor_tensor(eq[:, :, :], values[:, :, :], over(top[:, :], 2, T4), ALU.is_equal))
                        v.then(dve.tensor_scalar(eq[:, :, :], eq[:, :, :], -float(G), float(G), ALU.mult, ALU.add))
                        v.then(dve.tensor_tensor(eq[:, :, :], eq[:, :, :], over(f4[:, :], 1, T4), ALU.add))
                        v.then(dve.tensor_reduce(idx[:, :], eq[:, :, :], X, ALU.min))
                        v.then(dve.tensor_tensor(onehot[:, :, :], eq[:, :, :], over(idx[:, :], 2, T4), ALU.is_equal))

                    dve.wait_ge(s_po, 5)
                    v.did(dve.tensor_copy(f4[:, :], io4[:, :]))
                    v.did(dve.tensor_copy(f8[:, :], io16[:, 0:NT + 1]))
                    v.did(dve.tensor_copy(f32_[:, :], io32[:, :]))
                    v.did(dve.tensor_copy(f128[:, :], io128[:, :]))
                    v.did(dve.tensor_copy(tokf[:, :], tokid[:, :]))
                    v.done()
                    gl = L[:, :, 0:G]
                    choose(ohg, gl, mx)
                    v.did(dve.tensor_tensor(d4[:, :, :], gl, over(mx[:, :], 2, T4), ALU.subtract))
                    v.done()
                    dve.nop().then_inc(s_d4, 1)
                    v.then(dve.tensor_tensor(prod[:, :, :, :],
                                             L[:, :, G:NR].rearrange("p t (g e) -> p t e g", g=G),
                                             over(ohg[:, :, :], 2, [P, NT, EG, G]), ALU.mult))
                    v.then(dve.tensor_reduce(ing[:, :, :], prod[:, :, :, :], X, ALU.add))
                    choose(oh1, ing, t1)
                    v.then(dve.scalar_tensor_tensor(ing[:, :, :], oh1[:, :, :], -BIG, ing[:, :, :], ALU.mult, ALU.add))
                    choose(oh2, ing, t2)
                    v.then(dve.tensor_tensor(w1[:, :], t2[:, :], t1[:, :], ALU.subtract))
                    dve.nop().then_inc(s_exd, 1)
                    for o, oh in ((o1, oh1), (o2, oh2)):
                        v.did(dve.tensor_tensor(o[:, :, :].rearrange("p t (g e) -> p t g e", g=G),
                                                over(ohg[:, :, :], 3, [P, NT, G, EG]),
                                                over(oh[:, :, :], 2, [P, NT, G, EG]), ALU.mult))
                    v.did(dve.memset(pm[:, 0], 0.0))
                    v.done()
                    v.then(dve.tensor_tensor(mm[:, :, :], o1[:, :, :], o2[:, :, :], ALU.add))
                    for i in range(1, NT):
                        v.then(dve.tensor_tensor(pm[:, i], pm[:, i - 1], mm[:, i - 1], ALU.add))
                    v.then(dve.tensor_tensor(cnt[:, :], pm[:, NT - 1], mm[:, NT - 1], ALU.add))
                    dve.nop().then_inc(s_tot, 1)
                    dve.wait_ge(s_cnt, 1)
                    v.did(dve.tensor_copy(rk[:, :, :], ps[:, 0, 0:NT * NE].rearrange("p (t e) -> p t e", e=NE)))
                    v.then(dve.tensor_tensor(cmp8[:, :, :], over(ps[:, 1, 0:NE], 2, [P, NE, NT]),
                                             over(f8[:, 0:NT], 1, [P, NE, NT]), ALU.is_gt))
                    v.then(dve.tensor_reduce(nt_[:, :], cmp8[:, :, :], X, ALU.add))
                    v.did(dve.tensor_scalar(has[:, :], nt_[:, :], 0.0, None, ALU.is_gt))
                    v.then(dve.tensor_tensor_scan(inc[:, :], c["ones"][:, 0:NE], nt_[:, :], 0.0, ALU.mult, ALU.add))
                    v.did(dve.tensor_tensor_scan(prk[:, :], c["ones"][:, 0:NE], has[:, :], 0.0, ALU.mult, ALU.add))
                    v.then(dve.tensor_tensor(exc[:, :], inc[:, :], nt_[:, :], ALU.subtract))
                    v.did(dve.tensor_scalar(end[:, :], inc[:, NE - 1:NE], -1.0, None, ALU.add))
                    v.did(dve.tensor_copy(n_exp[:, :], prk[:, NE - 1:NE]))
                    v.then(dve.tensor_tensor(cmpt[:, :, :], over(prk[:, :], 1, [P, TS, NE]),
                                             over(f32_[:, :], 2, [P, TS, NE]), ALU.is_le))
                    v.then(dve.tensor_reduce(ef[:, :], cmpt[:, :, :], X, ALU.add))
                    v.then(dve.tensor_scalar(expert[:, :], ef[:, :], float(NE - 1), None, ALU.min))
                    dve.nop().then_inc(s_tables, 1)
                    v.then(dve.tensor_scalar(exq[:, :], has[:, :], -float(P), float(P), ALU.mult, ALU.add))
                    v.then(dve.tensor_tensor(exq[:, :], exq[:, :], exc[:, :], ALU.add))
                    v.then(dve.tensor_tensor(cmpt[:, :, :], over(exq[:, :], 1, [P, TS, NE]),
                                             over(f32_[:, :], 2, [P, TS, NE]), ALU.is_equal))
                    v.then(dve.tensor_reduce(ef[:, :], cmpt[:, :, :], X, ALU.add))
                    v.then(dve.memset(ef[:, 0:1], 0.0))
                    v.did(dve.tensor_copy(fresh[:, :], ef[:, :]))
                    v.then(dve.tensor_tensor_scan(enf[:, :], c["ones"][:, 0:TS], ef[:, :], 0.0, ALU.mult, ALU.add))
                    v.did(dve.tensor_copy(rank[:, :], enf[:, :]))
                    v.then(dve.tensor_scalar(exc[:, :], exc[:, :], float(P), None, ALU.mult))
                    v.then(dve.tensor_tensor(rk[:, :, :], rk[:, :, :], over(exc[:, :], 1, [P, NT, NE]), ALU.add))
                    for n, o in enumerate((o1, o2)):
                        v.then(dve.tensor_tensor(o[:, :, :], o[:, :, :], rk[:, :, :], ALU.mult))
                        v.then(dve.tensor_reduce(posn[:, :], o[:, :, :], X, ALU.add))
                        v.then(dve.tensor_copy(slot[:, n], posn[:, :]))
                        v.did(dve.tensor_scalar(lane[:, :], slot[:, n], P - 1, None, ALU.bitwise_and))
                        v.then(dve.tensor_scalar(div[:, :], slot[:, n], P.bit_length() - 1, None,
                                                 ALU.logical_shift_right))
                        v.did(dve.tensor_copy(lanef[:, n], lane[:, :]))
                        v.then(dve.tensor_copy(tilef[:, n], div[:, :]))
                        v.did(dve.tensor_tensor(at_lane[:, n], over(f128[:, :], 1, [P, NT, P]),
                                                over(lanef[:, n], 2, [P, NT, P]), ALU.is_equal))
                        v.then(dve.tensor_tensor(at_tile[:, n], over(f32_[:, :], 1, [P, NT, TS]),
                                                 over(tilef[:, n], 2, [P, NT, TS]), ALU.is_equal))
                        v.then(dve.tensor_tensor(at_tile[:, n], at_tile[:, n], over(tokf[:, :], 2, [P, NT, TS]), ALU.mult))
                        dve.nop().then_inc(s_slot, 1)
                    dve.wait_ge(s_ex, 2)
                    v.then(dve.tensor_reduce(sm[:, :], d4[:, :, :], X, ALU.add))
                    v.then(dve.reciprocal(sm[:, :], sm[:, :]))
                    v.then(dve.tensor_scalar(t1[:, :], w1[:, :], 1.0, None, ALU.add))
                    v.then(dve.reciprocal(t1[:, :], t1[:, :]))
                    v.then(dve.tensor_tensor(wts[:, 0], t1[:, :], sm[:, :], ALU.mult))
                    v.then(dve.tensor_tensor(wts[:, 1], wts[:, 0], w1[:, :], ALU.mult))
                    dve.wait_ge(s_tab, 1)
                    dve.tensor_copy(tok[:, :], ps[:, 2, 0:TS])

                @block.tensor
                def _(pe):
                    pe.wait_ge(s_tot, 1)
                    flat3 = "p t e -> p (t e)"
                    pe.matmul(ps[:, 0, 0:NT * NE], c["before"][:, :], mm[:, :, :].rearrange(flat3), start=True, stop=False)
                    pe.matmul(ps[:, 0, 0:NT * NE], c["ones"][:, :], pm[:, :, :].rearrange(flat3), start=False, stop=True)
                    pe.matmul(ps[:, 1, 0:NE], c["ones"][:, :], cnt[:, :], start=True, stop=True).then_inc(s_cnt, 1)
                    for n in range(2):
                        pe.wait_ge(s_slot, n + 1)
                        for i in range(NT):
                            last = pe.matmul(ps[:, 2, 0:TS], at_lane[:, n, i], at_tile[:, n, i],
                                             start=(n == 0 and i == 0), stop=(n == 1 and i == NT - 1))
                    last.then_inc(s_tab, 1)

        with ExitStack() as t_:
            def tb(name, shape, dt=F32):
                return t_.enter_context(nc.sbuf_tensor(name, shape, dt))

            rows = tb("rows", [P, 1], I32)
            xg = tb("xg", [P, D])
            xh, xl = tb("xh", [P, KD, P], F32R), tb("xl", [P, KD, P], F32R)
            sil, act_ = tb("sil", [P, F]), tb("act_", [P, F])
            ah, al = tb("ah", [P, KF, P], F32R), tb("al", [P, KF, P], F32R)
            y = tb("y", [P, 2, D])
            (s_rows, s_gat, s_xt, s_xh, s_xl, s_gmm, s_umm, s_dmm, s_sil, s_act, s_at, s_ah, s_al, s_y, s_yst) = (
                t_.enter_context(nc.semaphore(f"t_{n}")) for n in
                ("rows", "gat", "xt", "xh", "xl", "gmm", "umm", "dmm", "sil", "act", "at", "ah", "al", "y", "yst"))
            used = [s_gmm, s_umm, s_dmm]

            with nc.Block() as block:
                @block.sync
                def _(sp):
                    m_ = sp.value_load(n_exp[0:1, 0:1], min_val=2, max_val=NE)

                    def expert_of(r):
                        return sp.value_load(expert[0:1, ds(r, 1)], min_val=0, max_val=NE - 1)

                    def load_gate_up(r):
                        e = expert_of(r)
                        for part in range(2):
                            wait_alone(sp, s_lo[part], r * CH + LEAD)
                            load(sp, part, e)

                    def load_down(r):
                        wait_alone(sp, s_lo[2], r * CH + LEAD)
                        load(sp, 2, expert_of(r))

                    load_gate_up(1)
                    with sp.Fori(2, m_) as r:
                        load_gate_up(r)
                        load_down(r - 1)
                    load_down(m_ - 1)
                    for part in range(2):
                        wait_alone(sp, s_lo[part], m_ * CH + LEAD)
                        sp.dma_start(x1_half(part), x1[part]).then_inc(s_raw[part], 16)

                @block.gpsimd
                def _(pool):
                    def fetch(t):
                        pool.tensor_copy(rows[:, :], tok[:, ds(t, 1)]).then_inc(s_rows, 1)
                        wait_alone(pool, s_rows, t + 1)
                        pool.indirect_dma_start(xg[:, :], None, a["h2_dram"],
                                                bass.IndirectOffsetOnAxis(rows[:, :], 0)).then_inc(s_gat, 16)

                    end_t = pool.value_load(end[0:1, 0:1], min_val=1, max_val=MAXT - 1)
                    fetch(0)
                    with pool.Fori(1, end_t + 2) as t:
                        pool.wait_ge(s_xt, t)
                        fetch(t)

                @block.scalar
                def _(act):
                    end_t = act.value_load(end[0:1, 0:1], min_val=1, max_val=MAXT - 1)
                    act.nop().then_inc(s_yst, 1)

                    def table(t, tab, hi):
                        return act.value_load(tab[0:1, ds(t, 1)], min_val=0, max_val=hi)

                    def x_out(t):
                        act.wait_ge(s_xt, t + 1)
                        for b in range(2):
                            act.copy(xh[:, 4 * b:4 * b + 4].rearrange("p k t -> p (k t)"), ps[:, 4 + b]).then_inc(s_xh, 1)

                    def gate_out(t):
                        act.wait_ge(s_gmm, t * CH + CH)
                        act.activation(sil[:, :], ps[:, 0], ACT.Silu).then_inc(s_sil, 1)

                    def a_out(t):
                        act.wait_ge(s_at, t + 1)
                        act.copy(ah[:, :, :].rearrange("p k t -> p (k t)"), ps[:, 6]).then_inc(s_ah, 1)

                    def store(t):
                        act.wait_ge(s_y, 2 * t + 3)
                        act.wait_ge(s_yst, t * 16 + 1)
                        act.dma_start(a["y_dram"][ds(t * P, P), :], y[:, t % 2]).then_inc(s_yst, 16)

                    def renew(part, t, to, new):
                        with act.If(new > 0):
                            r = table(to, rank, NE - 1)
                            wait_alone(act, used[part], t * CH + CH)
                            round_high(act, part, r)

                    def tile(t, first):
                        if not first:
                            act.wait_ge(s_act, t)
                        gate_out(t)
                        new = table(t + 1, fresh, 1)
                        renew(0, t, t + 1, new)
                        act.wait_ge(s_umm, t * CH + CH)
                        x_out(t + 1)
                        renew(1, t, t + 1, new)
                        a_out(t)
                        if not first:
                            store(t - 1)
                            renew(2, t - 1, t, table(t, fresh, 1))

                    round_high(act, 0, 0)
                    x_out(0)
                    round_high(act, 1, 0)
                    round_high(act, 2, 0)
                    tile(0, True)
                    with act.Fori(1, end_t + 1) as t:
                        tile(t, False)
                    store(end_t)
                    wait_alone(act, s_yst, end_t * 16 + 17)

                @block.vector
                def _(dve):
                    end_t = dve.value_load(end[0:1, 0:1], min_val=1, max_val=MAXT - 1)
                    dve.nop().then_inc(s_y, 1)

                    def table(t, tab, hi):
                        return dve.value_load(tab[0:1, ds(t, 1)], min_val=0, max_val=hi)

                    def gated(t):
                        dve.wait_ge(s_sil, t + 1)
                        dve.wait_ge(s_umm, t * CH + CH)
                        dve.tensor_tensor(act_[:, :], sil[:, :], ps[:, 1], ALU.mult).then_inc(s_act, 1)

                    def x_low(t):
                        for b in range(2):
                            dve.wait_ge(s_xh, 2 * t + b + 1)
                            x_ = slice(4 * b, 4 * b + 4)
                            dve.tensor_tensor(xl[:, x_].rearrange("p k t -> p (k t)"), ps[:, 4 + b],
                                              xh[:, x_].rearrange("p k t -> p (k t)").bitcast(F32),
                                              ALU.subtract).then_inc(s_xl, 1)

                    def a_low(t):
                        dve.wait_ge(s_ah, t + 1)
                        dve.tensor_tensor(al[:, :, :].rearrange("p k t -> p (k t)"), ps[:, 6],
                                          ah[:, :, :].rearrange("p k t -> p (k t)").bitcast(F32),
                                          ALU.subtract).then_inc(s_al, 1)

                    def y_out(t):
                        dve.wait_ge(s_dmm, t * CH + CH)
                        dve.wait_ge(s_yst, t * 16 + 1)
                        for b in range(2):
                            cols = slice(b * HALF, (b + 1) * HALF)
                            dve.tensor_tensor(one(y[:, t % 2])[:, cols], ps[:, 2 + b], c["mod"][:, 3, cols],
                                              ALU.mult).then_inc(s_y, 1)

                    def renew(part, to, new):
                        with dve.If(new > 0):
                            take_low(dve, part, table(to, rank, NE - 1))

                    def tile(t, first):
                        new = table(t + 1, fresh, 1)
                        renew(0, t + 1, new)
                        if not first:
                            dve.wait_ge(s_at, t)
                        gated(t)
                        x_low(t + 1)
                        renew(1, t + 1, new)
                        if not first:
                            y_out(t - 1)
                        a_low(t)
                        if not first:
                            renew(2, t, table(t, fresh, 1))

                    take_low(dve, 0, 0)
                    x_low(0)
                    take_low(dve, 1, 0)
                    take_low(dve, 2, 0)
                    tile(0, True)
                    with dve.Fori(1, end_t + 1) as t:
                        tile(t, False)
                    y_out(end_t)

                @block.tensor
                def _(pe):
                    end_t = pe.value_load(end[0:1, 0:1], min_val=1, max_val=MAXT - 1)

                    def product(out, xs, k, part, cols, first, last_):
                        (h_, l_), wh, wl = xs, high[part][:, k, cols], low[part][:, k, cols]
                        pe.matmul(out, h_[:, k], wh, start=first, stop=False)
                        pe.matmul(out, h_[:, k], wl, start=False, stop=False)
                        return pe.matmul(out, l_[:, k], wh, start=False, stop=last_)

                    def turn_x(t):
                        pe.wait_ge(s_gat, 16 * t + 16)
                        for k in range(KD):
                            last = pe.transpose(ps[:, 4 + k // 4, (k % 4) * P:(k % 4 + 1) * P],
                                                xg[:, k * P:(k + 1) * P], c["ident"][:, :])
                        last.then_inc(s_xt, 1)

                    def gate_up(t, r):
                        pe.wait_ge(s_xl, 2 * t + 2)
                        if not isinstance(t, int):
                            pe.wait_ge(s_act, t)
                        for part in range(2):
                            for k in range(KD):
                                if k % 2 == 0:
                                    pe.wait_ge(s_lo[part], r * CH + LEAD + k // 2 + 1)
                                last = product(ps[:, part], (xh, xl), k, part, slice(0, F), k == 0, k == KD - 1)
                                if k % 2:
                                    last.then_inc(used[part], 1)

                    def down(t, r):
                        pe.wait_ge(s_al, t + 1)
                        pe.wait_ge(s_y, 2 * t + 1)
                        for k in range(KF):
                            pe.wait_ge(s_lo[2], r * CH + LEAD + k + 1)
                            for b in range(2):
                                last = product(ps[:, 2 + b], (ah, al), k, 2, slice(b * HALF, (b + 1) * HALF),
                                               k == 0, k == KF - 1)
                            last.then_inc(s_dmm, 1)

                    def turn_a(t):
                        pe.wait_ge(s_act, t + 1)
                        for k in range(KF):
                            last = pe.transpose(ps[:, 6, k * P:(k + 1) * P], act_[:, k * P:(k + 1) * P], c["ident"][:, :])
                        last.then_inc(s_at, 1)

                    def rank_of(t):
                        return pe.value_load(rank[0:1, ds(t, 1)], min_val=0, max_val=NE - 1)

                    turn_x(0)
                    gate_up(0, 0)
                    turn_x(1)
                    turn_a(0)
                    with pe.Fori(1, end_t + 1) as t:
                        gate_up(t, rank_of(t))
                        turn_x(t + 1)
                        down(t - 1, rank_of(t - 1))
                        turn_a(t)
                    down(end_t, rank_of(end_t))

        with ExitStack() as t_:
            def tb(name, shape, dt=F32):
                return t_.enter_context(nc.sbuf_tensor(name, shape, dt))

            YB = 4
            y1, y2 = (tb(n, [P, YB, D]) for n in ("cy1", "cy2"))
            s_done, s_ro, s_out = (t_.enter_context(nc.semaphore(f"c_{n}")) for n in ("done", "ro", "out"))
            y_sem = [t_.enter_context(nc.semaphore(f"c_y{b}")) for b in range(YB)]
            out = a["out"].rearrange("b s d -> (b s) d")

            def x1_tile(i):
                return x1_half(i // (NT // 2))[:, i % (NT // 2)]

            with nc.Block() as block:
                @block.gpsimd
                def _(pool):
                    for i in range(NT):
                        if i >= YB:
                            pool.wait_ge(s_ro, i - YB + 1)
                        for n, yy in enumerate((y1, y2)):
                            pool.indirect_dma_start(yy[:, i % YB], None, a["y_dram"],
                                                    bass.IndirectOffsetOnAxis(slot[:, n, i:i + 1], 0)
                                                    ).then_inc(y_sem[i % YB], 16)

                @block.scalar
                def _(act):
                    for i in range(NT):
                        act.wait_ge(s_ro, i + 1)
                        act.dma_start(out[i * P:(i + 1) * P, :], x1_tile(i)).then_inc(s_out, 16)
                    act.wait_ge(s_out, 16 * NT)

                @block.vector
                def _(dve):
                    m_ = dve.value_load(n_exp[0:1, 0:1], min_val=2, max_val=NE)
                    for part in range(2):
                        wait_alone(dve, s_raw[part], m_ * 16 + 16)
                    for i in range(NT):
                        r_ = x1_tile(i)
                        dve.wait_ge(y_sem[i % YB], 32 * (i // YB + 1))
                        dve.scalar_tensor_tensor(r_, y1[:, i % YB], wts[:, 0, i:i + 1], r_, ALU.mult,
                                                 ALU.add).then_inc(s_done, 1)
                        dve.wait_ge(s_done, i + 1)
                        dve.scalar_tensor_tensor(r_, y2[:, i % YB], wts[:, 1, i:i + 1], r_, ALU.mult,
                                                 ALU.add).then_inc(s_ro, 1)


_INS = ["x", "c", "w_ada", "b_ada", "norm1_g", "w_in", "b_fox", "q_norm_g", "k_norm_g", "attn_out_g",
        "hgrn_lb", "hgrn_out_g", "w_out", "norm2_g", "w_router_group", "b_router_group",
        "w_router_expert", "b_router_expert", "w_gate", "w_up", "w_down"]


def kernel(**inputs):
    import numpy as _np
    import concourse.bacc as _bacc
    from concourse import mybir as _mybir
    from concourse.bass_utils import run_bass_kernel_spmd as _run

    nc = _bacc.Bacc("TRN2", target_bir_lowering=False, num_devices=1)
    arrays, args = {}, {}
    for name in _INS:
        arr = _np.ascontiguousarray(inputs[name])
        arrays[f"in_{name}_dram"] = arr
        args[name] = nc.dram_tensor(f"in_{name}_dram", arr.shape, _mybir.dt.from_np(arr.dtype), kind="ExternalInput").ap()
    args["out"] = nc.dram_tensor("out_dram", (1, SEQ, D), _mybir.dt.float32, kind="ExternalOutput").ap()
    for name, shape, dt in (("x1_dram", (SEQ, D), F32), ("h2_dram", (SEQ, D), F32),
                            ("y_dram", (MAXT * P, D), F32)):
        args[name] = nc.dram_tensor(name, shape, dt, kind="Internal").ap()
    build(nc, args)
    r = _run(nc, [arrays], core_ids=[0])
    return r.results[0]["out_dram"]
```
